# Optimizing a Trainium2 kernel written in Bass

```python
import jax, jax.numpy as jnp
from jax import lax
import numpy as np

D_MODEL = 2048
BATCH = 1
SEQ = 256
DEPTH = 2

CTX_LEN = 256
GRID_W = 64
HEAD_DIM = 128
N_HEADS = (D_MODEL // 2) // HEAD_DIM
N_KV_HEADS = N_HEADS // 4
GQA_GROUP = N_HEADS // N_KV_HEADS
Q_WIDTH = N_HEADS * HEAD_DIM
KV_WIDTH = N_KV_HEADS * HEAD_DIM
N_FOURIER_GROUPS = 4
FOURIER_WIDTH = D_MODEL // 2
FOURIER_GROUP_DIM = FOURIER_WIDTH // N_FOURIER_GROUPS
EVEN_IN_WIDTH = FOURIER_WIDTH + Q_WIDTH + 2 * KV_WIDTH
EVEN_MIX_WIDTH = FOURIER_WIDTH + Q_WIDTH
WINDOW = 128
BLOCK = 128
ATTN_SCALE = HEAD_DIM ** -0.5
ROPE_THETA = 10000.0
ROPE_AXIS_DIM = HEAD_DIM // 2
CONV_WIDTH = 3
CONV_DIM = D_MODEL
D_FF = 4 * D_MODEL
N_MOD = 6
NORM_EPS = 1e-6
NEG_INF = -1e30

kernel_name = "hybrid_fourier_swa_shortconv_dit"

def rmsnorm(t, gain):
    tf = t.astype(jnp.float32)
    tf = tf * lax.rsqrt(jnp.mean(tf * tf, axis=-1, keepdims=True) + NORM_EPS)
    return tf.astype(t.dtype) * gain

def modulate(t, gain, shift, scale):
    return rmsnorm(t, gain) * (1 + scale) + shift

def axial_rope_tables(n_tok):
    rows = n_tok // GRID_W
    row = jnp.repeat(jnp.arange(rows, dtype=jnp.float32), GRID_W)
    col = jnp.tile(jnp.arange(GRID_W, dtype=jnp.float32), rows)
    inv_freq = ROPE_THETA ** (-jnp.arange(0, ROPE_AXIS_DIM, 2, dtype=jnp.float32) / ROPE_AXIS_DIM)
    ang = jnp.stack([row[:, None] * inv_freq, col[:, None] * inv_freq], axis=1)
    return jnp.cos(ang), jnp.sin(ang)

def apply_axial_rope(t, cos, sin):
    b, n, h, _ = t.shape
    tf = t.astype(jnp.float32).reshape(b, n, h, 2, 2, ROPE_AXIS_DIM // 2)
    t1, t2 = tf[..., 0, :], tf[..., 1, :]
    cs, sn = cos[None, :, None], sin[None, :, None]
    out = jnp.stack([t1 * cs - t2 * sn, t2 * cs + t1 * sn], axis=-2)
    return out.reshape(b, n, h, HEAD_DIM).astype(t.dtype)

def to_heads(t, n_heads):
    return t.reshape(t.shape[0], t.shape[1], n_heads, HEAD_DIM)

def fourier_mix(u):
    b, n, _ = u.shape
    ug = u.astype(jnp.float32).reshape(b, n, N_FOURIER_GROUPS, FOURIER_GROUP_DIM)
    y = jnp.fft.fft2(ug, axes=(1, 3)).real * (n * FOURIER_GROUP_DIM) ** -0.5
    return y.reshape(b, n, FOURIER_WIDTH).astype(u.dtype)

def sink_logits(sink):
    return sink.astype(jnp.float32).reshape(N_KV_HEADS, GQA_GROUP, 1, 1)

def sink_softmax(scores, sink_l):
    m = sink_l
    for s in scores:
        m = jnp.maximum(m, s.max(axis=-1, keepdims=True))
    exps = [jnp.exp(s - m) for s in scores]
    den = jnp.exp(sink_l - m)
    for e in exps:
        den = den + e.sum(axis=-1, keepdims=True)
    return [e / den for e in exps]

def band_blocks(t):
    b, n = t.shape[:2]
    tb = t.reshape(b, n // BLOCK, BLOCK, N_KV_HEADS, HEAD_DIM)
    tp = jnp.pad(tb, ((0, 0), (1, 1), (0, 0), (0, 0), (0, 0)))
    return jnp.concatenate([tp[:, :-2], tp[:, 1:-1], tp[:, 2:]], axis=2)

def window_attention(q, k, v, k_ctx, v_ctx, sink):
    b, n = q.shape[:2]
    nb = n // BLOCK
    qb = q.reshape(b, nb, BLOCK, N_KV_HEADS, GQA_GROUP, HEAD_DIM)
    kb, vb = band_blocks(k), band_blocks(v)
    s_loc = jnp.einsum('bnqkgd,bnskd->bnkgqs', qb, kb, preferred_element_type=jnp.float32) * ATTN_SCALE
    s_ctx = jnp.einsum('bnqkgd,bckd->bnkgqc', qb, k_ctx, preferred_element_type=jnp.float32) * ATTN_SCALE
    qi = jnp.arange(BLOCK)[:, None]
    kj = jnp.arange(3 * BLOCK)[None, :]
    kpos = (jnp.arange(nb)[:, None, None] - 1) * BLOCK + kj
    valid = (jnp.abs(kj - BLOCK - qi) <= WINDOW) & (kpos >= 0) & (kpos < n)
    s_loc = jnp.where(valid[None, :, None, None], s_loc, NEG_INF)
    p_loc, p_ctx = sink_softmax([s_loc, s_ctx], sink_logits(sink))
    o = (jnp.einsum('bnkgqs,bnskd->bnqkgd', p_loc.astype(v.dtype), vb)
         + jnp.einsum('bnkgqc,bckd->bnqkgd', p_ctx.astype(v.dtype), v_ctx))
    return o.reshape(b, n, Q_WIDTH)

def context_attention(q_c, k_c, v_c, sink):
    b, m = q_c.shape[:2]
    qg = q_c.reshape(b, m, N_KV_HEADS, GQA_GROUP, HEAD_DIM)
    s = jnp.einsum('bqkgd,bckd->bkgqc', qg, k_c, preferred_element_type=jnp.float32) * ATTN_SCALE
    (p,) = sink_softmax([s], sink_logits(sink))
    o = jnp.einsum('bkgqc,bckd->bqkgd', p.astype(v_c.dtype), v_c)
    return o.reshape(b, m, Q_WIDTH)

def split_even(p):
    return jnp.split(p, [FOURIER_WIDTH, FOURIER_WIDTH + Q_WIDTH, FOURIER_WIDTH + Q_WIDTH + KV_WIDTH], axis=-1)

def short_conv_mix(u, w_in, conv_w, w_out):
    gb, gc, xv = jnp.split(u @ w_in, 3, axis=-1)
    z = gc * xv
    zp = jnp.pad(z, ((0, 0), (1, 1), (0, 0)))
    y = conv_w[0] * zp[:, :-2] + conv_w[1] * zp[:, 1:-1] + conv_w[2] * zp[:, 2:]
    return (gb * y) @ w_out

def sq_relu_mlp(u, w1, w2):
    return jnp.square(jax.nn.relu(u @ w1)) @ w2

def setup_inputs(seed: int = 0) -> dict:
    key = jax.random.key(seed)
    ks = jax.random.split(key, 16)
    n_att = (DEPTH + 1) // 2
    n_conv = DEPTH // 2

    def nrm(k, shape, fan_in):
        return jax.random.normal(k, shape, jnp.float32) * fan_in ** -0.5

    return {
        "x": jax.random.normal(ks[0], (BATCH, SEQ, D_MODEL), jnp.float32),
        "c": jax.random.normal(ks[1], (BATCH, D_MODEL), jnp.float32),
        "ctx": jax.random.normal(ks[2], (BATCH, CTX_LEN, D_MODEL), jnp.float32),
        "c_ctx": jax.random.normal(ks[3], (D_MODEL,), jnp.float32),
        "w_mod": nrm(ks[4], (DEPTH, D_MODEL, N_MOD * D_MODEL), D_MODEL),
        "b_mod": 0.01 * jax.random.normal(ks[5], (DEPTH, N_MOD * D_MODEL), jnp.float32),
        "norm_gains": 1.0 + 0.01 * jax.random.normal(ks[6], (DEPTH, 4, D_MODEL), jnp.float32),
        "att_w_in": nrm(ks[7], (n_att, D_MODEL, EVEN_IN_WIDTH), D_MODEL),
        "att_sink": jax.random.normal(ks[8], (n_att, N_HEADS), jnp.float32),
        "att_w_out": nrm(ks[9], (n_att, EVEN_MIX_WIDTH, D_MODEL), EVEN_MIX_WIDTH),
        "conv_w_in": nrm(ks[10], (n_conv, D_MODEL, 3 * CONV_DIM), D_MODEL),
        "conv_w": nrm(ks[11], (n_conv, CONV_WIDTH, CONV_DIM), CONV_WIDTH),
        "conv_w_out": nrm(ks[12], (n_conv, CONV_DIM, D_MODEL), CONV_DIM),
        "mlp_w1": nrm(ks[13], (DEPTH, D_MODEL, D_FF), D_MODEL),
        "mlp_w2": nrm(ks[14], (DEPTH, D_FF, D_MODEL), D_FF),
    }

def reference(x, c, ctx, c_ctx, w_mod, b_mod, norm_gains, att_w_in, att_sink, att_w_out,
              conv_w_in, conv_w, conv_w_out, mlp_w1, mlp_w2):
    n_tok = x.shape[1]
    cos, sin = axial_rope_tables(n_tok)
    silu_c = jax.nn.silu(c)
    silu_cc = jax.nn.silu(c_ctx)
    h_ctx = ctx
    for l in range(DEPTH):
        g = norm_gains[l]
        is_attn = l % 2 == 0
        ctx_update = any(j % 2 == 0 for j in range(l + 1, DEPTH))
        sh_m, sc_m, gt_m, sh_f, sc_f, gt_f = [t[:, None] for t in
                                              jnp.split(silu_c @ w_mod[l] + b_mod[l], N_MOD, axis=-1)]
        if is_attn or ctx_update:
            csh_m, csc_m, cgt_m, csh_f, csc_f, cgt_f = jnp.split(silu_cc @ w_mod[l] + b_mod[l], N_MOD, axis=-1)

        ux = modulate(x, g[0], sh_m, sc_m)
        if is_attn:
            a = l // 2
            w_in, w_out, sink = att_w_in[a], att_w_out[a], att_sink[a]
            uc = modulate(h_ctx, g[0], csh_m, csc_m)
            if ctx_update:
                f_c, q_c, k_c, v_c = split_even(uc @ w_in)
            else:
                k_c, v_c = jnp.split(uc @ w_in[:, FOURIER_WIDTH + Q_WIDTH:], 2, axis=-1)
            k_c, v_c = to_heads(k_c, N_KV_HEADS), to_heads(v_c, N_KV_HEADS)
            f_x, q_x, k_x, v_x = split_even(ux @ w_in)
            q_x = apply_axial_rope(to_heads(q_x, N_HEADS), cos, sin)
            k_x = apply_axial_rope(to_heads(k_x, N_KV_HEADS), cos, sin)
            v_x = to_heads(v_x, N_KV_HEADS)
            attn_x = window_attention(q_x, k_x, v_x, k_c, v_c, sink)
            mix_x = jnp.concatenate([fourier_mix(f_x), attn_x], axis=-1) @ w_out
            if ctx_update:
                attn_c = context_attention(to_heads(q_c, N_HEADS), k_c, v_c, sink)
                mix_c = jnp.concatenate([fourier_mix(f_c), attn_c], axis=-1) @ w_out
        else:
            m = l // 2
            mix_x = short_conv_mix(ux, conv_w_in[m], conv_w[m], conv_w_out[m])
            if ctx_update:
                mix_c = short_conv_mix(modulate(h_ctx, g[0], csh_m, csc_m), conv_w_in[m], conv_w[m], conv_w_out[m])

        x = x + gt_m * rmsnorm(mix_x, g[1])
        x = x + gt_f * rmsnorm(sq_relu_mlp(modulate(x, g[2], sh_f, sc_f), mlp_w1[l], mlp_w2[l]), g[3])
        if ctx_update:
            h_ctx = h_ctx + cgt_m * rmsnorm(mix_c, g[1])
            h_ctx = h_ctx + cgt_f * rmsnorm(sq_relu_mlp(modulate(h_ctx, g[2], csh_f, csc_f), mlp_w1[l], mlp_w2[l]), g[3])
    return x


_drawn_inputs = setup_inputs


def setup_inputs(seed=0):
    import zlib

    import numpy as np

    out = dict(_drawn_inputs(seed))
    spreads = {}
    factors = {'b_mod': 2.704, 'norm_gains': 3.884, 'att_sink': 8.0}
    for name, (base, spread) in spreads.items():
        noise = np.random.default_rng([zlib.crc32(name.encode()), seed]).standard_normal(out[name].shape)
        drawn = base * np.exp(spread * noise) if base else spread * noise
        out[name] = __import__('jax').numpy.asarray(drawn.astype(out[name].dtype))
    for name, factor in factors.items():
        out[name] = (out[name] * factor).astype(out[name].dtype)
    return out
```

```python
from contextlib import ExitStack

import concourse.bass as bass
from concourse import mybir

F32 = mybir.dt.float32
F32R = mybir.dt.float32r
ALU = mybir.AluOpType
ACT = mybir.ActivationFunctionType
AX_X = mybir.AxisListType.X
RADD = bass.bass_isa.ReduceOp.add

P = 128
D = 2048
T = 256
KC = D // P
GW = 256
SLOTS = 4
CPS = KC // SLOTS
HEADS, KV_HEADS, HD = 8, 2, 128
GQA = HEADS // KV_HEADS
FOURIER = D // 2
FG = 4
D_FF = 4 * D
QUARTERS = D_FF // D
SCALE = float(HD) ** -0.5
EPS_COL, SEL_COL, TAB_W = 2050, 2048, 2052
HALF = D // 2
UNIT = KC

W_START = 0
START_GROUPS = 16
PG_K, PG_V, PG_Q, PG_F = 0, 2, 4, 8
PG_WO = 12
PG_MLP = (20, 116)
PG_CONV = 84
PG_CO = 108
W_K, W_V = 64, 68


def slab_of(pg):
    return 4 * pg + 56


UNITS = [(0, 2, 0), (0, 2, 1), (0, 4, 0), (0, 4, 1), (0, 3, 0), (0, 3, 1), (0, 5, 0), (0, 5, 1),
         (1, 0, 0), (1, 0, 1), (1, 1, 0), (1, 1, 1), (1, 2, 0), (1, 2, 1), (1, 4, 0), (1, 4, 1),
         (1, 3, 0), (1, 3, 1), (1, 5, 0), (1, 5, 1)]
U_Q, U_F, U_MID, U_WO, U_MLP0, U_CONV, U_CO, U_MLP1 = 0, 1, 2, 4, 6, 14, 16, 18


def unit_col(u):
    l, v, h = UNITS[u]
    return l * 6 * KC + v * KC + h * (KC // 2)


def backbone_program(nc, x_in, c_in, ctx_in, c_ctx, w_mod, b_mod, gains, att_w_in, sink, att_w_out,
                     conv_w_in, conv_w, conv_w_out, mlp_w1, mlp_w2, tables, out):
    with ExitStack() as ctx:
        def sb(name, shape, dt=F32):
            return ctx.enter_context(nc.sbuf_tensor(name, shape, dt))

        def sem(name):
            return ctx.enter_context(nc.semaphore(name))

        x = sb("x", [P, KC, T])
        u = sb("u", [P, KC, 2 * T], F32R)
        h = sb("h", [P, KC, 2 * T], F32R)
        y = sb("y", [P, KC, T])
        fq = sb("fq", [P, KC, T])
        raw = sb("raw", [P, SLOTS, 1024])
        whi = sb("whi", [P, SLOTS, 1024], F32R)
        wlo = sb("wlo", [P, SLOTS, 1024], F32R)
        mraw = sb("mraw", [P, 2, HALF])
        acc = sb("acc", [P, 2, HALF])
        red = sb("red", [P, HALF])
        kT = sb("kT", [P, KV_HEADS, 2 * T])
        v = sb("v", [P, 4, KV_HEADS * HD])
        tab = sb("tab", [P, TAB_W])
        tmp = sb("tmp", [P, 2, T])
        stat = sb("stat", [P, 4, T])
        small = sb("small", [P, 400])
        vt = sb("vt", [P, 12 * KC])
        modc = sb("modc", [P, 2, 2 * KC])
        cs = sb("cs", [P, 2 * KC])
        sg = sb("sg", [P, 2 * KC])
        der = sb("der", [P, 2, KC])
        t8 = sb("t8", [P, KC // 2])
        nsink = sb("nsink", [P, 2, HEADS])
        sinkr = sb("sinkr", [1, HEADS])
        sm = sb("sm", [P, 5, 2 * HEADS])
        ps = ctx.enter_context(nc.psum_tensor("ps", [P, 8, 512], F32))

        ident, ones = tab[:, 0:128], tab[:, 128:256]
        cosT, sinT = tab[:, 256:512], tab[:, 512:768]
        masks = (tab[:, 768:896], tab[:, 896:1024])
        dft = tab[:, 1024:2048].rearrange("p (k n) -> p k n", k=2)
        sel, eps = tab[0:4, SEL_COL:SEL_COL + 2], tab[:, EPS_COL:EPS_COL + 1]
        cT, gT = small[:, 0:32], small[:, 32:160]
        bT, cwT = small[:, 160:352], small[:, 352:400]
        xf = x[:, :, :].rearrange("p c t -> p (c t)")
        yf = y[:, :, :].rearrange("p c t -> p (c t)")
        ff = fq[:, :, :].rearrange("p c t -> p (c t)")
        qs, qsw = y[:, 0:2, :], y[:, 2:4, :]
        vsum = yf[:, 3072:4096].rearrange("p (g t) -> p g t", g=2)
        prob = [yf[:, 512 * i:512 * i + 512] for i in range(2)]
        probT = [yf[:, 1024 + 1024 * i:2048 + 1024 * i].rearrange("p (k q) -> p k q", k=4) for i in range(2)]
        ucs = yf[:, 3072:4096].rearrange("p (k n) -> p k n", k=2)
        row = (red[0:4, :], acc[0:4, 1, :])
        sqx = [ff[:, 1024 * i:1024 * i + 1024] for i in range(2)]
        ssq, sq = fq[:, 8:10, :], fq[:, 10:12, :]
        tsum, relu2 = fq[:, 8:10, :], fq[:, 10:12, :]
        cgb, cgc, cxv = fq[:, 8:10, :], fq[:, 10:12, :], fq[:, 12:14, :]
        zpad = ff[:, 0:2 * (T + 2)].rearrange("p (m t) -> p m t", m=2)
        cy = ff[:, 1024:1536].rearrange("p (m t) -> p m t", m=2)
        cv = ff[:, 1536:2048].rearrange("p (m t) -> p m t", m=2)

        tab_landed, small_landed, x_landed, ctx_landed = (sem(n) for n in (
            "tab_landed", "small_landed", "x_landed", "ctx_landed"))
        w_landed = [sem(f"w_landed{i}") for i in range(SLOTS)]
        m_landed = [sem(f"m_landed{i}") for i in range(2)]
        hi_ready, lo_ready, slab_used, m_used = (sem(n) for n in ("hi_ready", "lo_ready", "slab_used", "m_used"))
        b_copied, sum_done, y_part = (sem(n) for n in ("b_copied", "sum_done", "y_part"))
        small_t, small_copied, silu_exp, silu_step, crs_hi, crs_lo, crs_zero = (sem(n) for n in (
            "small_t", "small_copied", "silu_exp", "silu_step", "crs_hi", "crs_lo", "crs_zero"))
        sink_b, sink_copied = sem("sink_b"), sem("sink_copied")
        x_t, x_copied, ctx_t, ctx_copied = (sem(n) for n in ("x_t", "x_copied", "ctx_t", "ctx_copied"))
        row_copied, row_t, modc_step = sem("row_copied"), sem("row_t"), sem("modc_step")
        acc_zeroed, unit_summed, unit_masked, unit_read, mod_ready = (sem(n) for n in (
            "acc_zeroed", "unit_summed", "unit_masked", "unit_read", "mod_ready"))
        norm_sum, sd_ready, rstd_ready, sq_ready, sq_used, x_step, y_scaled = (sem(n) for n in (
            "norm_sum", "sd_ready", "rstd_ready", "sq_ready", "sq_used", "x_step", "y_scaled"))
        ysq_ready, ssq_done, ssq_zeroed, der_step = (sem(n) for n in ("ysq_ready", "ssq_done", "ssq_zeroed", "der_step"))
        u_scaled, u_hi, u_ready = sem("u_scaled"), sem("u_hi"), sem("u_ready")
        rope_step, v_t, v_ready = sem("rope_step"), sem("v_t"), sem("v_ready")
        s_done, masked, max_ready, negm_ready, p_ready, den_ready, rden_ready, pn_ready = (sem(n) for n in (
            "s_done", "masked", "max_ready", "negm_ready", "p_ready", "den_ready", "rden_ready", "pn_ready"))
        pt_done, pt_copied, pv_done, o_hi, o_ready = (sem(n) for n in (
            "pt_done", "pt_copied", "pv_done", "o_hi", "o_ready"))
        fa_done, fa_copied, fb_done, fb_hi, f_ready = (sem(n) for n in (
            "fa_done", "fa_copied", "fb_done", "fb_hi", "f_ready"))
        relu2_ready, h_hi, h_ready = sem("relu2_ready"), sem("h_hi"), sem("h_ready")
        z_edges, conv_step, v_hi, conv_ready = sem("z_edges"), sem("conv_step"), sem("v_hi"), sem("conv_ready")
        out_t, out_copied, out_stored = sem("out_t"), sem("out_copied"), sem("out_stored")

        block = ctx.enter_context(nc.Block())

        @block.sync
        def _(sp):
            def rows(t):
                return t.rearrange("(c p) -> c p", p=P)

            stage = acc[:, 0, :]
            sp.dma_start(tab[:, :], tables).then_inc(tab_landed, 16)
            sp.dma_start(stage[0:16, 0:128], rows(c_in.rearrange("a d -> (a d)"))).then_inc(small_landed, 16)
            sp.dma_start(stage[16:32, 0:128], rows(c_ctx)).then_inc(small_landed, 16)
            sp.dma_start(stage[:, 128:256], gains.rearrange("l g (c p) -> (l g c) p", p=P)).then_inc(small_landed, 16)
            for l in range(2):
                sp.dma_start(stage[0:96, 256 + 128 * l:384 + 128 * l],
                             b_mod[l].rearrange("(c p) -> c p", p=P)).then_inc(small_landed, 16)
            sp.dma_start(stage[0:48, 512:640], conv_w.rearrange("a k (c p) -> (a k c) p", p=P)).then_inc(small_landed, 16)
            sp.dma_start(sinkr[:, :], sink).then_inc(small_landed, 16)
            sp.dma_start(fq[:, :, :].rearrange("p c t -> p (c t)").rearrange("p (a d) -> p a d", a=2),
                         x_in[0].rearrange("(a p) d -> p a d", p=P)).then_inc(x_landed, 16)
            sp.dma_start(y[:, :, :].rearrange("p c t -> p (c t)").rearrange("p (a d) -> p a d", a=2),
                         ctx_in[0].rearrange("(a p) d -> p a d", p=P)).then_inc(ctx_landed, 16)

            def load_slab(w, s, src):
                if not (isinstance(w, int) and w < SLOTS):
                    sp.wait_ge(lo_ready, w - (SLOTS - 1))
                sp.dma_start(raw[:, s, :].rearrange("p (c n) -> p c n", c=CPS), src).then_inc(w_landed[s], 16)

            def w_slab(wt, row0, col0, s):
                return wt[bass.ds(row0 + s * CPS * P, CPS * P), bass.ds(col0, GW)].rearrange("(c p) n -> p c n", p=P)

            def load_unit_slab(m, slot, l, k, col0):
                if not (isinstance(m, int) and m < 2):
                    sp.wait_ge(m_used, m - 1)
                sp.dma_start(mraw[:, slot, :], w_mod[l, bass.ds(k * P, P), bass.ds(col0, HALF)]).then_inc(m_landed[slot], 16)

            def group_and_units(w0, wt, row0, col0, m0, k0, l, mcol, n_m):
                for s in range(SLOTS):
                    if wt is not None:
                        load_slab(w0 + s, s, w_slab(wt, row0, col0, s))
                    for j in range(s * n_m // SLOTS, (s + 1) * n_m // SLOTS):
                        load_unit_slab(m0 + j, j % 2, l, k0 + j, mcol)

            def stage_loads(w0, wt, row0, col0, n, m0, k_per_group, l, mcol, ahead):
                km = k_per_group
                def pair(b):
                    for j in range(2):
                        group_and_units(w0 + b * 8 + 4 * (j + 1), wt, row0, col0 + (b * 2 + (j + 1)) * GW,
                                        m0 + b * (2 * km) + j * km, b * (2 * km) + j * km, l, mcol, km)
                if n == 4:
                    pair(0)
                else:
                    with sp.Fori(0, n // 2 - 1) as b:
                        pair(b)
                b = n // 2 - 1
                group_and_units(w0 + (8 * b + 4), wt, row0, col0 + (2 * b + 1) * GW, m0 + 2 * b * km, 2 * b * km,
                                l, mcol, km)
                group_and_units(w0 + (8 * b + 8), *ahead, m0 + (2 * b + 1) * km, (2 * b + 1) * km, l, mcol, km)

            for hv in range(4):
                col0 = (1 - hv // 2) * D + (hv % 2) * HALF
                for k in range(KC):
                    w = W_START + hv * KC + k
                    load_slab(w, w % SLOTS, w_mod[0, k * P:(k + 1) * P, col0:col0 + HALF].rearrange(
                        "p (c n) -> p c n", c=CPS))
            wi = att_w_in[0]
            for w0, col0 in ((W_K, 2048), (W_V, 2304), (slab_of(PG_Q), 1024)):
                for s in range(SLOTS):
                    load_slab(w0 + s, s, w_slab(wi, 0, col0, s))
            sp.wait_ge(sq_used, 8)
            mcol = lambda un: UNITS[un][1] * D + UNITS[un][2] * HALF
            stage_loads(slab_of(PG_Q), wi, 0, 1024, 4, UNIT * U_Q, 4, 0, mcol(U_Q), (wi, 0, 0))
            stage_loads(slab_of(PG_F), wi, 0, 0, 4, UNIT * U_F, 4, 0, mcol(U_F), (att_w_out[0], 0, 0))
            for un in (U_MID, U_MID + 1):
                for k in range(KC):
                    load_unit_slab(UNIT * un + k, k % 2, 0, k, mcol(un))
            wo = att_w_out[0]
            stage_loads(slab_of(PG_WO), wo, 0, 0, 4, UNIT * U_WO, 4, 0, mcol(U_WO), (wo, 0, 4 * GW))
            stage_loads(slab_of(PG_WO + 4), wo, 0, 4 * GW, 4, UNIT * (U_WO + 1), 4, 0, mcol(U_WO + 1),
                        (mlp_w1[0], 0, 0))

            def mlp_loads(l, u0, loop_units, ahead):
                w1, w2 = mlp_w1[l], mlp_w2[l]
                w0 = slab_of(PG_MLP[l])

                def quarter(q, un, n_m, ml, mc1, mc2, nxt):
                    stage_loads(w0 + q * 64, w1, 0, q * D, 8, un * UNIT, n_m, ml, mc1, (w2, q * D, 0))
                    stage_loads(w0 + q * 64 + 32, w2, q * D, 0, 8, un * UNIT + UNIT, n_m, ml, mc2, nxt)
                quarter(0, u0, 2, l, 5 * D, 5 * D + HALF, (w1, 0, D))
                with sp.Fori(0, 2) as q:
                    quarter(q + 1, q * 2 + (u0 + 2), loop_units, 1, q * D, q * D + HALF, (w1, 0, (q + 2) * D))
                quarter(3, u0 + 6, loop_units, 1, 2 * D, 2 * D + HALF, ahead)

            mlp_loads(0, U_MLP0, 2, (conv_w_in[0], 0, 0))
            ci = conv_w_in[0]

            def triple_loads(t, w0, m0, k0, un, nxt_w, nxt_col):
                for j, (wt, col0) in enumerate(((ci, t * GW + D), (ci, t * GW + 2 * D), (nxt_w, nxt_col))):
                    for s in range(SLOTS):
                        load_slab(w0 + (4 * (j + 1) + s), s, w_slab(wt, 0, col0, s))
                        i = 4 * j + s
                        if i % 3 == 2:
                            load_unit_slab(m0 + i // 3, (i // 3) % 2, 1, k0 + i // 3, mcol(un))

            w0, un = slab_of(PG_CONV), U_CONV
            with sp.Fori(0, 4) as t:
                triple_loads(t, w0 + t * 12, UNIT * un + t * 4, t * 4, un, ci, t * GW + GW)
            with sp.Fori(0, 3) as t:
                triple_loads(t + 4, w0 + 48 + t * 12, UNIT * (un + 1) + t * 4, t * 4, un + 1, ci, t * GW + 5 * GW)
            triple_loads(7, w0 + 84, UNIT * (un + 1) + 12, 12, un + 1, conv_w_out[0], 0)
            co = conv_w_out[0]
            stage_loads(slab_of(PG_CO), co, 0, 0, 4, UNIT * U_CO, 4, 1, mcol(U_CO), (co, 0, 4 * GW))
            stage_loads(slab_of(PG_CO + 4), co, 0, 4 * GW, 4, UNIT * (U_CO + 1), 4, 1, mcol(U_CO + 1),
                        (mlp_w1[1], 0, 0))
            mlp_loads(1, U_MLP1, 0, (None, 0, 0))
            for b in range(4):
                for a in range(2):
                    sp.wait_ge(out_copied, 2 * b + a + 1)
                    sp.dma_start(out[0, a * P:(a + 1) * P, b * 512:(b + 1) * 512],
                                 ff[:, a * D + b * 512:a * D + (b + 1) * 512]).then_inc(out_stored, 16)
            sp.wait_ge(out_stored, 16 * 8)

        @block.tensor
        def _(pe):
            stage = acc[:, 0, :]
            pe.wait_ge(tab_landed, 16)
            pe.wait_ge(small_landed, 7 * 16)
            for n, col, dst in ((32, 0, 0), (128, 128, 32), (96, 256, 160), (96, 384, 256), (48, 512, 352)):
                last = pe.transpose(ps[:, 3, dst:dst + n], stage[0:n, col:col + 128], ident[0:n, 0:n])
            last.then_inc(small_t, 1)
            pe.matmul(ps[:, 2, 0:HEADS], ones[0:1, :], sinkr[:, :], start=True, stop=True).then_inc(sink_b, 1)
            for src, landed, turned, copied, bank in ((ff, x_landed, x_t, x_copied, 4),
                                                      (yf, ctx_landed, ctx_t, ctx_copied, 6)):
                pe.wait_ge(landed, 16)
                for i in range(8):
                    if i >= 2:
                        pe.wait_ge(copied, i - 1)
                    for c in range(2):
                        for a in range(2):
                            last = pe.transpose(ps[:, bank + i % 2, c * T + a * P:c * T + (a + 1) * P],
                                                src[:, a * D + (2 * i + c) * P:a * D + (2 * i + c + 1) * P], ident)
                    last.then_inc(turned, 1)

            def sums_of_squares(bank, n0):
                for b in range(4):
                    pe.wait_ge(sq_ready, n0 + b + 1)
                    for c in range(4):
                        last = pe.matmul(ps[:, bank, 0:T], ones, sqx_of(n0 + b)[:, c * T:(c + 1) * T],
                                         start=(b == 0 and c == 0), stop=(b == 3 and c == 3))
                    last.then_inc(sq_used, 1)

            def sqx_of(n):
                return mraw[:, n % 2, :] if n < 8 else sqx[n % 2]

            pe.wait_ge(crs_lo, 1)

            def mod_rows(hv):
                bank = 2 * (hv % 2)
                if hv >= 2:
                    pe.wait_ge(row_copied, hv - 1)
                if hv == 1:
                    pe.wait_ge(small_copied, 1)
                    pe.wait_ge(sink_copied, 1)
                for k in range(KC):
                    w = hv * KC + k
                    pe.wait_ge(lo_ready, w + 1)
                    for part in (whi, wlo):
                        for n in range(2):
                            last = pe.matmul(ps[:, bank + n, :], u[:, k, 0:128],
                                             part[:, w % SLOTS, n * 512:(n + 1) * 512],
                                             start=(k == 0 and part is whi), stop=(k == KC - 1 and part is wlo))
                    last.then_inc(slab_used, 1)

            def turn_rows(hv):
                pe.wait_ge(row_copied, hv + 1)
                for c in range(8):
                    last = pe.matmul(ps[:, 7, hv * 16 + 2 * c:hv * 16 + 2 * c + 2], row[hv % 2][:, c * P:(c + 1) * P], sel,
                                     start=True, stop=True)
                last.then_inc(row_t, 1)

            mod_rows(0)
            pe.wait_ge(ctx_copied, 8)
            sums_of_squares(6, 0)
            mod_rows(1)
            pe.wait_ge(sd_ready, 1)
            sums_of_squares(6, 4)
            turn_rows(0)
            mod_rows(2)
            turn_rows(1)
            mod_rows(3)
            turn_rows(2)
            turn_rows(3)

            def group(pg, w0, src, banks, input_waits, src2=None):
                if not (isinstance(pg, int) and pg < 2):
                    pe.wait_ge(sum_done, pg - 1)
                for s in range(SLOTS):
                    pe.wait_ge(lo_ready, w0 + (s + 1))
                    for sm_, n in input_waits(s):
                        pe.wait_ge(sm_, n)
                    for c in range(CPS):
                        k = s * CPS + c
                        for m in range(2):
                            for i, inp in enumerate((src,) if src2 is None else (src, src2)):
                                bk = banks[2 * i + m]
                                pe.matmul(ps[:, bk, :], whi[:, s, c * GW + m * P:c * GW + (m + 1) * P], inp[:, k, :],
                                          start=(k == 0), stop=False)
                                last = pe.matmul(ps[:, bk, 0:T], wlo[:, s, c * GW + m * P:c * GW + (m + 1) * P],
                                                 inp[:, k, 0:T], start=False, stop=(k == KC - 1))
                        if c == CPS - 1:
                            last.then_inc(slab_used, 1)

            u_waits = lambda base, per=1: (lambda s: [(u_ready, base + per * CPS * (s + 1))])
            group(PG_K, W_K, u, (0, 1, 2, 3), u_waits(0, 2), h)
            group(PG_V, W_V, u, (4, 5, 6, 7), lambda s: [], h)

            def stage_groups(pg0, n, src, input_waits):
                with pe.Fori(0, n // 2) as b:
                    for j in range(2):
                        pg = b * 2 + (pg0 + j)
                        group(pg, b * 8 + slab_of(pg0 + j), src, (2 * j, 2 * j + 1), input_waits)

            stage_groups(PG_Q, 4, u, lambda s: [])
            stage_groups(PG_F, 4, u, lambda s: [])

            pe.wait_ge(sum_done, PG_WO)
            pe.wait_ge(rope_step, 4 * 5)

            def scores(un):
                hd, qt = divmod(un, 2)
                if un >= 3:
                    pe.wait_ge(p_ready, un - 2)
                pe.matmul(ps[:, un % 3, :], fq[:, 8 + hd, qt * P:(qt + 1) * P], kT[:, hd // GQA, :],
                          start=True, stop=True).then_inc(s_done, 1)

            def turn_probs(un):
                pe.wait_ge(pn_ready, un + 1)
                if un >= 2:
                    pe.wait_ge(pt_copied, un - 1)
                for kt in range(4):
                    last = pe.transpose(ps[:, 4 + un % 2, kt * P:(kt + 1) * P], prob[un % 2][:, kt * P:(kt + 1) * P],
                                        ident)
                last.then_inc(pt_done, 1)

            def values(hd):
                pe.wait_ge(pt_copied, 2 * hd + 2)
                if hd >= 2:
                    pe.wait_ge(o_ready, hd - 1)
                for kt in range(4):
                    last = pe.matmul(ps[:, 6, (hd % 2) * T:(hd % 2 + 1) * T],
                                     v[:, kt, (hd // GQA) * HD:(hd // GQA + 1) * HD], probT[hd % 2][:, kt, :],
                                     start=(kt == 0), stop=(kt == 3))
                last.then_inc(pv_done, 1)

            def channel_dft(g):
                for a in range(2):
                    if 2 * g + a >= 1:
                        pe.wait_ge(fa_copied, 2 * (2 * g + a))
                    for kc in range(2):
                        last = pe.matmul(ps[:, 3, :], fq[:, 2 * g + kc, a * P:(a + 1) * P], dft[:, kc, :],
                                         start=(kc == 0), stop=(kc == 1))
                    last.then_inc(fa_done, 1)

            def token_dft(g):
                pe.wait_ge(fa_copied, 4 * g + 4)
                if g >= 1:
                    pe.wait_ge(f_ready, g)
                for m in range(2):
                    for i in range(4):
                        trig, a = divmod(i, 2)
                        last = pe.matmul(ps[:, 7, m * T:(m + 1) * T],
                                         ucs[:, a, trig * T + m * P:trig * T + (m + 1) * P],
                                         dft[:, a, trig * T:(trig + 1) * T], start=(i == 0), stop=(i == 3))
                last.then_inc(fb_done, 1)

            for un in range(3):
                scores(un)
            for kv in range(KV_HEADS):
                for kt in range(4):
                    last = pe.transpose(ps[:, 4 + kv, kt * P:(kt + 1) * P], vsum[:, kv, kt * P:(kt + 1) * P], ident)
                last.then_inc(v_t, 1)
            pe.wait_ge(v_ready, KV_HEADS)
            for un in range(2 * HEADS):
                turn_probs(un)
                if un + 3 < 2 * HEADS:
                    scores(un + 3)
                if un % 4 == 0:
                    channel_dft(un // 4)
                if un % 4 == 2:
                    token_dft(un // 4)
                if un % 2 == 0 and un >= 2:
                    values(un // 2 - 1)
            values(HEADS - 1)

            pe.wait_ge(f_ready, FG)
            pe.wait_ge(o_ready, HEADS)
            stage_groups(PG_WO, 8, u, lambda s: [])

            def boundary_sums(j, n_sq):
                pe.wait_ge(ssq_done, 8 * (j + 1))
                for m in range(2):
                    last = pe.matmul(ps[:, 6, 0:T], ones, ssq[:, m, :], start=(m == 0), stop=(m == 1))
                last.then_inc(norm_sum, 1)
                if n_sq:
                    sums_of_squares(7, 8 + 4 * j)

            def mlp_groups(l):
                pg0 = PG_MLP[l]
                u0 = (32, 64)[l]
                h0 = 32 * l

                def quarter(q):
                    for part, src in ((0, u), (1, h)):
                        waits = u_waits(u0) if part == 0 else (lambda s: [(h_ready, q * 8 + (h0 + 2 * (s + 1)))])
                        with pe.Fori(0, 4) as b:
                            for j in range(2):
                                pg = q * 16 + b * 2 + (pg0 + 8 * part + j)
                                group(pg, q * 64 + b * 8 + (slab_of(pg0) + 32 * part + 4 * j), src,
                                      (2 * j, 2 * j + 1), waits)
                quarter(0)
                with pe.Fori(0, 2) as q:
                    quarter(q + 1)
                quarter(3)

            boundary_sums(0, 4)
            mlp_groups(0)
            boundary_sums(1, 4)
            with pe.Fori(0, 8) as t:
                for j in range(3):
                    group(t * 3 + (PG_CONV + j), t * 12 + (slab_of(PG_CONV) + 4 * j), u, (2 * j, 2 * j + 1), u_waits(48))
            with pe.Fori(0, 4) as b:
                for j in range(2):
                    group(b * 2 + (PG_CO + j), b * 8 + slab_of(PG_CO + j), h, (2 * j, 2 * j + 1),
                          lambda s: [(conv_ready, 2 * (s + 1))])
            boundary_sums(2, 4)
            mlp_groups(1)
            boundary_sums(3, 0)
            for b in range(4):
                pe.wait_ge(x_step, 13 + b)
                for a in range(2):
                    n = 2 * b + a
                    if n >= 4:
                        pe.wait_ge(out_copied, n - 3)
                    for c in range(4):
                        last = pe.transpose(ps[:, n % 4, c * P:(c + 1) * P], x[:, 4 * b + c, a * P:(a + 1) * P], ident)
                    last.then_inc(out_t, 1)

        @block.scalar
        def _(act):
            def hi(w, s):
                act.wait_ge(w_landed[s], w * 4 + (16 - 4 * s) if not isinstance(w, int) else 16 * (w // SLOTS + 1))
                if not (isinstance(w, int) and w < SLOTS):
                    act.wait_ge(slab_used, w - (SLOTS - 1))
                act.activation(whi[:, s, :], raw[:, s, :], ACT.Copy).then_inc(hi_ready, 1)

            def his(w0):
                for s in range(SLOTS):
                    hi(w0 + s, s)

            act.wait_ge(small_copied, 1)
            act.activation(sg[:, :], cT, ACT.Exp, scale=-1.0).then_inc(silu_exp, 1)
            for i in range(8):
                act.wait_ge(ctx_t, i + 1)
                act.activation(fq[:, 2 * i:2 * i + 2, :], ps[:, 6 + i % 2, :].rearrange("p (c t) -> p c t", c=2),
                               ACT.Copy).then_inc(ctx_copied, 1)
            act.wait_ge(silu_step, 3)
            act.wait_ge(crs_zero, 1)
            act.activation(u[:, :, 0:2], cs[:, :].rearrange("p (w k) -> p k w", w=2), ACT.Copy).then_inc(crs_hi, 1)

            def square(n, src):
                if n >= 2:
                    act.wait_ge(sq_used, n - 1)
                dst = mraw[:, n % 2, :] if n < 8 else sqx[n % 2]
                act.activation(dst, src, ACT.Square).then_inc(sq_ready, 1)

            def root(dst, bank):
                act.activation(dst, ps[:, bank, 0:T], ACT.Sqrt, bias=eps, scale=1.0 / D).then_inc(sd_ready, 1)

            def copy_row(hv):
                act.wait_ge(slab_used, UNIT * (hv + 1))
                if hv == 1:
                    act.wait_ge(small_t, 1)
                if hv >= 2:
                    act.wait_ge(row_t, hv - 1)
                bank = 2 * (hv % 2)
                act.activation(row[hv % 2].rearrange("p (m n) -> p m n", m=2), ps[0:4, bank:bank + 2, :],
                               ACT.Copy).then_inc(row_copied, 1)

            for g in range(4):
                his(4 * g)
            act.wait_ge(x_copied, 8)
            square(0, xf[:, 0:1024])
            square(1, xf[:, 1024:2048])
            his(16)
            copy_row(0)
            square(2, xf[:, 2048:3072])
            square(3, xf[:, 3072:4096])
            for g in range(5, 8):
                his(4 * g)
            act.wait_ge(sq_used, 4)
            root(stat[:, 0, :], 6)
            act.wait_ge(ctx_copied, 8)
            square(4, ff[:, 0:1024])
            square(5, ff[:, 1024:2048])
            his(32)
            copy_row(1)
            square(6, ff[:, 2048:3072])
            square(7, ff[:, 3072:4096])
            for g in range(9, 12):
                his(4 * g)
            act.wait_ge(sq_used, 8)
            root(stat[:, 2, :], 6)
            his(48)
            copy_row(2)
            for g in range(13, 16):
                his(4 * g)
            his(W_K)
            copy_row(3)

            def modulated_hi(n, dst, mt, shift):
                act.wait_ge(u_scaled, n + 1)
                act.activation(dst, mt, ACT.Identity, bias=shift).then_inc(u_hi, 1)

            for c in range(KC):
                for w, dst in ((0, u), (1, h)):
                    n = 2 * c + w
                    modulated_hi(n, dst[:, c, 0:T], yf[:, (n % 4) * T:(n % 4 + 1) * T],
                                 modc[:, 1, n:n + 1])

            def right_half(pg, bank, w_end):
                act.wait_ge(slab_used, w_end)
                if not (isinstance(pg, int) and pg == 0):
                    act.wait_ge(sum_done, pg)
                act.activation(tmp[:, :, :], ps[:, bank:bank + 2, T:2 * T], ACT.Copy).then_inc(b_copied, 1)

            his(W_V)
            right_half(0, 0, W_K + 4)
            right_half(1, 2, W_K + 4)
            his(slab_of(PG_Q))
            right_half(2, 4, W_V + 4)
            right_half(3, 6, W_V + 4)

            def stage(pg0, n, after, q=None, last=False):
                w0 = slab_of(pg0)
                with act.Fori(0, n // 2) as b:
                    for j in range(2):
                        pg, w = b * 2 + (pg0 + j), b * 8 + (w0 + 4 * j)
                        if q is not None:
                            pg, w = q * 16 + pg, q * 64 + w
                        his(w + 4)
                        right_half(pg, 2 * j, w + 4)
                        after(pg, b * 2 + j)

            stage(PG_Q, 4, lambda pg, i: None)
            stage(PG_F, 4, lambda pg, i: None)

            def probabilities(un):
                hd = un // 2
                act.wait_ge(negm_ready, un + 1)
                if un >= 2:
                    act.wait_ge(pt_done, un - 1)
                act.activation(sm[:, 2, un:un + 1], nsink[:, 0, hd:hd + 1], ACT.Exp, bias=sm[:, 1, un:un + 1])
                act.activation(prob[un % 2], ps[:, un % 3, :], ACT.Exp, bias=sm[:, 1, un:un + 1], scale=SCALE,
                               accum_out=sm[:, 3, un:un + 1]).then_inc(p_ready, 1)

            def probs_turned(un):
                hd, qt = divmod(un, 2)
                act.wait_ge(pt_done, un + 1)
                if hd >= 2:
                    act.wait_ge(pv_done, hd - 1)
                act.activation(probT[hd % 2][:, :, qt * P:(qt + 1) * P],
                               ps[:, 4 + un % 2, :].rearrange("p (k q) -> p k q", k=4), ACT.Copy).then_inc(pt_copied, 1)

            probabilities(0)
            for un in range(2 * HEADS):
                if un + 1 < 2 * HEADS:
                    probabilities(un + 1)
                probs_turned(un)
                if un % 4 == 0:
                    g = un // 4
                    for a in range(2):
                        act.wait_ge(fa_done, 2 * g + a + 1)
                        if g >= 1:
                            act.wait_ge(fb_done, g)
                        for trig, sign in ((0, 1.0), (1, -1.0)):
                            act.activation(ucs[:, a, trig * T:(trig + 1) * T], ps[:, 3, trig * T:(trig + 1) * T],
                                           ACT.Copy, scale=sign / T).then_inc(fa_copied, 1)
                if un % 4 == 2:
                    g = un // 4
                    act.wait_ge(fb_done, g + 1)
                    act.activation(u[:, 2 * g:2 * g + 2, 0:T], ps[:, 7, :].rearrange("p (c t) -> p c t", c=2),
                                   ACT.Copy).then_inc(fb_hi, 1)
                if un % 2 == 0 and un >= 2:
                    hd = un // 2 - 1
                    act.wait_ge(pv_done, hd + 1)
                    act.activation(u[:, 8 + hd, 0:T], ps[:, 6, (hd % 2) * T:(hd % 2 + 1) * T], ACT.Copy).then_inc(o_hi, 1)
            hd = HEADS - 1
            act.wait_ge(pv_done, HEADS)
            act.activation(u[:, 8 + hd, 0:T], ps[:, 6, (hd % 2) * T:(hd % 2 + 1) * T], ACT.Copy).then_inc(o_hi, 1)

            def y_squares(pg, i):
                act.wait_ge(sum_done, pg + 1)
                act.activation(sq, y[:, bass.ds(i * 2, 2), :], ACT.Square).then_inc(ysq_ready, 1)

            def boundary(j, shift):
                act.wait_ge(norm_sum, j + 1)
                root(stat[:, 0, :], 6)
                if shift is None:
                    return
                for b in range(4):
                    act.wait_ge(x_step, 4 * j + b + 1)
                    square(8 + 4 * j + b, xf[:, b * 1024:(b + 1) * 1024])
                act.wait_ge(sq_used, 12 + 4 * j)
                root(stat[:, 2, :], 7)
                act.wait_ge(mod_ready, MOD_NEEDED[j])
                for c in range(KC):
                    modulated_hi(32 + 16 * j + c, u[:, c, 0:T], ff[:, (12 + c % 4) * T:(13 + c % 4) * T],
                                 vt[:, shift + c:shift + c + 1])

            def mlp(l):
                pg0 = PG_MLP[l]

                def h_high(q):
                    def f(pg, i):
                        act.wait_ge(relu2_ready, q * 8 + i + (32 * l + 1))
                        act.activation(h[:, bass.ds(i * 2, 2), 0:T], relu2, ACT.Copy).then_inc(h_hi, 1)
                    return f

                def quarter(q, after2):
                    stage(pg0, 8, h_high(q), q)
                    stage(pg0 + 8, 8, after2, q)
                quarter(0, lambda pg, i: None)
                with act.Fori(0, 2) as q:
                    quarter(q + 1, lambda pg, i: None)
                if l == 0:
                    quarter(3, y_squares)
                else:
                    stage(pg0, 8, h_high(3), 3)
                    stage_end(pg0 + 8, y_squares)

            def stage_end(pg0, after):
                w0 = slab_of(pg0) + 192
                pg0 += 48
                with act.Fori(0, 3) as b:
                    for j in range(2):
                        his(b * 8 + (w0 + 4 * j + 4))
                        right_half(b * 2 + (pg0 + j), 2 * j, b * 8 + (w0 + 4 * j + 4))
                        after(b * 2 + (pg0 + j), b * 2 + j)
                his(w0 + 28)
                right_half(pg0 + 6, 0, w0 + 28)
                after(pg0 + 6, 6)
                right_half(pg0 + 7, 2, w0 + 32)
                after(pg0 + 7, 7)

            stage(PG_WO, 8, y_squares)
            boundary(0, 3 * KC)
            mlp(0)
            boundary(1, 6 * KC)
            with act.Fori(0, 8) as t:
                for j in range(3):
                    pg, w = t * 3 + (PG_CONV + j), t * 12 + (slab_of(PG_CONV) + 4 * j)
                    his(w + 4)
                    right_half(pg, 2 * j, w + 4)
                act.wait_ge(conv_step, t * 5 + 5)
                act.activation(h[:, bass.ds(t * 2, 2), 0:T], cv, ACT.Copy).then_inc(v_hi, 1)
            stage(PG_CO, 8, y_squares)
            boundary(2, 6 * KC + 3 * KC)
            mlp(1)
            boundary(3, None)
            for n in range(8):
                b, a = divmod(n, 2)
                act.wait_ge(out_t, n + 1)
                act.activation(ff[:, a * D + b * 512:a * D + (b + 1) * 512], ps[:, n % 4, :], ACT.Copy).then_inc(out_copied, 1)

        @block.vector
        def _(dve):
            def lo(w, s):
                dve.wait_ge(hi_ready, w + 1)
                dve.tensor_tensor(wlo[:, s, :], raw[:, s, :], whi[:, s, :], ALU.subtract).then_inc(lo_ready, 1)

            def los(w0):
                for s in range(SLOTS):
                    lo(w0 + s, s)

            def unit_slab(m, un, k):
                slot, first_unit = m_slot(m), isinstance(un, int) and un == 0
                dve.wait_ge(m_landed[slot], m * 8 + (16 - 8 * slot) if not isinstance(m, int) else 16 * (m // 2 + 1))
                dve.wait_ge(acc_zeroed, un + 1)
                if not first_unit:
                    dve.wait_ge(m_used, m)
                a = acc[:, unit_parity[0], :]
                dve.scalar_tensor_tensor(out=a, in0=mraw[:, slot, :], scalar=cs[:, bass.ds(k, 1)], in1=a,
                                         op0=ALU.mult, op1=ALU.add).then_inc(m_used, 1)
                if first_unit:
                    dve.wait_ge(m_used, m + 1)

            m_parity, unit_parity = [0], [0]

            def m_slot(m):
                return m % 2 if isinstance(m, int) else m_parity[0]

            def unit_slabs(m0, un, k0, js, parity):
                for j in js:
                    m_parity[0], unit_parity[0] = j % 2, parity
                    unit_slab(m0 + j, un, k0 + j)

            def finish_unit(un, col):
                dve.wait_ge(unit_masked, un + 1)
                if not (isinstance(un, int) and un == 0):
                    dve.wait_ge(mod_ready, un)
                dve.tensor_reduce(t8[:, :], red[:, :].rearrange("p (c f) -> p c f", f=P), AX_X,
                                  ALU.add).then_inc(unit_read, 1)
                dve.wait_ge(unit_read, un + 1)
                dve.tensor_tensor(vt[:, bass.ds(col, KC // 2)], t8[:, :], bT[:, bass.ds(col, KC // 2)],
                                  ALU.add).then_inc(mod_ready, 1)

            dve.memset(u[:, :, 0:128].bitcast(F32), 0.0).then_inc(crs_zero, 1)
            dve.wait_ge(small_t, 1)
            dve.tensor_copy(small[:, :], ps[:, 3, 0:400]).then_inc(small_copied, 1)
            dve.wait_ge(sink_b, 1)
            dve.tensor_copy(nsink[:, 0, :], ps[:, 2, 0:HEADS])
            dve.tensor_scalar(nsink[:, 1, :], ps[:, 2, 0:HEADS], -1.0, None, ALU.mult).then_inc(sink_copied, 1)
            dve.wait_ge(silu_exp, 1)
            dve.tensor_scalar(sg[:, :], sg[:, :], 1.0, None, ALU.add).then_inc(silu_step, 1)
            dve.wait_ge(silu_step, 1)
            dve.reciprocal(sg[:, :], sg[:, :]).then_inc(silu_step, 1)
            dve.wait_ge(silu_step, 2)
            dve.wait_ge(small_copied, 1)
            dve.tensor_tensor(cs[:, :], cT, sg[:, :], ALU.mult).then_inc(silu_step, 1)
            for i in range(8):
                dve.wait_ge(x_t, i + 1)
                dve.tensor_copy(x[:, 2 * i:2 * i + 2, :],
                                ps[:, 4 + i % 2, :].rearrange("p (c t) -> p c t", c=2)).then_inc(x_copied, 1)
            dve.wait_ge(crs_hi, 1)
            dve.tensor_tensor(u[:, :, 2:4], cs[:, :].rearrange("p (w k) -> p k w", w=2), u[:, :, 0:2],
                              ALU.subtract).then_inc(crs_lo, 1)

            def reciprocal_root(n, i):
                dve.wait_ge(sd_ready, n)
                dve.reciprocal(stat[:, i + 1, :], stat[:, i, :]).then_inc(rstd_ready, 1)
                dve.wait_ge(rstd_ready, n)

            for g in range(9):
                los(4 * g)
            reciprocal_root(1, 0)
            for g in range(9, 13):
                los(4 * g)
            reciprocal_root(2, 2)
            for g in range(13, 16):
                los(4 * g)
            los(W_K)

            def both(a):
                return a.unsqueeze(2).broadcast_to([P, KC, 2])

            def pairs(a):
                return a.rearrange("p (c w) -> p c w", w=2)
            dve.wait_ge(row_t, 4)
            dve.tensor_tensor(pairs(modc[:, 0, :]), pairs(ps[:, 7, 0:32]), both(bT[:, KC:2 * KC]),
                              ALU.add).then_inc(modc_step, 1)
            dve.tensor_tensor(pairs(modc[:, 1, :]), pairs(ps[:, 7, 32:64]), both(bT[:, 0:KC]),
                              ALU.add).then_inc(modc_step, 1)
            dve.wait_ge(modc_step, 2)
            dve.scalar_tensor_tensor(out=pairs(modc[:, 0, :]), in0=pairs(modc[:, 0, :]), scalar=1.0,
                                     in1=both(gT[:, 0:KC]), op0=ALU.add, op1=ALU.mult).then_inc(modc_step, 1)
            dve.wait_ge(modc_step, 3)

            def modulate(n0, items):
                def scaled(i):
                    src, dst, mt, gs, shift, rstd = items[i]
                    if n0 + i >= 4:
                        dve.wait_ge(u_ready, n0 + i - 3)
                    dve.scalar_tensor_tensor(out=mt, in0=src, scalar=gs, in1=rstd, op0=ALU.mult,
                                             op1=ALU.mult).then_inc(u_scaled, 1)
                scaled(0)
                for i, (src, dst, mt, gs, shift, rstd) in enumerate(items):
                    if i + 1 < len(items):
                        scaled(i + 1)
                    dve.wait_ge(u_scaled, n0 + i + 1)
                    dve.wait_ge(u_hi, n0 + i + 1)
                    dve.scalar_tensor_tensor(out=dst[:, T:2 * T], in0=mt, scalar=shift, in1=dst[:, 0:T],
                                             op0=ALU.add, op1=ALU.subtract).then_inc(u_ready, 1)

            items = []
            for c in range(KC):
                for w, (src, dst) in enumerate(((x, u), (fq, h))):
                    n = 2 * c + w
                    items.append((src[:, c, :], dst[:, c, :], yf[:, (n % 4) * T:(n % 4 + 1) * T],
                                  modc[:, 0, n:n + 1], modc[:, 1, n:n + 1], stat[:, 1 + 2 * w, :]))
            dve.wait_ge(x_copied, 8)
            modulate(0, items)

            def add_halves(pg, bank, dst):
                dve.wait_ge(b_copied, pg + 1)
                dve.tensor_tensor(dst, ps[:, bank:bank + 2, 0:T], tmp[:, :, :], ALU.add).then_inc(sum_done, 1)

            def rope(pg, r, dst):
                dve.wait_ge(sum_done, pg + 1)
                for a, b in ((0, 32), (32, 0), (64, 96), (96, 64)):
                    last = dve.tensor_copy(qsw[a:a + 32], qs[b:b + 32])
                last.then_inc(rope_step, 1)
                dve.wait_ge(rope_step, r * 4 + 1)
                dve.tensor_tensor(qs, qs, cosT.unsqueeze(1).broadcast_to([P, 2, T]), ALU.mult).then_inc(rope_step, 1)
                dve.tensor_tensor(qsw, qsw, sinT.unsqueeze(1).broadcast_to([P, 2, T]), ALU.mult).then_inc(rope_step, 1)
                dve.wait_ge(rope_step, r * 4 + 3)
                dve.tensor_tensor(dst, qs, qsw, ALU.add).then_inc(rope_step, 1)
                dve.wait_ge(rope_step, r * 4 + 4)

            los(W_V)
            add_halves(0, 0, qs)
            rope(0, 0, kT[:, :, 0:T])
            add_halves(1, 2, kT[:, :, T:2 * T])
            los(slab_of(PG_Q))
            add_halves(2, 4, vsum[:, :, 0:T])
            add_halves(3, 6, vsum[:, :, T:2 * T])

            def stage(pg0, n, un, n_m, take, q=None, u_par=0):
                w0 = slab_of(pg0)
                with dve.Fori(0, n // 2) as b:
                    for j in range(2):
                        pg, w = b * 2 + (pg0 + j), b * 8 + (w0 + 4 * j + 4)
                        if q is not None:
                            pg, w = q * 16 + pg, q * 64 + w
                        for s in range(SLOTS):
                            lo(w + s, s)
                            js = range(s * n_m // SLOTS, (s + 1) * n_m // SLOTS)
                            if js:
                                unit_slabs(un * UNIT + (b * (2 * n_m) + j * n_m), un, b * (2 * n_m) + j * n_m, js, u_par)
                        take(pg, 2 * j, b * 2 + j)

            def take_q(pg, bank, i):
                add_halves(pg, bank, qs)
                rope(pg, i + 1, fq[:, bass.ds(i * 2 + 8, 2), :])
            stage(PG_Q, 4, U_Q, 4, take_q, u_par=0)
            stage(PG_F, 4, U_F, 4, lambda pg, bank, i: add_halves(pg, bank, fq[:, bass.ds(i * 2, 2), :]), u_par=1)
            finish_unit(0, unit_col(0))

            for kv in range(KV_HEADS):
                dve.wait_ge(v_t, kv + 1)
                dve.tensor_copy(v[:, :, kv * HD:(kv + 1) * HD],
                                ps[:, 4 + kv, :].rearrange("p (k d) -> p k d", k=4)).then_inc(v_ready, 1)

            def row_max(un):
                hd, qt = divmod(un, 2)
                dve.wait_ge(s_done, un + 1)
                far = ps[:, un % 3, (1 - qt) * P:(2 - qt) * P]
                dve.tensor_tensor(far, far, masks[qt], ALU.add).then_inc(masked, 1)
                dve.wait_ge(masked, un + 1)
                dve.tensor_reduce(sm[:, 0, un:un + 1], ps[:, un % 3, :], AX_X, ALU.max).then_inc(max_ready, 1)
                dve.wait_ge(max_ready, un + 1)
                dve.tensor_scalar(sm[:, 1, un:un + 1], sm[:, 0, un:un + 1], -SCALE, nsink[:, 1, hd:hd + 1],
                                  ALU.mult, ALU.min).then_inc(negm_ready, 1)

            def normalize(un):
                dve.wait_ge(p_ready, un + 1)
                col = slice(un, un + 1)
                dve.tensor_tensor(sm[:, 4, col], sm[:, 3, col], sm[:, 2, col], ALU.add).then_inc(den_ready, 1)
                dve.wait_ge(den_ready, un + 1)
                dve.reciprocal(sm[:, 4, col], sm[:, 4, col]).then_inc(rden_ready, 1)
                dve.wait_ge(rden_ready, un + 1)
                dve.tensor_scalar(prob[un % 2], prob[un % 2], sm[:, 4, col], None, ALU.mult).then_inc(pn_ready, 1)

            def o_low(hd):
                dve.wait_ge(o_hi, hd + 1)
                dve.tensor_tensor(u[:, 8 + hd, T:2 * T], ps[:, 6, (hd % 2) * T:(hd % 2 + 1) * T], u[:, 8 + hd, 0:T],
                                  ALU.subtract).then_inc(o_ready, 1)

            row_max(0)
            row_max(1)
            for un in range(2 * HEADS):
                normalize(un)
                if un + 2 < 2 * HEADS:
                    row_max(un + 2)
                mid = U_MID + un // HEADS
                unit_slabs(UNIT * U_MID + 2 * un, mid, (2 * un) % UNIT, range(2), mid % 2)
                if un % 4 == 2:
                    g = un // 4
                    dve.wait_ge(fb_hi, g + 1)
                    dve.tensor_tensor(u[:, 2 * g:2 * g + 2, T:2 * T], ps[:, 7, :].rearrange("p (c t) -> p c t", c=2),
                                      u[:, 2 * g:2 * g + 2, 0:T], ALU.subtract).then_inc(f_ready, 1)
                if un % 2 == 0 and un >= 2:
                    o_low(un // 2 - 1)
                if un == 6:
                    finish_unit(1, unit_col(1))
                if un == 14:
                    finish_unit(2, unit_col(2))
            o_low(HEADS - 1)

            def zero_squares(j):
                dve.memset(ssq, 0.0).then_inc(ssq_zeroed, 1)
                dve.wait_ge(ssq_zeroed, j + 1)

            def add_squares(n, j):
                dve.wait_ge(ysq_ready, n + 1)
                dve.tensor_tensor(ssq, ssq, sq, ALU.add).then_inc(ssq_done, 1)
                dve.wait_ge(ssq_done, n + 1)

            def take_y(j):
                def f(pg, bank, i):
                    add_halves(pg, bank, y[:, bass.ds(i * 2, 2), :])
                    add_squares(i + 8 * j, j)
                return f

            zero_squares(0)
            stage(PG_WO, 4, U_WO, 4, take_y(0), u_par=0)
            finish_unit(3, unit_col(3))

            def take_y_second(j):
                def f(pg, bank, i):
                    add_halves(pg, bank, y[:, bass.ds(i * 2 + 8, 2), :])
                    add_squares(i + (8 * j + 4), j)
                return f
            stage(PG_WO + 4, 4, U_WO + 1, 4, take_y_second(0), u_par=1)
            finish_unit(4, unit_col(4))

            def boundary(j, gate, gain, scale, gain2, shift, last_unit):
                if last_unit is not None:
                    finish_unit(last_unit, unit_col(last_unit))
                dve.wait_ge(mod_ready, MOD_NEEDED[j])
                dve.tensor_tensor(der[:, 0, :], vt[:, gate:gate + KC], gT[:, gain:gain + KC],
                                  ALU.mult).then_inc(der_step, 1)
                if scale is not None:
                    dve.scalar_tensor_tensor(out=der[:, 1, :], in0=vt[:, scale:scale + KC], scalar=1.0,
                                             in1=gT[:, gain2:gain2 + KC], op0=ALU.add,
                                             op1=ALU.mult).then_inc(der_step, 1)
                dve.wait_ge(der_step, 2 * j + (2 if scale is not None else 1))
                reciprocal_root(3 + 2 * j, 0)

                def scale_y(b):
                    for c in range(4 * b, 4 * b + 4):
                        last = dve.scalar_tensor_tensor(out=y[:, c, :], in0=y[:, c, :], scalar=der[:, 0, c:c + 1],
                                                        in1=stat[:, 1, :], op0=ALU.mult, op1=ALU.mult)
                    last.then_inc(y_scaled, 1)
                scale_y(0)
                for b in range(4):
                    if b < 3:
                        scale_y(b + 1)
                    dve.wait_ge(y_scaled, 4 * j + b + 1)
                    dve.tensor_tensor(x[:, 4 * b:4 * b + 4, :], x[:, 4 * b:4 * b + 4, :], y[:, 4 * b:4 * b + 4, :],
                                      ALU.add).then_inc(x_step, 1)
                if scale is None:
                    return
                reciprocal_root(4 + 2 * j, 2)
                dve.wait_ge(x_step, 4 * j + 4)
                modulate(32 + 16 * j, [(x[:, c, :], u[:, c, :], ff[:, (12 + c % 4) * T:(13 + c % 4) * T],
                                        der[:, 1, c:c + 1], vt[:, shift + c:shift + c + 1], stat[:, 3, :])
                                       for c in range(KC)])

            def mlp(l, u0, loop_units):
                pg0 = PG_MLP[l]

                def take_h(q):
                    def f(pg, bank, i):
                        n = q * 8 + i + 32 * l
                        add_halves(pg, bank, tsum)
                        dve.wait_ge(sum_done, pg + 1)
                        dve.scalar_tensor_tensor(out=relu2, in0=tsum, scalar=0.0, in1=tsum, op0=ALU.max,
                                                 op1=ALU.mult).then_inc(relu2_ready, 1)
                        dve.wait_ge(h_hi, n + 1)
                        dve.wait_ge(relu2_ready, n + 1)
                        dve.tensor_tensor(h[:, bass.ds(i * 2, 2), T:2 * T], relu2, h[:, bass.ds(i * 2, 2), 0:T],
                                          ALU.subtract).then_inc(h_ready, 1)
                        dve.wait_ge(h_ready, n + 1)
                    return f

                def add_to_y(q):
                    def f(pg, bank, i):
                        n = q * 8 + i + (24 * l - 8)
                        yi = y[:, bass.ds(i * 2, 2), :]
                        dve.wait_ge(b_copied, pg + 1)
                        dve.tensor_tensor(yi, ps[:, bank:bank + 2, 0:T], yi, ALU.add).then_inc(y_part, 1)
                        dve.wait_ge(y_part, n + 1)
                        dve.tensor_tensor(yi, tmp[:, :, :], yi, ALU.add).then_inc(sum_done, 1)
                    return f

                def quarter(q, un, n_m, col, take2, first=False):
                    stage(pg0, 8, un, n_m, take_h(q), q, 0)
                    if n_m and not first:
                        finish_unit(un - 1, col - 8)
                    stage(pg0 + 8, 8, un + 1, n_m, take2, q, 1)
                    if n_m:
                        finish_unit(un, col)
                quarter(0, u0, 2, unit_col(u0), lambda pg, bank, i: add_halves(pg, bank, y[:, bass.ds(i * 2, 2), :]),
                        first=True)
                with dve.Fori(0, 2) as q:
                    quarter(q + 1, q * 2 + (u0 + 2), loop_units, q * KC + unit_col(8), add_to_y(q + 1))

                def take_last(pg, bank, i):
                    add_to_y(3)(pg, bank, i)
                    add_squares(i + (8 + 16 * l), 1 + 2 * l)
                stage(pg0, 8, u0 + 6, loop_units, take_h(3), 3, 0)
                if loop_units:
                    finish_unit(u0 + 5, unit_col(u0 + 5))
                else:
                    finish_unit(u0 + 1, unit_col(u0 + 1))
                zero_squares(1 + 2 * l)
                if l == 0:
                    stage(pg0 + 8, 8, u0 + 7, loop_units, take_last, 3, 1)
                    finish_unit(u0 + 6, unit_col(u0 + 6))
                    return
                pg1, w1 = pg0 + 56, slab_of(pg0 + 56)
                with dve.Fori(0, 3) as b:
                    for j in range(2):
                        los(b * 8 + (w1 + 4 * j + 4))
                        take_last(b * 2 + (pg1 + j), 2 * j, b * 2 + j)
                los(w1 + 28)
                take_last(pg1 + 6, 0, 6)
                take_last(pg1 + 7, 2, 7)

            boundary(0, 2 * KC, KC, 4 * KC, 2 * KC, 3 * KC, 5)
            mlp(0, U_MLP0, 2)
            L1, G1 = 6 * KC, 4 * KC
            boundary(1, 5 * KC, 3 * KC, L1 + KC, G1, L1, None)

            dve.memset(zpad[:, :, 0:1], 0.0)
            dve.memset(zpad[:, :, T + 1:T + 2], 0.0).then_inc(z_edges, 1)
            dve.wait_ge(z_edges, 1)

            def triples(t0, un, u_par):
                with dve.Fori(0, 4) as t:
                    tt = t + t0
                    for j, dst in enumerate((cgb, cgc, cxv)):
                        pg = t * 3 + (PG_CONV + 3 * t0 + j)
                        w = t * 12 + (slab_of(PG_CONV) + 12 * t0 + 4 * j + 4)
                        for s in range(SLOTS):
                            lo(w + s, s)
                            i = 4 * j + s
                            if i % 3 == 2:
                                unit_slabs(un * UNIT + t * 4, un, t * 4, (i // 3,), u_par)
                        add_halves(pg, 2 * j, dst)
                    step = t * 5 + 5 * t0
                    dve.wait_ge(sum_done, t * 3 + (PG_CONV + 3 * t0 + 3))
                    dve.tensor_tensor(zpad[:, :, 1:T + 1], cgc, cxv, ALU.mult).then_inc(conv_step, 1)
                    dve.wait_ge(conv_step, step + 1)
                    for tap, first, wait in ((1, 1, 2), (0, 0, 3), (2, 2, 4)):
                        for m in range(2):
                            z = zpad[:, m, first:first + T]
                            w_tap = cwT[:, bass.ds(t * 2 + (tap * KC + 2 * t0 + m), 1)]
                            if tap == 1:
                                last = dve.tensor_scalar(cy[:, m, :], z, w_tap, None, ALU.mult)
                            else:
                                last = dve.scalar_tensor_tensor(out=cy[:, m, :], in0=z, scalar=w_tap, in1=cy[:, m, :],
                                                                op0=ALU.mult, op1=ALU.add)
                        last.then_inc(conv_step, 1)
                        dve.wait_ge(conv_step, step + wait)
                    dve.tensor_tensor(cv, cgb, cy, ALU.mult).then_inc(conv_step, 1)
                    dve.wait_ge(conv_step, step + 5)
                    dve.wait_ge(v_hi, tt + 1)
                    dve.tensor_tensor(h[:, bass.ds(t * 2 + 2 * t0, 2), T:2 * T], cv, h[:, bass.ds(t * 2 + 2 * t0, 2), 0:T],
                                      ALU.subtract).then_inc(conv_ready, 1)
                    dve.wait_ge(conv_ready, tt + 1)

            triples(0, U_CONV, 0)
            finish_unit(13, unit_col(13))
            triples(4, U_CONV + 1, 1)
            finish_unit(14, unit_col(14))
            zero_squares(2)
            stage(PG_CO, 4, U_CO, 4, take_y(2), u_par=0)
            finish_unit(15, unit_col(15))
            stage(PG_CO + 4, 4, U_CO + 1, 4, take_y_second(2), u_par=1)
            finish_unit(16, unit_col(16))
            boundary(2, L1 + 2 * KC, G1 + KC, L1 + 4 * KC, G1 + 2 * KC, L1 + 3 * KC, 17)
            mlp(1, U_MLP1, 0)
            boundary(3, L1 + 5 * KC, G1 + 3 * KC, None, None, None, None)

        @block.gpsimd
        def _(pool):
            pool.wait_ge(small_t, 1)
            pool.wait_ge(row_t, 4)
            for i in range(2):
                pool.memset(acc[:, i, :], 0.0).then_inc(acc_zeroed, 1)
            for un in range(len(UNITS)):
                pool.wait_ge(m_used, UNIT * (un + 1))
                if un:
                    pool.wait_ge(unit_read, un)
                pool.partition_all_reduce(red[:, :], acc[:, un % 2, :], P, RADD).then_inc(unit_summed, 1)
                pool.wait_ge(unit_summed, un + 1)
                r = red[:, :].rearrange("p (c f) -> p c f", f=P)
                pool.tensor_tensor(r, r, ident.unsqueeze(1).broadcast_to([P, KC // 2, P]), ALU.mult).then_inc(unit_masked, 1)
                if un + 2 < len(UNITS):
                    pool.memset(acc[:, un % 2, :], 0.0).then_inc(acc_zeroed, 1)


MOD_NEEDED = (6, 13, 18, 20)


def shape_tables():
    import numpy as np

    f = np.float32
    t = np.zeros((P, TAB_W), f)
    t[:, 0:128] = np.eye(P)
    t[:, 128:256] = 1
    tok = np.arange(T)
    inv_freq = f(10000.0) ** (-np.arange(0, 64, 2, dtype=f) / f(64))
    for p in range(P):
        axis, second, i = p // 64, (p % 64) // 32, p % 32
        pos = (tok // 64, tok % 64)[axis].astype(f)
        ang = pos * inv_freq[i]
        t[p, 256:512] = np.cos(ang)
        t[p, 512:768] = np.sin(ang) if second else -np.sin(ang)
    q, k = np.arange(P)[:, None], np.arange(P)[None, :]
    t[:, 768:896] = np.where(k <= q, 0, -1e30)
    t[:, 896:1024] = np.where(q <= k, 0, -1e30)
    i = np.arange(T)
    ang = 2 * np.pi * ((i[:, None] * i[None, :]) % T) / T
    dft = np.concatenate([np.cos(ang), np.sin(ang)], axis=1).astype(f)
    t[:, 1024:2048] = dft.reshape(2, P, 2 * T).transpose(1, 0, 2).reshape(P, 4 * T)
    t[0:4, SEL_COL:SEL_COL + 2] = [[1, 0], [0, 1], [1, 0], [0, 1]]
    t[:, EPS_COL] = 1e-6
    return t


_INS = ["x", "c", "ctx", "c_ctx", "w_mod", "b_mod", "norm_gains", "att_w_in", "att_sink", "att_w_out", "conv_w_in",
        "conv_w", "conv_w_out", "mlp_w1", "mlp_w2"]


def kernel(**inputs):
    import numpy as _np
    import concourse.bacc as _bacc
    from concourse import mybir as _mybir
    from concourse.bass_utils import run_bass_kernel_spmd as _run

    nc = _bacc.Bacc("TRN2", target_bir_lowering=False, num_devices=1)
    arrays = {f"in_{n}_dram": _np.ascontiguousarray(inputs[n]) for n in _INS}
    arrays["tables_dram"] = shape_tables()
    args = [nc.dram_tensor(n, a.shape, _mybir.dt.from_np(a.dtype), kind="ExternalInput").ap()
            for n, a in arrays.items()]
    args.append(nc.dram_tensor("out_0_dram", (1, T, D), F32, kind="ExternalOutput").ap())
    backbone_program(nc, *args)
    r = _run(nc, [arrays], core_ids=[0])
    return r.results[0]["out_0_dram"]
```

```python
from contextlib import ExitStack

import concourse.bass as bass
from concourse import mybir

F32 = mybir.dt.float32
F32R = mybir.dt.float32r
ALU = mybir.AluOpType
ACT = mybir.ActivationFunctionType
AX_X = mybir.AxisListType.X
RADD = bass.bass_isa.ReduceOp.add

P = 128
D = 2048
T = 256
KC = D // P
GW = 256
SLOTS = 4
CPS = KC // SLOTS
HEADS, KV_HEADS, HD = 8, 2, 128
GQA = HEADS // KV_HEADS
FOURIER = D // 2
FG = 4
D_FF = 4 * D
QUARTERS = D_FF // D
SCALE = float(HD) ** -0.5
EPS_COL, TAB_W = 2048, 2050
HALF = D // 2
UNIT = KC

W_START = 0
START_GROUPS = 16
PG_Q, PG_K, PG_V, PG_F = 0, 4, 6, 8
PG_WO = 12
PG_MLP = (20, 116)
PG_CONV = 84
PG_CO = 108
W_Q, W_K, W_V = 64, 80, 84


def slab_of(pg):
    return 4 * pg + 56


UNITS = [(0, 2, 0), (0, 2, 1), (0, 4, 0), (0, 4, 1), (0, 3, 0), (0, 3, 1), (0, 5, 0), (0, 5, 1),
         (1, 0, 0), (1, 0, 1), (1, 1, 0), (1, 1, 1), (1, 2, 0), (1, 2, 1), (1, 4, 0), (1, 4, 1),
         (1, 3, 0), (1, 3, 1), (1, 5, 0), (1, 5, 1)]
U_MID, U_WO, U_MLP0, U_CONV, U_CO, U_MLP1 = 2, 4, 6, 14, 17, 18
HOOKS = ((), (), (), (0,), (1,), (2, 3))
BATCHES = ((0, 1), (1, 1), (2, 2), (4, 4), (8, 4), (12, 4))


def unit_col(u):
    l, v, h = UNITS[u]
    return l * 6 * KC + v * KC + h * (KC // 2)


def backbone_program(nc, x_in, c_in, ctx_in, c_ctx, w_mod, b_mod, gains, att_w_in, sink, att_w_out,
                     conv_w_in, conv_w, conv_w_out, mlp_w1, mlp_w2, tables, out):
    with ExitStack() as ctx:
        def sb(name, shape, dt=F32):
            return ctx.enter_context(nc.sbuf_tensor(name, shape, dt))

        def sem(name):
            return ctx.enter_context(nc.semaphore(name))

        x = sb("x", [P, KC, T])
        u = sb("u", [P, KC, 2 * T], F32R)
        h = sb("h", [P, KC, 2 * T], F32R)
        y = sb("y", [P, KC, T])
        fq = sb("fq", [P, KC, T])
        raw = sb("raw", [P, SLOTS, 1024])
        whi = sb("whi", [P, SLOTS, 1024], F32R)
        wlo = sb("wlo", [P, SLOTS, 1024], F32R)
        mraw = sb("mraw", [P, 2, HALF])
        acc = sb("acc", [P, 2, HALF])
        red = sb("red", [P, HALF])
        kT = sb("kT", [P, KV_HEADS, 2 * T])
        v = sb("v", [P, 4, KV_HEADS * HD])
        tab = sb("tab", [P, TAB_W])
        tmp = sb("tmp", [P, 2, T])
        stat = sb("stat", [P, 4, T])
        small = sb("small", [P, 400])
        vt = sb("vt", [P, 12 * KC])
        modc = sb("modc", [P, 2, 2 * KC])
        cs = sb("cs", [P, 2 * KC])
        sg = sb("sg", [P, 2 * KC])
        der = sb("der", [P, 2, KC])
        t8 = sb("t8", [P, KC // 2])
        nsink = sb("nsink", [P, 2, HEADS])
        sinkr = sb("sinkr", [1, HEADS])
        sm = sb("sm", [P, 5, 2 * HEADS])
        ps = ctx.enter_context(nc.psum_tensor("ps", [P, 8, 512], F32))

        ident, ones = tab[:, 0:128], tab[:, 128:256]
        cosT, sinT = tab[:, 256:512], tab[:, 512:768]
        masks = (tab[:, 768:896], tab[:, 896:1024])
        dft = tab[:, 1024:2048].rearrange("p (k n) -> p k n", k=2)
        eps = tab[:, EPS_COL:EPS_COL + 1]
        cT, gT = small[:, 0:32], small[:, 32:160]
        bT, cwT = small[:, 160:352], small[:, 352:400]
        xf = x[:, :, :].rearrange("p c t -> p (c t)")
        yf = y[:, :, :].rearrange("p c t -> p (c t)")
        ff = fq[:, :, :].rearrange("p c t -> p (c t)")
        qs, qsw = y[:, 0:2, :], y[:, 2:4, :]
        qh = y[:, 8:16, :]
        vsum = yf[:, 1024:2048].rearrange("p (g t) -> p g t", g=2)
        prob = [yf[:, 512 * i:512 * i + 512] for i in range(2)]
        probT = [ff[:, 2048 + 1024 * i:3072 + 1024 * i].rearrange("p (k q) -> p k q", k=4) for i in range(2)]
        ucs = yf[:, 1024:2048].rearrange("p (k n) -> p k n", k=2)
        row = (red[0:4, :], acc[0:4, 1, :])
        sqx = [ff[:, 1024 * i:1024 * i + 1024] for i in range(2)]
        ssq, sq = fq[:, 8:10, :], fq[:, 10:12, :]
        tsum, relu2 = fq[:, 8:10, :], fq[:, 10:12, :]
        cgc, cxv, cgb = fq[:, 8:10, :], fq[:, 10:12, :], fq[:, 12:14, :]
        zpad = ff[:, 0:2 * (T + 2)].rearrange("p (m t) -> p m t", m=2)
        cy = ff[:, 1024:1536].rearrange("p (m t) -> p m t", m=2)
        cv = ff[:, 1536:2048].rearrange("p (m t) -> p m t", m=2)

        tab_landed, small_landed, x_landed, ctx_landed = (sem(n) for n in (
            "tab_landed", "small_landed", "x_landed", "ctx_landed"))
        w_landed = [sem(f"w_landed{i}") for i in range(SLOTS)]
        m_landed = [sem(f"m_landed{i}") for i in range(2)]
        hi_ready, lo_ready, slab_used, m_used = (sem(n) for n in ("hi_ready", "lo_ready", "slab_used", "m_used"))
        b_copied, sum_done, y_part = (sem(n) for n in ("b_copied", "sum_done", "y_part"))
        small_t, small_copied, silu_exp, silu_step, crs_hi, crs_lo, crs_zero = (sem(n) for n in (
            "small_t", "small_copied", "silu_exp", "silu_step", "crs_hi", "crs_lo", "crs_zero"))
        sink_b, sink_copied = sem("sink_b"), sem("sink_copied")
        x_t, x_copied, ctx_t, ctx_copied = (sem(n) for n in ("x_t", "x_copied", "ctx_t", "ctx_copied"))
        row_copied, row_t, modc_step = sem("row_copied"), sem("row_t"), sem("modc_step")
        acc_zeroed, unit_summed, unit_masked, unit_read, mod_ready = (sem(n) for n in (
            "acc_zeroed", "unit_summed", "unit_masked", "unit_read", "mod_ready"))
        norm_sum, sd_ready, rstd_ready, sq_ready, sq_used, x_step, y_scaled = (sem(n) for n in (
            "norm_sum", "sd_ready", "rstd_ready", "sq_ready", "sq_used", "x_step", "y_scaled"))
        ysq_ready, ssq_done, ssq_zeroed, gg_ready, gs_ready, yg_ready = (sem(n) for n in (
            "ysq_ready", "ssq_done", "ssq_zeroed", "gg_ready", "gs_ready", "yg_ready"))
        u_scaled, u_shifted, u_shifted_dve, u_hi, u_ready = (sem(n) for n in (
            "u_scaled", "u_shifted", "u_shifted_dve", "u_hi", "u_ready"))
        c_scaled, c_shifted, c_hi, c_ready = (sem(n) for n in ("c_scaled", "c_shifted", "c_hi", "c_ready"))
        rope_step, v_t, v_ready = sem("rope_step"), sem("v_t"), sem("v_ready")
        s_done, masked, max_ready, negm_ready, p_ready, den_ready, rden_ready, pn_ready = (sem(n) for n in (
            "s_done", "masked", "max_ready", "negm_ready", "p_ready", "den_ready", "rden_ready", "pn_ready"))
        pt_done, pt_copied, pv_done, o_hi, o_ready = (sem(n) for n in (
            "pt_done", "pt_copied", "pv_done", "o_hi", "o_ready"))
        fa_done, fa_copied, fb_done, fb_hi, f_ready = (sem(n) for n in (
            "fa_done", "fa_copied", "fb_done", "fb_hi", "f_ready"))
        relu2_ready, h_hi, h_ready = sem("relu2_ready"), sem("h_hi"), sem("h_ready")
        z_edges, conv_step, v_hi, conv_ready = sem("z_edges"), sem("conv_step"), sem("v_hi"), sem("conv_ready")
        out_t, out_copied, out_stored = sem("out_t"), sem("out_copied"), sem("out_stored")

        def modc_col(what, which):
            return modc[:, what, :].rearrange("p (c w) -> p c w", w=2)[:, :, which:which + 1]

        def four_chunks(a):
            return a.rearrange("p (c t) -> p c t", c=4)

        start_xr = [four_chunks(yf[:, 1024 * i:1024 * i + 1024]) for i in range(2)]
        start_mt = [four_chunks(yf[:, 2048 + 1024 * i:3072 + 1024 * i]) for i in range(2)]
        late_xr = [four_chunks(ff[:, 1024 * i:1024 * i + 1024]) for i in range(2)]
        late_mt = [four_chunks(ff[:, 2048 + 1024 * i:3072 + 1024 * i]) for i in range(2)]

        block = ctx.enter_context(nc.Block())

        @block.sync
        def _(sp):
            def rows(t):
                return t.rearrange("(c p) -> c p", p=P)

            stage = acc[:, 0, :]
            sp.dma_start(tab[:, :], tables).then_inc(tab_landed, 16)
            sp.dma_start(stage[0:16, 0:128], rows(c_in.rearrange("a d -> (a d)"))).then_inc(small_landed, 16)
            sp.dma_start(stage[16:32, 0:128], rows(c_ctx)).then_inc(small_landed, 16)
            sp.dma_start(stage[:, 128:256], gains.rearrange("l g (c p) -> (l g c) p", p=P)).then_inc(small_landed, 16)
            for l in range(2):
                sp.dma_start(stage[0:96, 256 + 128 * l:384 + 128 * l],
                             b_mod[l].rearrange("(c p) -> c p", p=P)).then_inc(small_landed, 16)
            sp.dma_start(stage[0:48, 512:640], conv_w.rearrange("a k (c p) -> (a k c) p", p=P)).then_inc(small_landed, 16)
            sp.dma_start(sinkr[:, :], sink).then_inc(small_landed, 16)
            sp.dma_start(fq[:, :, :].rearrange("p c t -> p (c t)").rearrange("p (a d) -> p a d", a=2),
                         x_in[0].rearrange("(a p) d -> p a d", p=P)).then_inc(x_landed, 16)
            def load_slab(w, s, src):
                if not (isinstance(w, int) and w < SLOTS):
                    sp.wait_ge(lo_ready, w - (SLOTS - 1))
                sp.dma_start(raw[:, s, :].rearrange("p (c n) -> p c n", c=CPS), src).then_inc(w_landed[s], 16)

            def w_slab(wt, row0, col0, s):
                return wt[bass.ds(row0 + s * CPS * P, CPS * P), bass.ds(col0, GW)].rearrange("(c p) n -> p c n", p=P)

            def load_unit_slab(m, slot, l, k, col0):
                if not (isinstance(m, int) and m < 2):
                    sp.wait_ge(m_used, m - 1)
                sp.dma_start(mraw[:, slot, :], w_mod[l, bass.ds(k * P, P), bass.ds(col0, HALF)]).then_inc(m_landed[slot], 16)

            def group_and_units(w0, wt, row0, col0, m0, k0, l, mcol, n_m):
                for s in range(SLOTS):
                    if wt is not None:
                        load_slab(w0 + s, s, w_slab(wt, row0, col0, s))
                    for j in range(s * n_m // SLOTS, (s + 1) * n_m // SLOTS):
                        load_unit_slab(m0 + j, j % 2, l, k0 + j, mcol)

            def stage_loads(w0, wt, row0, col0, n, m0, k_per_group, l, mcol, ahead):
                km = k_per_group
                def pair(b):
                    for j in range(2):
                        group_and_units(w0 + b * 8 + 4 * (j + 1), wt, row0, col0 + (b * 2 + (j + 1)) * GW,
                                        m0 + b * (2 * km) + j * km, b * (2 * km) + j * km, l, mcol, km)
                if n == 4:
                    pair(0)
                else:
                    with sp.Fori(0, n // 2 - 1) as b:
                        pair(b)
                b = n // 2 - 1
                group_and_units(w0 + (8 * b + 4), wt, row0, col0 + (2 * b + 1) * GW, m0 + 2 * b * km, 2 * b * km,
                                l, mcol, km)
                group_and_units(w0 + (8 * b + 8), *ahead, m0 + (2 * b + 1) * km, (2 * b + 1) * km, l, mcol, km)

            for hv in range(4):
                col0 = (1 - hv // 2) * D + (hv % 2) * HALF
                for k in range(KC):
                    w = W_START + hv * KC + k
                    load_slab(w, w % SLOTS, w_mod[0, k * P:(k + 1) * P, col0:col0 + HALF].rearrange(
                        "p (c n) -> p c n", c=CPS))
                if hv == 0:
                    sp.dma_start(yf.rearrange("p (a d) -> p a d", a=2),
                                 ctx_in[0].rearrange("(a p) d -> p a d", p=P)).then_inc(ctx_landed, 16)
            wi, wo = att_w_in[0], att_w_out[0]
            mcol = lambda un: UNITS[un][1] * D + UNITS[un][2] * HALF
            for s in range(SLOTS):
                load_slab(W_Q + s, s, w_slab(wi, 0, 1024, s))
            sp.wait_ge(sq_used, 8)
            m = 0
            for i, (wt, col0) in enumerate([(wi, 1280), (wi, 1536), (wi, 1792), (wi, 2048), (wi, 2304), (wi, 0),
                                            (wi, 256), (wi, 512), (wi, 768), (wo, 0)]):
                n_m = UNIT_SHARE[i]
                group_and_units(W_Q + 4 * (i + 1), wt, 0, col0, m, m % UNIT, 0, mcol(m // UNIT), n_m)
                m += n_m
            for un in (U_MID, U_MID + 1):
                for k in range(KC):
                    load_unit_slab(UNIT * un + k, k % 2, 0, k, mcol(un))
            stage_loads(slab_of(PG_WO), wo, 0, 0, 4, UNIT * U_WO, 4, 0, mcol(U_WO), (wo, 0, 4 * GW))
            stage_loads(slab_of(PG_WO + 4), wo, 0, 4 * GW, 4, UNIT * (U_WO + 1), 4, 0, mcol(U_WO + 1),
                        (mlp_w1[0], 0, 0))

            def mlp_loads(l, u0, loop_units, ahead):
                w1, w2 = mlp_w1[l], mlp_w2[l]
                w0 = slab_of(PG_MLP[l])

                def quarter(q, un, n_m, ml, mc1, mc2, nxt):
                    stage_loads(w0 + q * 64, w1, 0, q * D, 8, un * UNIT, n_m, ml, mc1, (w2, q * D, 0))
                    stage_loads(w0 + q * 64 + 32, w2, q * D, 0, 8, un * UNIT + UNIT, n_m, ml, mc2, nxt)
                quarter(0, u0, 2, l, 5 * D, 5 * D + HALF, (w1, 0, D))
                with sp.Fori(0, 2) as q:
                    quarter(q + 1, q * 2 + (u0 + 2), loop_units, 1, q * D, q * D + HALF, (w1, 0, (q + 2) * D))
                quarter(3, u0 + 6, loop_units, 1, 2 * D, 2 * D + HALF, ahead)

            mlp_loads(0, U_MLP0, 2, (conv_w_in[0], 0, D))
            ci = conv_w_in[0]

            def triple_loads(t, t0, w0, m0, k0, l, col, n_m, nxt_w, nxt_col):
                for j, (wt, col0) in enumerate(((ci, t * GW + (t0 * GW + 2 * D)), (ci, t * GW + t0 * GW),
                                                 (nxt_w, nxt_col))):
                    for s in range(SLOTS):
                        load_slab(w0 + (4 * (j + 1) + s), s, w_slab(wt, 0, col0, s))
                        for i in conv_unit_slabs(4 * j + s, n_m):
                            load_unit_slab(m0 + i, i % 2, l, k0 + i, col)

            w0 = slab_of(PG_CONV)
            for t0, n_t, un, n_m in CONV_PARTS:
                whole = n_t if t0 + n_t < 8 else n_t - 1
                with sp.Fori(1, whole + 1) as t:
                    triple_loads(t, t0 - 1, t * 12 + (w0 + 12 * (t0 - 1)), t * n_m + (UNIT * un - n_m),
                                 t * n_m - n_m, 1, mcol(un), n_m, ci, t * GW + (D + t0 * GW))
            triple_loads(7, 0, w0 + 84, UNIT * un + 7 % n_t * n_m, 7 % n_t * n_m, 1, mcol(un), n_m, conv_w_out[0], 0)
            co = conv_w_out[0]
            stage_loads(slab_of(PG_CO), co, 0, 0, 8, UNIT * U_CO, 2, 1, mcol(U_CO), (mlp_w1[1], 0, 0))
            mlp_loads(1, U_MLP1, 0, (None, 0, 0))
            for b in range(4):
                for a in range(2):
                    sp.wait_ge(out_copied, 2 * b + a + 1)
                    sp.dma_start(out[0, a * P:(a + 1) * P, b * 512:(b + 1) * 512],
                                 ff[:, a * D + b * 512:a * D + (b + 1) * 512]).then_inc(out_stored, 16)
            sp.wait_ge(out_stored, 16 * 8)

        @block.tensor
        def _(pe):
            stage = acc[:, 0, :]
            pe.wait_ge(tab_landed, 16)
            pe.wait_ge(small_landed, 7 * 16)
            for n, col, dst in ((32, 0, 0), (128, 128, 32), (96, 256, 160), (96, 384, 256), (48, 512, 352)):
                last = pe.transpose(ps[:, 3, dst:dst + n], stage[0:n, col:col + 128], ident[0:n, 0:n])
            last.then_inc(small_t, 1)
            pe.matmul(ps[:, 2, 0:HEADS], ones[0:1, :], sinkr[:, :], start=True, stop=True).then_inc(sink_b, 1)

            def turn_input(src, landed, turned, copied, bank):
                pe.wait_ge(landed, 16)
                for i in range(8):
                    if i >= 2:
                        pe.wait_ge(copied, i - 1)
                    for c in range(2):
                        for a in range(2):
                            last = pe.transpose(ps[:, bank + i % 2, c * T + a * P:c * T + (a + 1) * P],
                                                src[:, a * D + (2 * i + c) * P:a * D + (2 * i + c + 1) * P], ident)
                    last.then_inc(turned, 1)
            turn_input(ff, x_landed, x_t, x_copied, 4)

            def sums_of_squares(bank, n0):
                for b in range(4):
                    pe.wait_ge(sq_ready, n0 + b + 1)
                    for c in range(4):
                        last = pe.matmul(ps[:, bank, 0:T], ones, sqx_of(n0 + b)[:, c * T:(c + 1) * T],
                                         start=(b == 0 and c == 0), stop=(b == 3 and c == 3))
                    last.then_inc(sq_used, 1)

            def sqx_of(n):
                return mraw[:, n % 2, :] if n < 8 else sqx[n % 2]

            pe.wait_ge(crs_lo, 1)

            def mod_rows(hv):
                bank = 2 * (hv % 2)
                if hv >= 2:
                    pe.wait_ge(row_copied, hv - 1)
                if hv == 1:
                    pe.wait_ge(small_copied, 1)
                    pe.wait_ge(sink_copied, 1)
                for k in range(KC):
                    w = hv * KC + k
                    pe.wait_ge(lo_ready, w + 1)
                    for part in (whi, wlo):
                        for n in range(2):
                            last = pe.matmul(ps[:, bank + n, :], u[:, k, 0:128],
                                             part[:, w % SLOTS, n * 512:(n + 1) * 512],
                                             start=(k == 0 and part is whi), stop=(k == KC - 1 and part is wlo))
                    last.then_inc(slab_used, 1)

            def turn_rows(hv):
                pe.wait_ge(row_copied, hv + 1)
                for c in range(8):
                    last = pe.transpose(ps[:, 7, hv * 32 + 4 * c:hv * 32 + 4 * c + 4],
                                        row[hv % 2][:, c * P:(c + 1) * P], ident[0:4, 0:4])
                last.then_inc(row_t, 1)

            mod_rows(0)
            turn_input(yf, ctx_landed, ctx_t, ctx_copied, 6)
            pe.wait_ge(ctx_copied, 8)
            sums_of_squares(6, 0)
            mod_rows(1)
            pe.wait_ge(sd_ready, 1)
            sums_of_squares(6, 4)
            turn_rows(0)
            mod_rows(2)
            turn_rows(1)
            mod_rows(3)
            turn_rows(2)
            turn_rows(3)

            def group(pg, w0, src, banks, input_waits, src2=None, free=None):
                if not (isinstance(pg, int) and pg < 2):
                    pe.wait_ge(sum_done, pg - 1 if free is None else free)
                for s in range(SLOTS):
                    pe.wait_ge(lo_ready, w0 + (s + 1))
                    for sm_, n in input_waits(s):
                        pe.wait_ge(sm_, n)
                    for c in range(CPS):
                        k = s * CPS + c
                        for m in range(2):
                            for i, inp in enumerate((src,) if src2 is None else (src, src2)):
                                bk = banks[2 * i + m]
                                pe.matmul(ps[:, bk, :], whi[:, s, c * GW + m * P:c * GW + (m + 1) * P], inp[:, k, :],
                                          start=(k == 0), stop=False)
                                last = pe.matmul(ps[:, bk, 0:T], wlo[:, s, c * GW + m * P:c * GW + (m + 1) * P],
                                                 inp[:, k, 0:T], start=False, stop=(k == KC - 1))
                        if c == CPS - 1:
                            last.then_inc(slab_used, 1)

            u_waits = lambda base: (lambda s: [(u_ready, base + s + 3)])

            def stage_groups(pg0, n, src, input_waits, w0=None):
                with pe.Fori(0, n // 2) as b:
                    for j in range(2):
                        w = (slab_of(pg0) if w0 is None else w0) + 4 * j
                        pe_pg = b * 2 + (pg0 + j)
                        group(pe_pg, b * 8 + w, src, (2 * j, 2 * j + 1), input_waits)

            for i in range(4):
                group(PG_Q + i, W_Q + 4 * i, u, (2 * (i % 2), 2 * (i % 2) + 1), u_waits(0) if i == 0 else lambda s: [])
            group(PG_K, W_K, u, (0, 1, 4, 5), lambda s: [(c_ready, s + 1)], h)
            group(PG_V, W_V, u, (2, 3, 6, 7), lambda s: [], h, free=4)
            stage_groups(PG_F, 4, u, lambda s: [])

            pe.wait_ge(sum_done, PG_WO)
            pe.wait_ge(rope_step, 4 * 5)

            def scores(un):
                hd, qt = divmod(un, 2)
                if un >= 3:
                    pe.wait_ge(p_ready, un - 2)
                pe.matmul(ps[:, un % 3, :], qh[:, hd, qt * P:(qt + 1) * P], kT[:, hd // GQA, :],
                          start=True, stop=True).then_inc(s_done, 1)

            def turn_probs(un):
                pe.wait_ge(pn_ready, un + 1)
                if un >= 2:
                    pe.wait_ge(pt_copied, un - 1)
                for kt in range(4):
                    last = pe.transpose(ps[:, 4 + un % 2, kt * P:(kt + 1) * P], prob[un % 2][:, kt * P:(kt + 1) * P],
                                        ident)
                last.then_inc(pt_done, 1)

            def values(hd):
                pe.wait_ge(pt_copied, 2 * hd + 2)
                if hd >= 1:
                    pe.wait_ge(o_ready, hd)
                for kt in range(4):
                    last = pe.matmul(ps[:, 6, (hd % 2) * T:(hd % 2 + 1) * T],
                                     v[:, kt, (hd // GQA) * HD:(hd // GQA + 1) * HD], probT[hd % 2][:, kt, :],
                                     start=(kt == 0), stop=(kt == 3))
                last.then_inc(pv_done, 1)

            def channel_dft(g, a):
                if 2 * g + a >= 1:
                    pe.wait_ge(fa_copied, 2 * (2 * g + a))
                for kc in range(2):
                    last = pe.matmul(ps[:, 3, :], fq[:, 2 * g + kc, a * P:(a + 1) * P], dft[:, kc, :],
                                     start=(kc == 0), stop=(kc == 1))
                last.then_inc(fa_done, 1)

            def token_dft(g, m):
                if m == 0:
                    pe.wait_ge(fa_copied, 4 * g + 4)
                    if g >= 1:
                        pe.wait_ge(f_ready, g)
                for i in range(4):
                    trig, a = divmod(i, 2)
                    last = pe.matmul(ps[:, 7, m * T:(m + 1) * T],
                                     ucs[:, a, trig * T + m * P:trig * T + (m + 1) * P],
                                     dft[:, a, trig * T:(trig + 1) * T], start=(i == 0), stop=(i == 3))
                last.then_inc(fb_done, 1)

            for un in range(3):
                scores(un)
            for kv in range(KV_HEADS):
                for kt in range(4):
                    last = pe.transpose(ps[:, 4 + kv, kt * P:(kt + 1) * P], vsum[:, kv, kt * P:(kt + 1) * P], ident)
                last.then_inc(v_t, 1)
            pe.wait_ge(v_ready, KV_HEADS)
            for un in range(2 * HEADS):
                turn_probs(un)
                if un + 3 < 2 * HEADS:
                    scores(un + 3)
                (channel_dft if un % 4 < 2 else token_dft)(un // 4, un % 2)
                if un % 2 == 1 and un >= 3:
                    values(un // 2 - 1)
            values(HEADS - 1)

            pe.wait_ge(f_ready, FG)
            pe.wait_ge(o_ready, HEADS)
            stage_groups(PG_WO, 8, u, lambda s: [])

            def boundary_sums(j, n_sq):
                pe.wait_ge(ssq_done, 8 * (j + 1))
                for m in range(2):
                    last = pe.matmul(ps[:, 6, 0:T], ones, ssq[:, m, :], start=(m == 0), stop=(m == 1))
                last.then_inc(norm_sum, 1)
                if n_sq:
                    sums_of_squares(7, 8 + 4 * j)

            def mlp_groups(l):
                pg0 = PG_MLP[l]
                u0 = (6, 18)[l]
                h0 = 32 * l

                def quarter(q):
                    for part, src in ((0, u), (1, h)):
                        waits = u_waits(u0) if part == 0 else (lambda s: [(h_ready, q * 8 + (h0 + 2 * (s + 1)))])
                        with pe.Fori(0, 4) as b:
                            for j in range(2):
                                pg = q * 16 + b * 2 + (pg0 + 8 * part + j)
                                group(pg, q * 64 + b * 8 + (slab_of(pg0) + 32 * part + 4 * j), src,
                                      (2 * j, 2 * j + 1), waits)
                quarter(0)
                with pe.Fori(0, 2) as q:
                    quarter(q + 1)
                quarter(3)

            boundary_sums(0, 4)
            mlp_groups(0)
            boundary_sums(1, 4)
            with pe.Fori(0, 8) as t:
                for j in range(3):
                    group(t * 3 + (PG_CONV + j), t * 12 + (slab_of(PG_CONV) + 4 * j), u, (2 * j, 2 * j + 1), u_waits(12))
            with pe.Fori(0, 4) as b:
                for j in range(2):
                    group(b * 2 + (PG_CO + j), b * 8 + slab_of(PG_CO + j), h, (2 * j, 2 * j + 1),
                          lambda s: [(conv_ready, 2 * (s + 1))])
            boundary_sums(2, 4)
            mlp_groups(1)
            boundary_sums(3, 0)
            for b in range(4):
                pe.wait_ge(x_step, 13 + b)
                for a in range(2):
                    n = 2 * b + a
                    if n >= 4:
                        pe.wait_ge(out_copied, n - 3)
                    for c in range(4):
                        last = pe.transpose(ps[:, n % 4, c * P:(c + 1) * P], x[:, 4 * b + c, a * P:(a + 1) * P], ident)
                    last.then_inc(out_t, 1)

        @block.scalar
        def _(act):
            def hi(w, s):
                act.wait_ge(w_landed[s], w * 4 + (16 - 4 * s) if not isinstance(w, int) else 16 * (w // SLOTS + 1))
                if not (isinstance(w, int) and w < SLOTS):
                    act.wait_ge(slab_used, w - (SLOTS - 1))
                act.activation(whi[:, s, :], raw[:, s, :], ACT.Copy).then_inc(hi_ready, 1)

            def his(w0):
                for s in range(SLOTS):
                    hi(w0 + s, s)

            act.wait_ge(small_copied, 1)
            act.activation(sg[:, :], cT, ACT.Exp, scale=-1.0).then_inc(silu_exp, 1)
            act.wait_ge(silu_step, 3)
            act.wait_ge(crs_zero, 1)
            act.activation(u[:, :, 0:2], cs[:, :].rearrange("p (w k) -> p k w", w=2), ACT.Copy).then_inc(crs_hi, 1)

            def square(n, src):
                if n >= 2:
                    act.wait_ge(sq_used, n - 1)
                dst = mraw[:, n % 2, :] if n < 8 else sqx[n % 2]
                act.activation(dst, src, ACT.Square).then_inc(sq_ready, 1)

            def root(dst, bank):
                act.activation(dst, ps[:, bank, 0:T], ACT.Sqrt, bias=eps, scale=1.0 / D).then_inc(sd_ready, 1)

            def copy_row(hv):
                act.wait_ge(slab_used, UNIT * (hv + 1))
                if hv == 1:
                    act.wait_ge(small_t, 1)
                if hv >= 2:
                    act.wait_ge(row_t, hv - 1)
                bank = 2 * (hv % 2)
                act.activation(row[hv % 2].rearrange("p (m n) -> p m n", m=2), ps[0:4, bank:bank + 2, :],
                               ACT.Copy).then_inc(row_copied, 1)

            for g in range(4):
                his(4 * g)
            act.wait_ge(x_copied, 8)
            square(0, xf[:, 0:1024])
            square(1, xf[:, 1024:2048])
            his(16)
            copy_row(0)
            act.wait_ge(x_copied, 8)
            for i in range(8):
                act.wait_ge(ctx_t, i + 1)
                act.activation(fq[:, 2 * i:2 * i + 2, :], ps[:, 6 + i % 2, :].rearrange("p (c t) -> p c t", c=2),
                               ACT.Copy).then_inc(ctx_copied, 1)
            square(2, xf[:, 2048:3072])
            square(3, xf[:, 3072:4096])
            for g in range(5, 8):
                his(4 * g)
            act.wait_ge(sq_used, 4)
            root(stat[:, 0, :], 6)
            act.wait_ge(ctx_copied, 8)
            square(4, ff[:, 0:1024])
            square(5, ff[:, 1024:2048])
            his(32)
            copy_row(1)
            square(6, ff[:, 2048:3072])
            square(7, ff[:, 3072:4096])
            for g in range(9, 12):
                his(4 * g)
            act.wait_ge(sq_used, 8)
            root(stat[:, 2, :], 6)
            his(48)
            copy_row(2)
            for g in range(13, 16):
                his(4 * g)
            his(W_Q)
            copy_row(3)

            def modulate(n0, xr, mt, gs, shift, hooks):
                for b, (c0, n) in enumerate(BATCHES):
                    act.wait_ge(u_scaled, n0 + b + 1)
                    if n0 + b >= 2:
                        act.wait_ge(u_ready, n0 + b - 1)
                    mine = n if n < 4 else 3
                    for c in range(mine):
                        last = act.activation(mt[b % 2][:, c, :], xr[b % 2][:, c, :], ACT.Identity,
                                              scale=gs[:, c0 + c], bias=shift[:, c0 + c])
                    last.then_inc(u_shifted, 1)
                    act.wait_ge(u_shifted, n0 + b + 1)
                    if mine < n:
                        act.wait_ge(u_shifted_dve, n0 // 2 + b - 2)
                    act.activation(u[:, c0:c0 + n, 0:T], mt[b % 2][:, 0:n, :], ACT.Copy).then_inc(u_hi, 1)
                    for s in HOOKS[b]:
                        hooks(s)

            act.wait_ge(modc_step, 5)
            modulate(0, start_xr, start_mt, modc_col(0, 0), modc_col(1, 0), lambda s: hi(W_Q + 4 + s, s))

            def context_high(b):
                act.wait_ge(c_scaled, b + 1)
                for c in range(4 * b, 4 * b + 4):
                    last = act.activation(fq[:, c, :], fq[:, c, :], ACT.Identity, scale=modc_col(0, 1)[:, c],
                                          bias=modc_col(1, 1)[:, c])
                last.then_inc(c_shifted, 1)
                act.wait_ge(c_shifted, b + 1)
                act.activation(h[:, 4 * b:4 * b + 4, 0:T], fq[:, 4 * b:4 * b + 4, :], ACT.Copy).then_inc(c_hi, 1)

            def right_half(pg, bank, w_end):
                act.wait_ge(slab_used, w_end)
                if not (isinstance(pg, int) and pg == 0):
                    act.wait_ge(sum_done, pg)
                act.activation(tmp[:, :, :], ps[:, bank:bank + 2, T:2 * T], ACT.Copy).then_inc(b_copied, 1)

            for i in range(4):
                if i:
                    his(W_Q + 4 * i + 4)
                context_high(i)
                right_half(PG_Q + i, 2 * (i % 2), W_Q + 4 * i + 4)
            his(W_V)
            right_half(PG_K, 0, W_K + 4)
            right_half(PG_K + 1, 4, W_K + 4)
            his(slab_of(PG_F))
            right_half(PG_V, 2, W_V + 4)
            right_half(PG_V + 1, 6, W_V + 4)

            def stage(pg0, n, after, q=None, opened=False):
                w0 = slab_of(pg0)

                def pair(b, ready):
                    for j in range(2):
                        pg, w = b * 2 + (pg0 + j), b * 8 + (w0 + 4 * j)
                        if q is not None:
                            pg, w = q * 16 + pg, q * 64 + w
                        if not (ready and j == 0):
                            his(w + 4)
                        right_half(pg, 2 * j, w + 4)
                        after(pg, b * 2 + j)
                if opened:
                    pair(0, True)
                with act.Fori(1 if opened else 0, n // 2) as b:
                    pair(b, False)

            stage(PG_F, 4, lambda pg, i: None)

            def probabilities(un):
                hd = un // 2
                act.wait_ge(negm_ready, un + 1)
                if un >= 2:
                    act.wait_ge(pt_done, un - 1)
                act.activation(sm[:, 2, un:un + 1], nsink[:, 0, hd:hd + 1], ACT.Exp, bias=sm[:, 1, un:un + 1])
                act.activation(prob[un % 2], ps[:, un % 3, :], ACT.Exp, bias=sm[:, 1, un:un + 1], scale=SCALE,
                               accum_out=sm[:, 3, un:un + 1]).then_inc(p_ready, 1)

            def probs_turned(un):
                hd, qt = divmod(un, 2)
                act.wait_ge(pt_done, un + 1)
                if hd >= 2:
                    act.wait_ge(pv_done, hd - 1)
                act.activation(probT[hd % 2][:, :, qt * P:(qt + 1) * P],
                               ps[:, 4 + un % 2, :].rearrange("p (k q) -> p k q", k=4), ACT.Copy).then_inc(pt_copied, 1)

            def channel_transformed(g, a):
                act.wait_ge(fa_done, 2 * g + a + 1)
                if g >= 1:
                    act.wait_ge(fb_done, 2 * g)
                for trig, sign in ((0, 1.0), (1, -1.0)):
                    act.activation(ucs[:, a, trig * T:(trig + 1) * T], ps[:, 3, trig * T:(trig + 1) * T],
                                   ACT.Copy, scale=sign / T).then_inc(fa_copied, 1)

            def fourier_high(g):
                act.wait_ge(fb_done, 2 * g + 2)
                act.activation(u[:, 2 * g:2 * g + 2, 0:T], ps[:, 7, :].rearrange("p (c t) -> p c t", c=2),
                               ACT.Copy).then_inc(fb_hi, 1)

            def o_high(hd):
                act.wait_ge(pv_done, hd + 1)
                act.activation(u[:, 8 + hd, 0:T], ps[:, 6, (hd % 2) * T:(hd % 2 + 1) * T], ACT.Copy).then_inc(o_hi, 1)

            probabilities(0)
            for un in range(2 * HEADS):
                if un + 1 < 2 * HEADS:
                    probabilities(un + 1)
                probs_turned(un)
                if un % 4 == 0 and un:
                    fourier_high(un // 4 - 1)
                if un % 4 < 2:
                    channel_transformed(un // 4, un % 4)
                if un % 2 == 0 and un >= 4:
                    o_high(un // 2 - 2)
            fourier_high(FG - 1)
            o_high(HEADS - 2)
            o_high(HEADS - 1)

            def y_squares(pg, i):
                act.wait_ge(sum_done, pg + 1)
                act.activation(sq, y[:, bass.ds(i * 2, 2), :], ACT.Square).then_inc(ysq_ready, 1)
                act.wait_ge(ysq_ready, y_count(pg) + i + 1)
                for m in range(2):
                    c = bass.ds(i * 2 + m, 1)
                    last = act.activation(y[:, c, :], y[:, c, :], ACT.Copy, scale=der[:, 0, c])
                last.then_inc(yg_ready, 1)

            y_stage = [0]

            def y_count(pg):
                return 8 * y_stage[0]

            def boundary(j, shift, hooks):
                act.wait_ge(norm_sum, j + 1)
                root(stat[:, 0, :], 6)
                if shift is None:
                    return
                for b in range(4):
                    act.wait_ge(x_step, 4 * j + b + 1)
                    square(8 + 4 * j + b, xf[:, b * 1024:(b + 1) * 1024])
                act.wait_ge(sq_used, 12 + 4 * j)
                root(stat[:, 2, :], 7)
                act.wait_ge(gs_ready, j + 1)
                modulate(6 + 6 * j, late_xr, late_mt, der[:, 1, :].unsqueeze(2), vt[:, shift:shift + KC].unsqueeze(2),
                         hooks)

            def mlp(l):
                pg0 = PG_MLP[l]

                def h_high(q):
                    def f(pg, i):
                        act.wait_ge(relu2_ready, q * 8 + i + (32 * l + 1))
                        act.activation(h[:, bass.ds(i * 2, 2), 0:T], relu2, ACT.Copy).then_inc(h_hi, 1)
                    return f

                def quarter(q, after2, opened=False):
                    stage(pg0, 8, h_high(q), q, opened)
                    stage(pg0 + 8, 8, after2, q)
                quarter(0, lambda pg, i: None, opened=True)
                with act.Fori(0, 2) as q:
                    quarter(q + 1, lambda pg, i: None)
                y_stage[0] = 1 + 2 * l
                if l == 0:
                    quarter(3, y_squares)
                else:
                    stage(pg0, 8, h_high(3), 3)
                    stage_end(pg0 + 8, y_squares)

            def stage_end(pg0, after):
                w0 = slab_of(pg0) + 192
                pg0 += 48
                with act.Fori(0, 3) as b:
                    for j in range(2):
                        his(b * 8 + (w0 + 4 * j + 4))
                        right_half(b * 2 + (pg0 + j), 2 * j, b * 8 + (w0 + 4 * j + 4))
                        after(b * 2 + (pg0 + j), b * 2 + j)
                his(w0 + 28)
                right_half(pg0 + 6, 0, w0 + 28)
                after(pg0 + 6, 6)
                right_half(pg0 + 7, 2, w0 + 32)
                after(pg0 + 7, 7)

            act.wait_ge(gg_ready, 1)
            stage(PG_WO, 8, y_squares)
            boundary(0, 3 * KC, lambda s: hi(slab_of(PG_MLP[0]) + 4 + s, s))
            mlp(0)
            boundary(1, 6 * KC, lambda s: hi(slab_of(PG_CONV) + 4 + s, s))

            def triple(t, opened=False):
                for j in range(3):
                    pg, w = t * 3 + (PG_CONV + j), t * 12 + (slab_of(PG_CONV) + 4 * j)
                    if not (opened and j == 0):
                        his(w + 4)
                    right_half(pg, 2 * j, w + 4)
                act.wait_ge(conv_step, t * 5 + 5)
                act.activation(h[:, bass.ds(t * 2, 2), 0:T], cv, ACT.Copy).then_inc(v_hi, 1)
            triple(0, opened=True)
            with act.Fori(1, 8) as t:
                triple(t)
            act.wait_ge(gg_ready, 3)
            y_stage[0] = 2
            stage(PG_CO, 8, y_squares)
            boundary(2, 6 * KC + 3 * KC, lambda s: hi(slab_of(PG_MLP[1]) + 4 + s, s))
            mlp(1)
            boundary(3, None, None)
            for n in range(8):
                b, a = divmod(n, 2)
                act.wait_ge(out_t, n + 1)
                act.activation(ff[:, a * D + b * 512:a * D + (b + 1) * 512], ps[:, n % 4, :], ACT.Copy).then_inc(out_copied, 1)

        @block.vector
        def _(dve):
            def lo(w, s):
                dve.wait_ge(hi_ready, w + 1)
                dve.tensor_tensor(wlo[:, s, :], raw[:, s, :], whi[:, s, :], ALU.subtract).then_inc(lo_ready, 1)

            def los(w0):
                for s in range(SLOTS):
                    lo(w0 + s, s)

            def unit_slab(m, un, k):
                slot = m_slot(m)
                dve.wait_ge(m_landed[slot], m * 8 + (16 - 8 * slot) if not isinstance(m, int) else 16 * (m // 2 + 1))
                dve.wait_ge(acc_zeroed, un + 1)
                if not (isinstance(m, int) and m == 0):
                    dve.wait_ge(m_used, m)
                a = acc[:, unit_parity[0], :]
                dve.scalar_tensor_tensor(out=a, in0=mraw[:, slot, :], scalar=cs[:, bass.ds(k, 1)], in1=a,
                                         op0=ALU.mult, op1=ALU.add).then_inc(m_used, 1)

            m_parity, unit_parity = [0], [0]

            def m_slot(m):
                return m % 2 if isinstance(m, int) else m_parity[0]

            def unit_slabs(m0, un, k0, js, parity):
                for j in js:
                    m_parity[0], unit_parity[0] = j % 2, parity
                    unit_slab(m0 + j, un, k0 + j)

            def finish_unit(un, col):
                dve.wait_ge(unit_masked, un + 1)
                if not (isinstance(un, int) and un == 0):
                    dve.wait_ge(mod_ready, un)
                dve.tensor_reduce(t8[:, :], red[:, :].rearrange("p (c f) -> p c f", f=P), AX_X,
                                  ALU.add).then_inc(unit_read, 1)
                dve.wait_ge(unit_read, un + 1)
                dve.tensor_tensor(vt[:, bass.ds(col, KC // 2)], t8[:, :], bT[:, bass.ds(col, KC // 2)],
                                  ALU.add).then_inc(mod_ready, 1)

            dve.memset(u[:, :, 0:128].bitcast(F32), 0.0).then_inc(crs_zero, 1)
            dve.wait_ge(small_t, 1)
            dve.tensor_copy(small[:, :], ps[:, 3, 0:400]).then_inc(small_copied, 1)
            dve.wait_ge(sink_b, 1)
            dve.tensor_copy(nsink[:, 0, :], ps[:, 2, 0:HEADS])
            dve.tensor_scalar(nsink[:, 1, :], ps[:, 2, 0:HEADS], -1.0, None, ALU.mult).then_inc(sink_copied, 1)
            dve.wait_ge(silu_exp, 1)
            dve.tensor_scalar(sg[:, :], sg[:, :], 1.0, None, ALU.add).then_inc(silu_step, 1)
            dve.wait_ge(silu_step, 1)
            dve.reciprocal(sg[:, :], sg[:, :]).then_inc(silu_step, 1)
            dve.wait_ge(silu_step, 2)
            dve.wait_ge(small_copied, 1)
            dve.tensor_tensor(cs[:, :], cT, sg[:, :], ALU.mult).then_inc(silu_step, 1)
            for i in range(8):
                dve.wait_ge(x_t, i + 1)
                dve.tensor_copy(x[:, 2 * i:2 * i + 2, :],
                                ps[:, 4 + i % 2, :].rearrange("p (c t) -> p c t", c=2)).then_inc(x_copied, 1)
            dve.wait_ge(crs_hi, 1)
            dve.tensor_tensor(u[:, :, 2:4], cs[:, :].rearrange("p (w k) -> p k w", w=2), u[:, :, 0:2],
                              ALU.subtract).then_inc(crs_lo, 1)

            def reciprocal_root(n, i):
                dve.wait_ge(sd_ready, n)
                dve.reciprocal(stat[:, i + 1, :], stat[:, i, :]).then_inc(rstd_ready, 1)
                dve.wait_ge(rstd_ready, n)

            for g in range(9):
                los(4 * g)
            reciprocal_root(1, 0)
            for g in range(9, 13):
                los(4 * g)
            reciprocal_root(2, 2)
            for g in range(13, 16):
                los(4 * g)
            los(W_Q)

            def both(a):
                return a.unsqueeze(2).broadcast_to([P, KC, 2])

            def pairs(a):
                return a.rearrange("p (c w) -> p c w", w=2)
            dve.wait_ge(row_t, 4)
            for what, col in ((0, KC), (1, 0)):
                turned = ps[:, 7, 64 * what:64 * what + 64].rearrange("p (c r) -> p c r", r=4)
                dve.tensor_tensor(pairs(modc[:, what, :]), turned[:, :, 0:2], both(bT[:, col:col + KC]),
                                  ALU.add).then_inc(modc_step, 1)
                dve.wait_ge(modc_step, 2 * what + 1)
                dve.tensor_tensor(pairs(modc[:, what, :]), turned[:, :, 2:4], pairs(modc[:, what, :]),
                                  ALU.add).then_inc(modc_step, 1)
            dve.wait_ge(modc_step, 4)
            dve.scalar_tensor_tensor(out=pairs(modc[:, 0, :]), in0=pairs(modc[:, 0, :]), scalar=1.0,
                                     in1=both(gT[:, 0:KC]), op0=ALU.add, op1=ALU.mult).then_inc(modc_step, 1)
            dve.wait_ge(modc_step, 5)

            def modulate(n0, rstd, xr, mt, gs, shift, hooks):
                def scaled(b):
                    c0, n = BATCHES[b]
                    dve.tensor_tensor(xr[b % 2][:, 0:n, :], x[:, c0:c0 + n, :],
                                      rstd.unsqueeze(1).broadcast_to([P, n, T]), ALU.mult).then_inc(u_scaled, 1)
                scaled(0)
                for b, (c0, n) in enumerate(BATCHES):
                    if b + 1 < len(BATCHES):
                        if b >= 1:
                            dve.wait_ge(u_ready, n0 + b)
                        scaled(b + 1)
                    if n == 4:
                        dve.wait_ge(u_scaled, n0 + b + 1)
                        dve.tensor_scalar(mt[b % 2][:, 3, :], xr[b % 2][:, 3, :], gs[:, c0 + 3], shift[:, c0 + 3],
                                          ALU.mult, ALU.add).then_inc(u_shifted_dve, 1)
                    dve.wait_ge(u_hi, n0 + b + 1)
                    dve.tensor_tensor(u[:, c0:c0 + n, T:2 * T], mt[b % 2][:, 0:n, :], u[:, c0:c0 + n, 0:T],
                                      ALU.subtract).then_inc(u_ready, 1)
                    for s in HOOKS[b]:
                        hooks(s)

            dve.wait_ge(x_copied, 8)
            modulate(0, stat[:, 1, :], start_xr, start_mt, modc_col(0, 0), modc_col(1, 0),
                     lambda s: lo(W_Q + 4 + s, s))

            def context_low(b):
                c = fq[:, 4 * b:4 * b + 4, :]
                dve.tensor_tensor(c, c, stat[:, 3, :].unsqueeze(1).broadcast_to([P, 4, T]), ALU.mult).then_inc(c_scaled, 1)
                dve.wait_ge(c_hi, b + 1)
                dve.tensor_tensor(h[:, 4 * b:4 * b + 4, T:2 * T], c, h[:, 4 * b:4 * b + 4, 0:T],
                                  ALU.subtract).then_inc(c_ready, 1)

            def add_halves(pg, bank, dst):
                dve.wait_ge(b_copied, pg + 1)
                dve.tensor_tensor(dst, ps[:, bank:bank + 2, 0:T], tmp[:, :, :], ALU.add).then_inc(sum_done, 1)

            def rope(pg, r, dst):
                dve.wait_ge(sum_done, pg + 1)
                for a, b in ((0, 32), (32, 0), (64, 96), (96, 64)):
                    last = dve.tensor_copy(qsw[a:a + 32], qs[b:b + 32])
                last.then_inc(rope_step, 1)
                dve.wait_ge(rope_step, r * 4 + 1)
                dve.tensor_tensor(qs, qs, cosT.unsqueeze(1).broadcast_to([P, 2, T]), ALU.mult).then_inc(rope_step, 1)
                dve.tensor_tensor(qsw, qsw, sinT.unsqueeze(1).broadcast_to([P, 2, T]), ALU.mult).then_inc(rope_step, 1)
                dve.wait_ge(rope_step, r * 4 + 3)
                dve.tensor_tensor(dst, qs, qsw, ALU.add).then_inc(rope_step, 1)
                dve.wait_ge(rope_step, r * 4 + 4)

            def att_group(i):
                m0 = sum(UNIT_SHARE[:i])
                n_m = UNIT_SHARE[i]
                for s in range(SLOTS):
                    if i:
                        lo(W_Q + 4 * i + 4 + s, s)
                    for j in range(s * n_m // SLOTS, (s + 1) * n_m // SLOTS):
                        m = m0 + j
                        unit_slabs(m, m // UNIT, m % UNIT, (0,), m // UNIT)

            for i in range(4):
                att_group(i)
                context_low(i)
                add_halves(PG_Q + i, 2 * (i % 2), qs)
                rope(PG_Q + i, i, qh[:, 2 * i:2 * i + 2, :])
            att_group(4)
            add_halves(PG_K, 0, qs)
            rope(PG_K, 4, kT[:, :, 0:T])
            add_halves(PG_K + 1, 4, kT[:, :, T:2 * T])
            att_group(5)
            add_halves(PG_V, 2, vsum[:, :, 0:T])
            add_halves(PG_V + 1, 6, vsum[:, :, T:2 * T])
            for i in range(4):
                att_group(6 + i)
                add_halves(PG_F + i, 2 * (i % 2), fq[:, 2 * i:2 * i + 2, :])

            def stage(pg0, n, un, n_m, take, q=None, u_par=0, opened=False):
                w0 = slab_of(pg0)

                def pair(b, ready):
                    for j in range(2):
                        pg, w = b * 2 + (pg0 + j), b * 8 + (w0 + 4 * j + 4)
                        if q is not None:
                            pg, w = q * 16 + pg, q * 64 + w
                        for s in range(SLOTS):
                            if not (ready and j == 0):
                                lo(w + s, s)
                            js = range(s * n_m // SLOTS, (s + 1) * n_m // SLOTS)
                            if js:
                                unit_slabs(un * UNIT + (b * (2 * n_m) + j * n_m), un, b * (2 * n_m) + j * n_m, js, u_par)
                        take(pg, 2 * j, b * 2 + j)
                if opened:
                    pair(0, True)
                with dve.Fori(1 if opened else 0, n // 2) as b:
                    pair(b, False)

            finish_unit(0, unit_col(0))

            for kv in range(KV_HEADS):
                dve.wait_ge(v_t, kv + 1)
                dve.tensor_copy(v[:, :, kv * HD:(kv + 1) * HD],
                                ps[:, 4 + kv, :].rearrange("p (k d) -> p k d", k=4)).then_inc(v_ready, 1)

            def row_max(un):
                hd, qt = divmod(un, 2)
                dve.wait_ge(s_done, un + 1)
                far = ps[:, un % 3, (1 - qt) * P:(2 - qt) * P]
                dve.tensor_tensor(far, far, masks[qt], ALU.add).then_inc(masked, 1)
                dve.wait_ge(masked, un + 1)
                dve.tensor_reduce(sm[:, 0, un:un + 1], ps[:, un % 3, :], AX_X, ALU.max).then_inc(max_ready, 1)
                dve.wait_ge(max_ready, un + 1)
                dve.tensor_scalar(sm[:, 1, un:un + 1], sm[:, 0, un:un + 1], -SCALE, nsink[:, 1, hd:hd + 1],
                                  ALU.mult, ALU.min).then_inc(negm_ready, 1)

            def normalize(un):
                dve.wait_ge(p_ready, un + 1)
                col = slice(un, un + 1)
                dve.tensor_tensor(sm[:, 4, col], sm[:, 3, col], sm[:, 2, col], ALU.add).then_inc(den_ready, 1)
                dve.wait_ge(den_ready, un + 1)
                dve.reciprocal(sm[:, 4, col], sm[:, 4, col]).then_inc(rden_ready, 1)
                dve.wait_ge(rden_ready, un + 1)
                dve.tensor_scalar(prob[un % 2], prob[un % 2], sm[:, 4, col], None, ALU.mult).then_inc(pn_ready, 1)

            def o_low(hd):
                dve.wait_ge(o_hi, hd + 1)
                dve.tensor_tensor(u[:, 8 + hd, T:2 * T], ps[:, 6, (hd % 2) * T:(hd % 2 + 1) * T], u[:, 8 + hd, 0:T],
                                  ALU.subtract).then_inc(o_ready, 1)

            def fourier_low(g):
                dve.wait_ge(fb_hi, g + 1)
                dve.tensor_tensor(u[:, 2 * g:2 * g + 2, T:2 * T], ps[:, 7, :].rearrange("p (c t) -> p c t", c=2),
                                  u[:, 2 * g:2 * g + 2, 0:T], ALU.subtract).then_inc(f_ready, 1)

            row_max(0)
            row_max(1)
            for un in range(2 * HEADS):
                normalize(un)
                if un + 2 < 2 * HEADS:
                    row_max(un + 2)
                mid = U_MID + un // HEADS
                unit_slabs(UNIT * U_MID + 2 * un, mid, (2 * un) % UNIT, range(2), mid % 2)
                if un % 4 == 0 and un:
                    fourier_low(un // 4 - 1)
                if un % 2 == 0 and un >= 4:
                    o_low(un // 2 - 2)
                if un == 6:
                    finish_unit(1, unit_col(1))
                if un == 14:
                    finish_unit(2, unit_col(2))
            fourier_low(FG - 1)
            o_low(HEADS - 2)
            o_low(HEADS - 1)

            def open_y(j, gate, gain):
                dve.memset(ssq, 0.0).then_inc(ssq_zeroed, 1)
                dve.tensor_tensor(der[:, 0, :], vt[:, gate:gate + KC], gT[:, gain:gain + KC], ALU.mult).then_inc(gg_ready, 1)
                dve.wait_ge(ssq_zeroed, j + 1)

            def add_squares(n, j):
                dve.wait_ge(ysq_ready, n + 1)
                dve.tensor_tensor(ssq, ssq, sq, ALU.add).then_inc(ssq_done, 1)
                dve.wait_ge(ssq_done, n + 1)

            def take_y(j):
                def f(pg, bank, i):
                    add_halves(pg, bank, y[:, bass.ds(i * 2, 2), :])
                    add_squares(i + 8 * j, j)
                return f

            open_y(0, 2 * KC, KC)
            stage(PG_WO, 4, U_WO, 4, take_y(0), u_par=0)
            finish_unit(3, unit_col(3))

            def take_y_second(j):
                def f(pg, bank, i):
                    add_halves(pg, bank, y[:, bass.ds(i * 2 + 8, 2), :])
                    add_squares(i + (8 * j + 4), j)
                return f
            stage(PG_WO + 4, 4, U_WO + 1, 4, take_y_second(0), u_par=1)
            finish_unit(4, unit_col(4))

            def boundary(j, scale, gain, last_unit, hooks, shift=None):
                reciprocal_root(3 + 2 * j, 0)

                def chunks(t, b):
                    return t[:, 4 * b:4 * b + 4, :]

                def scale_y(b):
                    dve.wait_ge(yg_ready, 8 * j + min(2 * b + 2, 8))
                    dve.tensor_tensor(chunks(y, b), chunks(y, b), stat[:, 1, :].unsqueeze(1).broadcast_to([P, 4, T]),
                                      ALU.mult).then_inc(y_scaled, 1)
                scale_y(0)
                for b in range(4):
                    if b < 3:
                        scale_y(b + 1)
                    dve.wait_ge(y_scaled, 4 * j + b + 1)
                    dve.tensor_tensor(chunks(x, b), chunks(x, b), chunks(y, b), ALU.add).then_inc(x_step, 1)
                if scale is None:
                    return
                if last_unit is not None:
                    finish_unit(last_unit, unit_col(last_unit))
                dve.wait_ge(mod_ready, MOD_NEEDED[j])
                dve.scalar_tensor_tensor(out=der[:, 1, :], in0=vt[:, scale:scale + KC], scalar=1.0,
                                         in1=gT[:, gain:gain + KC], op0=ALU.add, op1=ALU.mult).then_inc(gs_ready, 1)
                dve.wait_ge(gs_ready, j + 1)
                reciprocal_root(4 + 2 * j, 2)
                dve.wait_ge(x_step, 4 * j + 4)
                modulate(6 + 6 * j, stat[:, 3, :], late_xr, late_mt, der[:, 1, :].unsqueeze(2),
                         vt[:, shift:shift + KC].unsqueeze(2), hooks)

            def mlp(l, u0, loop_units):
                pg0 = PG_MLP[l]

                def take_h(q):
                    def f(pg, bank, i):
                        n = q * 8 + i + 32 * l
                        add_halves(pg, bank, tsum)
                        dve.wait_ge(sum_done, pg + 1)
                        dve.scalar_tensor_tensor(out=relu2, in0=tsum, scalar=0.0, in1=tsum, op0=ALU.max,
                                                 op1=ALU.mult).then_inc(relu2_ready, 1)
                        dve.wait_ge(h_hi, n + 1)
                        dve.wait_ge(relu2_ready, n + 1)
                        dve.tensor_tensor(h[:, bass.ds(i * 2, 2), T:2 * T], relu2, h[:, bass.ds(i * 2, 2), 0:T],
                                          ALU.subtract).then_inc(h_ready, 1)
                        dve.wait_ge(h_ready, n + 1)
                    return f

                def add_to_y(q):
                    def f(pg, bank, i):
                        n = q * 8 + i + (24 * l - 8)
                        yi = y[:, bass.ds(i * 2, 2), :]
                        dve.wait_ge(b_copied, pg + 1)
                        dve.tensor_tensor(yi, ps[:, bank:bank + 2, 0:T], yi, ALU.add).then_inc(y_part, 1)
                        dve.wait_ge(y_part, n + 1)
                        dve.tensor_tensor(yi, tmp[:, :, :], yi, ALU.add).then_inc(sum_done, 1)
                    return f

                def quarter(q, un, n_m, col, take2, first=False):
                    stage(pg0, 8, un, n_m, take_h(q), q, 0, first)
                    if n_m and not first:
                        finish_unit(un - 1, col - 8)
                    stage(pg0 + 8, 8, un + 1, n_m, take2, q, 1)
                    if n_m:
                        finish_unit(un, col)
                quarter(0, u0, 2, unit_col(u0), lambda pg, bank, i: add_halves(pg, bank, y[:, bass.ds(i * 2, 2), :]),
                        first=True)
                with dve.Fori(0, 2) as q:
                    quarter(q + 1, q * 2 + (u0 + 2), loop_units, q * KC + unit_col(8), add_to_y(q + 1))

                def take_last(pg, bank, i):
                    add_to_y(3)(pg, bank, i)
                    add_squares(i + (8 + 16 * l), 1 + 2 * l)
                stage(pg0, 8, u0 + 6, loop_units, take_h(3), 3, 0)
                if loop_units:
                    finish_unit(u0 + 5, unit_col(u0 + 5))
                else:
                    finish_unit(u0 + 1, unit_col(u0 + 1))
                dve.wait_ge(mod_ready, (8, 20)[l])
                open_y(1 + 2 * l, l * 6 * KC + 5 * KC, l * 4 * KC + 3 * KC)
                if l == 0:
                    stage(pg0 + 8, 8, u0 + 7, loop_units, take_last, 3, 1)
                    finish_unit(u0 + 6, unit_col(u0 + 6))
                    return
                pg1, w1 = pg0 + 56, slab_of(pg0 + 56)
                with dve.Fori(0, 3) as b:
                    for j in range(2):
                        los(b * 8 + (w1 + 4 * j + 4))
                        take_last(b * 2 + (pg1 + j), 2 * j, b * 2 + j)
                los(w1 + 28)
                take_last(pg1 + 6, 0, 6)
                take_last(pg1 + 7, 2, 7)

            boundary(0, 4 * KC, 2 * KC, 5, lambda s: lo(slab_of(PG_MLP[0]) + 4 + s, s), 3 * KC)
            mlp(0, U_MLP0, 2)
            L1, G1 = 6 * KC, 4 * KC
            boundary(1, L1 + KC, G1, None, lambda s: lo(slab_of(PG_CONV) + 4 + s, s), L1)

            dve.memset(zpad[:, :, 0:1], 0.0)
            dve.memset(zpad[:, :, T + 1:T + 2], 0.0).then_inc(z_edges, 1)
            dve.wait_ge(z_edges, 1)

            def triple(t, t0, un, n_m, opened=False):
                for j, dst in enumerate((cgc, cxv, cgb)):
                    pg = t * 3 + (PG_CONV + 3 * t0 + j)
                    w = t * 12 + (slab_of(PG_CONV) + 12 * t0 + 4 * j + 4)
                    for s in range(SLOTS):
                        if not (opened and j == 0):
                            lo(w + s, s)
                        unit_slabs(un * UNIT + t * n_m, un, t * n_m, conv_unit_slabs(4 * j + s, n_m), un % 2)
                    add_halves(pg, 2 * j, dst)
                    step = t * 5 + 5 * t0
                    if j == 1:
                        dve.wait_ge(sum_done, pg + 1)
                        dve.tensor_tensor(zpad[:, :, 1:T + 1], cgc, cxv, ALU.mult).then_inc(conv_step, 1)
                        dve.wait_ge(conv_step, step + 1)
                        for tap, wait in ((1, 2), (0, 3), (2, 4)):
                            for m in range(2):
                                z = zpad[:, m, tap:tap + T]
                                w_tap = cwT[:, bass.ds(t * 2 + (tap * KC + 2 * t0 + m), 1)]
                                if tap == 1:
                                    last = dve.tensor_scalar(cy[:, m, :], z, w_tap, None, ALU.mult)
                                else:
                                    last = dve.scalar_tensor_tensor(out=cy[:, m, :], in0=z, scalar=w_tap,
                                                                    in1=cy[:, m, :], op0=ALU.mult, op1=ALU.add)
                            last.then_inc(conv_step, 1)
                            dve.wait_ge(conv_step, step + wait)
                hc = bass.ds(t * 2 + 2 * t0, 2)
                dve.wait_ge(sum_done, pg + 1)
                dve.tensor_tensor(cv, cgb, cy, ALU.mult).then_inc(conv_step, 1)
                dve.wait_ge(conv_step, step + 5)
                dve.wait_ge(v_hi, t + (t0 + 1))
                dve.tensor_tensor(h[:, hc, T:2 * T], cv, h[:, hc, 0:T], ALU.subtract).then_inc(conv_ready, 1)
                dve.wait_ge(conv_ready, t + (t0 + 1))

            for t0, n_t, un, n_m in CONV_PARTS:
                if t0 == 0:
                    triple(0, 0, un, n_m, opened=True)
                with dve.Fori(1 if t0 == 0 else 0, n_t) as t:
                    triple(t, t0, un, n_m)
                finish_unit(un - 1, unit_col(un - 1))
            open_y(2, L1 + 2 * KC, G1 + KC)
            stage(PG_CO, 8, U_CO, 2, take_y(2), u_par=1)
            finish_unit(16, unit_col(16))
            boundary(2, L1 + 4 * KC, G1 + 2 * KC, 17, lambda s: lo(slab_of(PG_MLP[1]) + 4 + s, s), L1 + 3 * KC)
            mlp(1, U_MLP1, 0)
            boundary(3, None, None, None, None)

        @block.gpsimd
        def _(pool):
            pool.wait_ge(small_t, 1)
            pool.wait_ge(row_t, 4)
            for i in range(2):
                pool.memset(acc[:, i, :], 0.0).then_inc(acc_zeroed, 1)
            for un in range(len(UNITS)):
                pool.wait_ge(m_used, UNIT * (un + 1))
                if un:
                    pool.wait_ge(unit_read, un)
                pool.partition_all_reduce(red[:, :], acc[:, un % 2, :], P, RADD).then_inc(unit_summed, 1)
                pool.wait_ge(unit_summed, un + 1)
                r = red[:, :].rearrange("p (c f) -> p c f", f=P)
                pool.tensor_tensor(r, r, ident.unsqueeze(1).broadcast_to([P, KC // 2, P]), ALU.mult).then_inc(unit_masked, 1)
                if un + 2 < len(UNITS):
                    pool.memset(acc[:, un % 2, :], 0.0).then_inc(acc_zeroed, 1)


UNIT_SHARE = (2, 2, 2, 2, 8, 8, 2, 2, 2, 2)
CONV_PARTS = ((0, 2, 14, 8), (2, 2, 15, 8), (4, 4, 16, 4))


def conv_unit_slabs(i, n_m):
    return range(i * n_m // 12, (i + 1) * n_m // 12)


MOD_NEEDED = (6, 13, 18, 20)


def shape_tables():
    import numpy as np

    f = np.float32
    t = np.zeros((P, TAB_W), f)
    t[:, 0:128] = np.eye(P)
    t[:, 128:256] = 1
    tok = np.arange(T)
    inv_freq = f(10000.0) ** (-np.arange(0, 64, 2, dtype=f) / f(64))
    for p in range(P):
        axis, second, i = p // 64, (p % 64) // 32, p % 32
        pos = (tok // 64, tok % 64)[axis].astype(f)
        ang = pos * inv_freq[i]
        t[p, 256:512] = np.cos(ang)
        t[p, 512:768] = np.sin(ang) if second else -np.sin(ang)
    q, k = np.arange(P)[:, None], np.arange(P)[None, :]
    t[:, 768:896] = np.where(k <= q, 0, -1e30)
    t[:, 896:1024] = np.where(q <= k, 0, -1e30)
    i = np.arange(T)
    ang = 2 * np.pi * ((i[:, None] * i[None, :]) % T) / T
    dft = np.concatenate([np.cos(ang), np.sin(ang)], axis=1).astype(f)
    t[:, 1024:2048] = dft.reshape(2, P, 2 * T).transpose(1, 0, 2).reshape(P, 4 * T)
    t[:, EPS_COL] = 1e-6
    return t


_INS = ["x", "c", "ctx", "c_ctx", "w_mod", "b_mod", "norm_gains", "att_w_in", "att_sink", "att_w_out", "conv_w_in",
        "conv_w", "conv_w_out", "mlp_w1", "mlp_w2"]


def kernel(**inputs):
    import numpy as _np
    import concourse.bacc as _bacc
    from concourse import mybir as _mybir
    from concourse.bass_utils import run_bass_kernel_spmd as _run

    nc = _bacc.Bacc("TRN2", target_bir_lowering=False, num_devices=1)
    arrays = {f"in_{n}_dram": _np.ascontiguousarray(inputs[n]) for n in _INS}
    arrays["tables_dram"] = shape_tables()
    args = [nc.dram_tensor(n, a.shape, _mybir.dt.from_np(a.dtype), kind="ExternalInput").ap()
            for n, a in arrays.items()]
    args.append(nc.dram_tensor("out_0_dram", (1, T, D), F32, kind="ExternalOutput").ap())
    backbone_program(nc, *args)
    r = _run(nc, [arrays], core_ids=[0])
    return r.results[0]["out_0_dram"]
```

```python
from contextlib import ExitStack

import concourse.bass as bass
from concourse import mybir

F32 = mybir.dt.float32
F32R = mybir.dt.float32r
ALU = mybir.AluOpType
ACT = mybir.ActivationFunctionType
AX_X = mybir.AxisListType.X
RADD = bass.bass_isa.ReduceOp.add

P = 128
D = 2048
T = 256
KC = D // P
GW = 256
SLOTS = 4
CPS = KC // SLOTS
HEADS, KV_HEADS, HD = 8, 2, 128
GQA = HEADS // KV_HEADS
FG = 4
D_FF = 4 * D
SCALE = float(HD) ** -0.5
EPS_COL, TAB_W = 2048, 2050
HALF = D // 2
UNIT = KC

W_START = 0
PG_F, PG_Q, PG_K, PG_V = 0, 4, 8, 10
PG_WO = 12
PG_MLP = (20, 116)
PG_CONV = 84
PG_CO = 108
W_F, W_K, W_V = 64, 96, 100


def slab_of(pg):
    return 4 * pg + 56


UNITS = [(0, 2, 0), (0, 2, 1), (0, 4, 0), (0, 4, 1), (0, 3, 0), (0, 3, 1), (0, 5, 0), (0, 5, 1),
         (1, 0, 0), (1, 0, 1), (1, 1, 0), (1, 1, 1), (1, 2, 0), (1, 2, 1), (1, 4, 0), (1, 4, 1),
         (1, 3, 0), (1, 3, 1), (1, 5, 0), (1, 5, 1)]
U_WO, U_MLP0, U_CO, U_MLP1 = 5, 6, 17, 18
BATCHES = ((0, 1), (1, 1), (2, 2), (4, 4), (8, 4), (12, 4))
HOOKS = ((), (), (), (0,), (1,), (2, 3))
START_HOOKS = ((), (), (), (), (0, 1), (2, 3))


def unit_col(u):
    l, v, h = UNITS[u]
    return l * 6 * KC + v * KC + h * (KC // 2)


def backbone_program(nc, x_in, c_in, ctx_in, c_ctx, w_mod, b_mod, gains, att_w_in, sink, att_w_out,
                     conv_w_in, conv_w, conv_w_out, mlp_w1, mlp_w2, tables, out):
    with ExitStack() as ctx:
        def sb(name, shape, dt=F32):
            return ctx.enter_context(nc.sbuf_tensor(name, shape, dt))

        def sem(name):
            return ctx.enter_context(nc.semaphore(name))

        x = sb("x", [P, KC, T])
        u = sb("u", [P, KC, 2 * T], F32R)
        h = sb("h", [P, KC, 2 * T], F32R)
        y = sb("y", [P, KC, T])
        fq = sb("fq", [P, KC, T])
        raw = sb("raw", [P, SLOTS, 1024])
        whi = sb("whi", [P, SLOTS, 1024], F32R)
        wlo = sb("wlo", [P, SLOTS, 1024], F32R)
        mraw = sb("mraw", [P, 2, HALF])
        acc = sb("acc", [P, 2, HALF])
        red = sb("red", [P, HALF])
        kT = sb("kT", [P, KV_HEADS, 2 * T])
        v = sb("v", [P, 4, KV_HEADS * HD])
        tab = sb("tab", [P, TAB_W])
        tmp = sb("tmp", [P, 2, T])
        stat = sb("stat", [P, 4, T])
        small = sb("small", [P, 400])
        vt = sb("vt", [P, 12 * KC])
        modc = sb("modc", [P, 2, 2 * KC])
        cs = sb("cs", [P, 2 * KC])
        sg = sb("sg", [P, 2 * KC])
        der = sb("der", [P, 2, KC])
        t8 = sb("t8", [P, KC // 2])
        nsink = sb("nsink", [P, 2, HEADS])
        sinkr = sb("sinkr", [1, HEADS])
        sm = sb("sm", [P, 5, 2 * HEADS])
        ps = ctx.enter_context(nc.psum_tensor("ps", [P, 8, 512], F32))

        ident, ones = tab[:, 0:128], tab[:, 128:256]
        cosT, sinT = tab[:, 256:512], tab[:, 512:768]
        masks = (tab[:, 768:896], tab[:, 896:1024])
        dft = tab[:, 1024:2048].rearrange("p (k n) -> p k n", k=2)
        eps = tab[:, EPS_COL:EPS_COL + 1]
        cT, gT = small[:, 0:32], small[:, 32:160]
        bT, cwT = small[:, 160:352], small[:, 352:400]
        xf = x[:, :, :].rearrange("p c t -> p (c t)")
        yf = y[:, :, :].rearrange("p c t -> p (c t)")
        ff = fq[:, :, :].rearrange("p c t -> p (c t)")
        qs, qsw = y[:, 0:2, :], y[:, 2:4, :]
        fin = y[:, 8:16, :]
        qh = fq[:, 0:8, :]
        vsum = yf[:, 1024:2048].rearrange("p (g t) -> p g t", g=2)
        prob = [yf[:, 512 * i:512 * i + 512] for i in range(2)]
        probT = [ff[:, 2048 + 1024 * i:3072 + 1024 * i].rearrange("p (k q) -> p k q", k=4) for i in range(2)]
        ucs = yf[:, 1024:2048].rearrange("p (k n) -> p k n", k=2)
        row = (red[0:4, :], acc[0:4, 1, :])
        sqx = [ff[:, 1024 * i:1024 * i + 1024] for i in range(2)]
        ssq, sq = fq[:, 8:10, :], fq[:, 10:12, :]
        tsum, relu2 = fq[:, 8:10, :], fq[:, 10:12, :]
        cgc, cxv, cgb = fq[:, 8:10, :], fq[:, 10:12, :], fq[:, 12:14, :]
        zpad = ff[:, 0:2 * (T + 2)].rearrange("p (m t) -> p m t", m=2)
        cy = ff[:, 1024:1536].rearrange("p (m t) -> p m t", m=2)
        cv = ff[:, 1536:2048].rearrange("p (m t) -> p m t", m=2)

        tab_landed, small_landed, x_landed, ctx_landed = (sem(n) for n in (
            "tab_landed", "small_landed", "x_landed", "ctx_landed"))
        w_landed = [sem(f"w_landed{i}") for i in range(SLOTS)]
        m_landed = [sem(f"m_landed{i}") for i in range(2)]
        mid_landed = [sem(f"mid_landed{i}") for i in range(SLOTS)]
        hi_ready, lo_ready, slab_used, m_used = (sem(n) for n in ("hi_ready", "lo_ready", "slab_used", "m_used"))
        b_copied, sum_done, y_part = (sem(n) for n in ("b_copied", "sum_done", "y_part"))
        small_t, small_copied, silu_exp, silu_step, crs_hi, crs_lo, crs_zero = (sem(n) for n in (
            "small_t", "small_copied", "silu_exp", "silu_step", "crs_hi", "crs_lo", "crs_zero"))
        sink_b, sink_copied = sem("sink_b"), sem("sink_copied")
        x_t, x_copied, ctx_t, ctx_copied = (sem(n) for n in ("x_t", "x_copied", "ctx_t", "ctx_copied"))
        row_copied, row_t, modc_part, modc_step = (sem(n) for n in ("row_copied", "row_t", "modc_part", "modc_step"))
        acc_zeroed, unit_summed, unit_masked, unit_read, mod_ready = (sem(n) for n in (
            "acc_zeroed", "unit_summed", "unit_masked", "unit_read", "mod_ready"))
        norm_sum, sd_ready, rstd_ready, sq_ready, sq_used, x_step, y_scaled = (sem(n) for n in (
            "norm_sum", "sd_ready", "rstd_ready", "sq_ready", "sq_used", "x_step", "y_scaled"))
        ysq_ready, ssq_done, ssq_zeroed, gg_ready, gs_ready, yg_ready = (sem(n) for n in (
            "ysq_ready", "ssq_done", "ssq_zeroed", "gg_ready", "gs_ready", "yg_ready"))
        u_scaled, u_shifted, u_shifted_dve, u_hi, u_ready = (sem(n) for n in (
            "u_scaled", "u_shifted", "u_shifted_dve", "u_hi", "u_ready"))
        c_scaled, c_shifted, c_hi, c_ready = (sem(n) for n in ("c_scaled", "c_shifted", "c_hi", "c_ready"))
        rope_swapped, rope_step, v_t, v_ready = sem("rope_swapped"), sem("rope_step"), sem("v_t"), sem("v_ready")
        s_done, masked, max_ready, negm_ready, p_ready, den_ready, rden_ready, pn_ready = (sem(n) for n in (
            "s_done", "masked", "max_ready", "negm_ready", "p_ready", "den_ready", "rden_ready", "pn_ready"))
        pt_done, pt_copied, pv_done, o_hi, o_ready = (sem(n) for n in (
            "pt_done", "pt_copied", "pv_done", "o_hi", "o_ready"))
        fa_done, fa_copied, fb_done, fb_hi, f_ready = (sem(n) for n in (
            "fa_done", "fa_copied", "fb_done", "fb_hi", "f_ready"))
        relu2_ready, h_hi, h_ready = sem("relu2_ready"), sem("h_hi"), sem("h_ready")
        z_edges, conv_step, v_hi, conv_ready = sem("z_edges"), sem("conv_step"), sem("v_hi"), sem("conv_ready")
        out_t, out_copied, out_stored = sem("out_t"), sem("out_copied"), sem("out_stored")

        def modc_col(what, which):
            return modc[:, what, :].rearrange("p (c w) -> p c w", w=2)[:, :, which:which + 1]

        def four_chunks(a):
            return a.rearrange("p (c t) -> p c t", c=4)

        start_xr = [four_chunks(yf[:, 1024 * i:1024 * i + 1024]) for i in range(2)]
        start_mt = [four_chunks(yf[:, 2048 + 1024 * i:3072 + 1024 * i]) for i in range(2)]
        late_xr = [four_chunks(ff[:, 1024 * i:1024 * i + 1024]) for i in range(2)]
        late_mt = [four_chunks(ff[:, 2048 + 1024 * i:3072 + 1024 * i]) for i in range(2)]

        block = ctx.enter_context(nc.Block())

        @block.sync
        def _(sp):
            def rows(t):
                return t.rearrange("(c p) -> c p", p=P)

            stage = acc[:, 0, :]
            sp.dma_start(tab[:, 0:256], tables[:, 0:256]).then_inc(tab_landed, 16)
            sp.dma_start(stage[0:16, 0:128], rows(c_in.rearrange("a d -> (a d)"))).then_inc(small_landed, 16)
            sp.dma_start(stage[16:32, 0:128], rows(c_ctx)).then_inc(small_landed, 16)
            sp.dma_start(stage[:, 128:256], gains.rearrange("l g (c p) -> (l g c) p", p=P)).then_inc(small_landed, 16)
            for l in range(2):
                sp.dma_start(stage[0:96, 256 + 128 * l:384 + 128 * l],
                             b_mod[l].rearrange("(c p) -> c p", p=P)).then_inc(small_landed, 16)
            sp.dma_start(stage[0:48, 512:640], conv_w.rearrange("a k (c p) -> (a k c) p", p=P)).then_inc(small_landed, 16)
            sp.dma_start(sinkr[:, :], sink).then_inc(small_landed, 16)
            def load_slab(w, s, src):
                if not (isinstance(w, int) and w < SLOTS):
                    sp.wait_ge(lo_ready, w - (SLOTS - 1))
                sp.dma_start(raw[:, s, :].rearrange("p (c n) -> p c n", c=CPS), src).then_inc(w_landed[s], 16)

            def w_slab(wt, row0, col0, s):
                return wt[bass.ds(row0 + s * CPS * P, CPS * P), bass.ds(col0, GW)].rearrange("(c p) n -> p c n", p=P)

            def load_unit_slab(m, slot, l, k, col0):
                if not (isinstance(m, int) and m < 2):
                    sp.wait_ge(m_used, m - 1)
                sp.dma_start(mraw[:, slot, :], w_mod[l, bass.ds(k * P, P), bass.ds(col0, HALF)]).then_inc(m_landed[slot], 16)

            def group_slabs(wt, row0, col0):
                return lambda s: w_slab(wt, row0, col0, s)

            def pair_slabs(wt, row0, col0, half):
                return lambda i: w_slab(wt, row0, col0 + i % 2 * GW, 2 * half + i // 2)

            def group_and_units(w0, source, m0, k0, l, mcol, n_m, units_last=False):
                for s in range(SLOTS):
                    if source is not None:
                        load_slab(w0 + s, s, source(s))
                    if not units_last:
                        for j in range(s * n_m // SLOTS, (s + 1) * n_m // SLOTS):
                            load_unit_slab(m0 + j, j % 2, l, k0 + j, mcol)
                if units_last:
                    for j in range(n_m):
                        load_unit_slab(m0 + j, j % 2, l, k0 + j, mcol)

            def stage_loads(w0, wt, row0, col0, n, m0, k_per_group, l, mcol, ahead, opened=False):
                km = k_per_group

                def pair(b, first=False):
                    for j in range(2):
                        source = (pair_slabs(wt, row0, col0, 1) if first and j == 0
                                  else group_slabs(wt, row0, col0 + (b * 2 + (j + 1)) * GW))
                        group_and_units(w0 + b * 8 + 4 * (j + 1), source,
                                        m0 + b * (2 * km) + j * km, b * (2 * km) + j * km, l, mcol, km,
                                        first and j == 1)
                if n == 4 or opened:
                    pair(0, opened)
                if n > 4:
                    with sp.Fori(1 if opened else 0, n // 2 - 1) as b:
                        pair(b)
                b = n // 2 - 1
                group_and_units(w0 + (8 * b + 4), group_slabs(wt, row0, col0 + (2 * b + 1) * GW), m0 + 2 * b * km,
                                2 * b * km, l, mcol, km)
                group_and_units(w0 + (8 * b + 8), ahead, m0 + (2 * b + 1) * km, (2 * b + 1) * km, l, mcol, km)

            for hv in range(4):
                col0 = (1 - hv // 2) * D + (hv % 2) * HALF
                for k in range(KC):
                    w = W_START + hv * KC + k
                    load_slab(w, w % SLOTS, w_mod[0, k * P:(k + 1) * P, col0:col0 + HALF].rearrange(
                        "p (c n) -> p c n", c=CPS))
                    if w == LOAD_X:
                        sp.dma_start(ff.rearrange("p (a d) -> p a d", a=2),
                                     x_in[0].rearrange("(a p) d -> p a d", p=P)).then_inc(x_landed, 16)
                        sp.dma_start(tab[:, 256:TAB_W], tables[:, 256:TAB_W]).then_inc(tab_landed, 16)
                    if w == LOAD_CTX:
                        sp.dma_start(yf.rearrange("p (a d) -> p a d", a=2),
                                     ctx_in[0].rearrange("(a p) d -> p a d", p=P)).then_inc(ctx_landed, 16)
            wi, wo = att_w_in[0], att_w_out[0]
            mcol = lambda un: UNITS[un][1] * D + UNITS[un][2] * HALF
            for s in range(SLOTS):
                load_slab(W_F + s, s, pair_slabs(wi, 0, 0, 0)(s))
            sp.wait_ge(sq_used, 8)
            m = 0
            for i in range(10):
                source = pair_slabs(wi, 0, 0, 1) if i == 0 else group_slabs(wi, 0, (i + 1) * GW)
                for s in range(SLOTS):
                    if i < 9:
                        load_slab(W_F + 4 * (i + 1) + s, s, source(s))
                    for j in unit_places(i, s):
                        load_unit_slab(m + j, (m + j) % 2, 0, (m + j) % UNIT, mcol((m + j) // UNIT))
                m += UNIT_SHARE[i]
            for m in range(M_MID, M_WO):
                slot = (m - M_MID) % SLOTS
                if m < M_MID + SLOTS:
                    sp.wait_ge(lo_ready, W_V + slot + 1)
                else:
                    sp.wait_ge(m_used, m - (SLOTS - 1))
                sp.dma_start(raw[:, slot, :], w_mod[0, m % UNIT * P:(m % UNIT + 1) * P,
                                                    mcol(m // UNIT):mcol(m // UNIT) + HALF]
                             ).then_inc(mid_landed[slot], 16)
            for s in range(SLOTS):
                sp.wait_ge(m_used, M_WO - (M_WO - 1 - M_MID - s) % SLOTS)
                load_slab(slab_of(PG_WO) + s, s, w_slab(wo, 0, 0, s))
            stage_loads(slab_of(PG_WO), wo, 0, 0, 8, UNIT * U_WO, 2, 0, mcol(U_WO), pair_slabs(mlp_w1[0], 0, 0, 0))

            def mlp_loads(l, u0, loop_units, ahead):
                w1, w2 = mlp_w1[l], mlp_w2[l]
                w0 = slab_of(PG_MLP[l])

                def quarter(q, un, n_m, ml, mc1, mc2, nxt, opened=False):
                    stage_loads(w0 + q * 64, w1, 0, q * D, 8, un * UNIT, n_m, ml, mc1, group_slabs(w2, q * D, 0), opened)
                    stage_loads(w0 + q * 64 + 32, w2, q * D, 0, 8, un * UNIT + UNIT, n_m, ml, mc2, nxt)
                quarter(0, u0, 2, l, 5 * D, 5 * D + HALF, group_slabs(w1, 0, D), opened=True)
                with sp.Fori(0, 2) as q:
                    quarter(q + 1, q * 2 + (u0 + 2), loop_units, 1, q * D, q * D + HALF,
                            group_slabs(w1, 0, (q + 2) * D))
                quarter(3, u0 + 6, loop_units, 1, 2 * D, 2 * D + HALF, ahead)

            ci = conv_w_in[0]
            mlp_loads(0, U_MLP0, 2, lambda i: w_slab(ci, 0, (1 + i % 2) * D, i // 2))

            def triple_loads(t, t0, w0, m0, k0, l, col, n_m, nxt_w, nxt_col, opened=False):
                for j, (wt, col0) in enumerate(((ci, t * GW + (t0 * GW + 2 * D)), (ci, t * GW + t0 * GW),
                                                 (nxt_w, nxt_col))):
                    for s in range(SLOTS):
                        source = (w_slab(ci, 0, (1 + s % 2) * D, 2 + s // 2) if opened and j == 0
                                  else w_slab(wt, 0, col0, s))
                        load_slab(w0 + (4 * (j + 1) + s), s, source)
                        if not (opened and j == 1):
                            for i in conv_unit_slabs(4 * j + s, n_m):
                                load_unit_slab(m0 + i, i % 2, l, k0 + i, col)
                    if opened and j == 1:
                        for i in range(4 * n_m // 12, 8 * n_m // 12):
                            load_unit_slab(m0 + i, i % 2, l, k0 + i, col)

            w0 = slab_of(PG_CONV)
            for t0, n_t, un, n_m in CONV_PARTS:
                whole = n_t if t0 + n_t < 8 else n_t - 1
                if t0 == 0:
                    triple_loads(0, 0, w0, UNIT * un, 0, 1, mcol(un), n_m, ci, D + GW, opened=True)
                with sp.Fori(2 if t0 == 0 else 1, whole + 1) as t:
                    triple_loads(t, t0 - 1, t * 12 + (w0 + 12 * (t0 - 1)), t * n_m + (UNIT * un - n_m),
                                 t * n_m - n_m, 1, mcol(un), n_m, ci, t * GW + (D + t0 * GW))
            triple_loads(7, 0, w0 + 84, UNIT * un + 7 % n_t * n_m, 7 % n_t * n_m, 1, mcol(un), n_m, conv_w_out[0], 0)
            co = conv_w_out[0]
            stage_loads(slab_of(PG_CO), co, 0, 0, 8, UNIT * U_CO, 2, 1, mcol(U_CO), pair_slabs(mlp_w1[1], 0, 0, 0))
            mlp_loads(1, U_MLP1, 0, None)
            for b in range(4):
                for a in range(2):
                    sp.wait_ge(out_copied, 2 * b + a + 1)
                    sp.dma_start(out[0, a * P:(a + 1) * P, b * 512:(b + 1) * 512],
                                 ff[:, a * D + b * 512:a * D + (b + 1) * 512]).then_inc(out_stored, 16)
            sp.wait_ge(out_stored, 16 * 8)

        @block.tensor
        def _(pe):
            stage = acc[:, 0, :]
            pe.wait_ge(tab_landed, 16)
            pe.wait_ge(small_landed, 7 * 16)
            for n, col, dst in ((32, 0, 0), (128, 128, 32), (96, 256, 160), (96, 384, 256), (48, 512, 352)):
                last = pe.transpose(ps[:, 3, dst:dst + n], stage[0:n, col:col + 128], ident[0:n, 0:n])
            last.then_inc(small_t, 1)
            pe.matmul(ps[:, 2, 0:HEADS], ones[0:1, :], sinkr[:, :], start=True, stop=True).then_inc(sink_b, 1)

            def turn_input(i, src, landed, turned, copied, bank):
                if i == 0:
                    pe.wait_ge(landed, 16)
                if i >= 2:
                    pe.wait_ge(copied, i - 1)
                for c in range(2):
                    for a in range(2):
                        last = pe.transpose(ps[:, bank + i % 2, c * T + a * P:c * T + (a + 1) * P],
                                            src[:, a * D + (2 * i + c) * P:a * D + (2 * i + c + 1) * P], ident)
                last.then_inc(turned, 1)

            def sum_squares(n, b, bank):
                src = mraw[:, n % 2, :] if n < 8 else sqx[n % 2]
                pe.wait_ge(sq_ready, n + 1)
                for c in range(4):
                    last = pe.matmul(ps[:, bank, 0:T], ones, src[:, c * T:(c + 1) * T],
                                     start=(b == 0 and c == 0), stop=(b == 3 and c == 3))
                last.then_inc(sq_used, 1)

            def turn_rows(hv):
                pe.wait_ge(row_copied, hv + 1)
                for c in range(8):
                    last = pe.transpose(ps[:, 5, hv * 32 + 4 * c:hv * 32 + 4 * c + 4],
                                        row[hv % 2][:, c * P:(c + 1) * P], ident[0:4, 0:4])
                last.then_inc(row_t, 1)

            def beside_slab(w):
                if 0 <= w - PE_TURN_X < 8:
                    turn_input(w - PE_TURN_X, ff, x_landed, x_t, x_copied, 4)
                if w in PE_SUM_X:
                    b = PE_SUM_X.index(w)
                    sum_squares(b, b, 6)
                if 0 <= w - PE_TURN_CTX < 8:
                    if w == PE_TURN_CTX:
                        pe.wait_ge(sd_ready, 1)
                    turn_input(w - PE_TURN_CTX, yf, ctx_landed, ctx_t, ctx_copied, 6)
                if w in PE_SUM_CTX:
                    b = PE_SUM_CTX.index(w)
                    sum_squares(4 + b, b, 4)
                if w % KC == PE_TURN_ROWS and w > KC:
                    if w < 2 * KC:
                        pe.wait_ge(x_copied, 8)
                    turn_rows(w // KC - 1)

            pe.wait_ge(crs_lo, 1)
            for w in range(4 * KC):
                hv, k = divmod(w, KC)
                beside_slab(w)
                if k == 0 and hv == 1:
                    pe.wait_ge(small_copied, 1)
                    pe.wait_ge(sink_copied, 1)
                if k == 0 and hv >= 2:
                    pe.wait_ge(row_copied, hv - 1)
                pe.wait_ge(lo_ready, w + 1)
                for part in (whi, wlo):
                    for n in range(2):
                        last = pe.matmul(ps[:, 2 * (hv % 2) + n, :], u[:, k, 0:128],
                                         part[:, w % SLOTS, n * 512:(n + 1) * 512],
                                         start=(k == 0 and part is whi), stop=(k == KC - 1 and part is wlo))
                last.then_inc(slab_used, 1)
            turn_rows(3)

            def group(pg, w0, src, banks, input_waits, src2=None, free=None):
                if not (isinstance(pg, int) and pg < 2):
                    pe.wait_ge(sum_done, pg - 1 if free is None else free)
                for s in range(SLOTS):
                    pe.wait_ge(lo_ready, w0 + (s + 1))
                    for sm_, n in input_waits(s):
                        pe.wait_ge(sm_, n)
                    for c in range(CPS):
                        k = s * CPS + c
                        for m in range(2):
                            for i, inp in enumerate((src,) if src2 is None else (src, src2)):
                                bk = banks[2 * i + m]
                                pe.matmul(ps[:, bk, :], whi[:, s, c * GW + m * P:c * GW + (m + 1) * P], inp[:, k, :],
                                          start=(k == 0), stop=False)
                                last = pe.matmul(ps[:, bk, 0:T], wlo[:, s, c * GW + m * P:c * GW + (m + 1) * P],
                                                 inp[:, k, 0:T], start=False, stop=(k == KC - 1))
                        if c == CPS - 1:
                            last.then_inc(slab_used, 1)

            def open_pair(pg0, w0, src, base):
                first_batch = [0, 1, 2, 2]
                for i in range(2):
                    if pg0:
                        pe.wait_ge(sum_done, pg0 - 1 + i)
                for i in range(2 * SLOTS):
                    s, g = divmod(i, 2)
                    pe.wait_ge(lo_ready, w0 + i + 1)
                    if g == 0 and s:
                        pe.wait_ge(u_ready, base + s + 3)
                    for c in range(CPS):
                        k = s * CPS + c
                        if i == 0 and (c == 0 or first_batch[c] > first_batch[c - 1]):
                            pe.wait_ge(u_ready, base + first_batch[c] + 1)
                        for m in range(2):
                            cols = slice(c * GW + m * P, c * GW + (m + 1) * P)
                            pe.matmul(ps[:, 2 * g + m, :], whi[:, i % SLOTS, cols], src[:, k, :],
                                      start=(k == 0), stop=False)
                            last = pe.matmul(ps[:, 2 * g + m, 0:T], wlo[:, i % SLOTS, cols], src[:, k, 0:T],
                                             start=False, stop=(k == KC - 1))
                    last.then_inc(slab_used, 1)

            def stage_groups(pg0, n, src, input_waits):
                with pe.Fori(0, n // 2) as b:
                    for j in range(2):
                        group(b * 2 + (pg0 + j), b * 8 + slab_of(pg0 + j), src, (2 * j, 2 * j + 1), input_waits)

            open_pair(PG_F, W_F, u, 0)
            with pe.Fori(1, 4) as b:
                for j in range(2):
                    group(b * 2 + (PG_F + j), b * 8 + (W_F + 4 * j), u, (2 * j, 2 * j + 1), lambda s: [])
            pe.wait_ge(modc_step, 4)
            group(PG_K, W_K, u, (0, 1, 4, 5), lambda s: [(c_ready, s + 1)], h)
            group(PG_V, W_V, u, (2, 3, 6, 7), lambda s: [], h, free=PG_K)

            pe.wait_ge(rope_step, 3 * 5)
            pe.wait_ge(sum_done, PG_K + 2)
            pe.wait_ge(tab_landed, 32)

            def scores(un):
                hd, qt = divmod(un, 2)
                if un >= 3:
                    pe.wait_ge(p_ready, un - 2)
                pe.matmul(ps[:, un % 3, :], qh[:, hd, qt * P:(qt + 1) * P], kT[:, hd // GQA, :],
                          start=True, stop=True).then_inc(s_done, 1)

            def turn_probs(un):
                pe.wait_ge(pn_ready, un + 1)
                if un >= 2:
                    pe.wait_ge(pt_copied, un - 1)
                for kt in range(4):
                    last = pe.transpose(ps[:, 4 + un % 2, kt * P:(kt + 1) * P], prob[un % 2][:, kt * P:(kt + 1) * P],
                                        ident)
                last.then_inc(pt_done, 1)

            def values(hd):
                pe.wait_ge(pt_copied, 2 * hd + 2)
                if hd >= 1:
                    pe.wait_ge(o_ready, hd)
                for kt in range(4):
                    last = pe.matmul(ps[:, 6, (hd % 2) * T:(hd % 2 + 1) * T],
                                     v[:, kt, (hd // GQA) * HD:(hd // GQA + 1) * HD], probT[hd % 2][:, kt, :],
                                     start=(kt == 0), stop=(kt == 3))
                last.then_inc(pv_done, 1)

            def channel_dft(g, a):
                if 2 * g + a >= 1:
                    pe.wait_ge(fa_copied, 2 * (2 * g + a))
                for kc in range(2):
                    last = pe.matmul(ps[:, 3, :], fin[:, 2 * g + kc, a * P:(a + 1) * P], dft[:, kc, :],
                                     start=(kc == 0), stop=(kc == 1))
                last.then_inc(fa_done, 1)

            def token_dft(g, m):
                if m == 0:
                    pe.wait_ge(fa_copied, 4 * g + 4)
                    if g >= 1:
                        pe.wait_ge(f_ready, g)
                for i in range(4):
                    trig, a = divmod(i, 2)
                    last = pe.matmul(ps[:, 7, m * T:(m + 1) * T],
                                     ucs[:, a, trig * T + m * P:trig * T + (m + 1) * P],
                                     dft[:, a, trig * T:(trig + 1) * T], start=(i == 0), stop=(i == 3))
                last.then_inc(fb_done, 1)

            for un in range(2):
                scores(un)
            pe.wait_ge(sum_done, PG_WO)
            scores(2)
            for kv in range(KV_HEADS):
                for kt in range(4):
                    last = pe.transpose(ps[:, 4 + kv, kt * P:(kt + 1) * P], vsum[:, kv, kt * P:(kt + 1) * P], ident)
                last.then_inc(v_t, 1)
            pe.wait_ge(v_ready, KV_HEADS)
            for un in range(2 * HEADS):
                turn_probs(un)
                if un + 3 < 2 * HEADS:
                    scores(un + 3)
                (channel_dft if un % 4 < 2 else token_dft)(un // 4, un % 2)
                if un % 2 == 1 and un >= 3:
                    values(un // 2 - 1)
            values(HEADS - 1)

            pe.wait_ge(f_ready, FG)
            pe.wait_ge(o_ready, HEADS)
            stage_groups(PG_WO, 8, u, lambda s: [])

            def boundary_sums(j, n_sq):
                pe.wait_ge(ssq_done, 8 * (j + 1))
                for m in range(2):
                    last = pe.matmul(ps[:, 6, 0:T], ones, ssq[:, m, :], start=(m == 0), stop=(m == 1))
                last.then_inc(norm_sum, 1)
                if n_sq:
                    for b in range(4):
                        sum_squares(8 + 4 * j + b, b, 7)

            def mlp_groups(l):
                pg0 = PG_MLP[l]
                u0 = (6, 18)[l]
                h0 = 32 * l

                def quarter(q, opened=False):
                    for part, src in ((0, u), (1, h)):
                        waits = (lambda s: []) if part == 0 else (lambda s: [(h_ready, q * 8 + (h0 + 2 * (s + 1)))])
                        first = opened and part == 0
                        if first:
                            open_pair(pg0, slab_of(pg0), u, u0)
                        with pe.Fori(1 if first else 0, 4) as b:
                            for j in range(2):
                                pg = q * 16 + b * 2 + (pg0 + 8 * part + j)
                                group(pg, q * 64 + b * 8 + (slab_of(pg0) + 32 * part + 4 * j), src,
                                      (2 * j, 2 * j + 1), waits)
                quarter(0, opened=True)
                with pe.Fori(0, 2) as q:
                    quarter(q + 1)
                quarter(3)

            boundary_sums(0, 4)
            mlp_groups(0)
            boundary_sums(1, 4)
            open_pair(PG_CONV, slab_of(PG_CONV), u, 12)
            group(PG_CONV + 2, slab_of(PG_CONV + 2), u, (4, 5), lambda s: [])
            with pe.Fori(1, 8) as t:
                for j in range(3):
                    group(t * 3 + (PG_CONV + j), t * 12 + (slab_of(PG_CONV) + 4 * j), u, (2 * j, 2 * j + 1),
                          lambda s: [])
            with pe.Fori(0, 4) as b:
                for j in range(2):
                    group(b * 2 + (PG_CO + j), b * 8 + slab_of(PG_CO + j), h, (2 * j, 2 * j + 1),
                          lambda s: [(conv_ready, 2 * (s + 1))])
            boundary_sums(2, 4)
            mlp_groups(1)
            boundary_sums(3, 0)
            for b in range(4):
                pe.wait_ge(x_step, 13 + b)
                for a in range(2):
                    n = 2 * b + a
                    if n >= 4:
                        pe.wait_ge(out_copied, n - 3)
                    for c in range(4):
                        last = pe.transpose(ps[:, n % 4, c * P:(c + 1) * P], x[:, 4 * b + c, a * P:(a + 1) * P], ident)
                    last.then_inc(out_t, 1)

        @block.scalar
        def _(act):
            def hi(w, s):
                act.wait_ge(w_landed[s], w * 4 + (16 - 4 * s) if not isinstance(w, int) else 16 * (w // SLOTS + 1))
                if not (isinstance(w, int) and w < SLOTS):
                    act.wait_ge(slab_used, w - (SLOTS - 1))
                act.activation(whi[:, s, :], raw[:, s, :], ACT.Copy).then_inc(hi_ready, 1)

            def his(w0, after_first=None):
                for s in range(SLOTS):
                    hi(w0 + s, s)
                    if s == 0 and after_first:
                        after_first()

            act.wait_ge(small_copied, 1)
            act.activation(sg[:, :], cT, ACT.Exp, scale=-1.0).then_inc(silu_exp, 1)
            act.wait_ge(silu_step, 3)
            act.wait_ge(crs_zero, 1)
            act.activation(u[:, :, 0:2], cs[:, :].rearrange("p (w k) -> p k w", w=2), ACT.Copy).then_inc(crs_hi, 1)

            def square(n, src):
                if n >= 2:
                    act.wait_ge(sq_used, n - 1)
                dst = mraw[:, n % 2, :] if n < 8 else sqx[n % 2]
                act.activation(dst, src, ACT.Square).then_inc(sq_ready, 1)

            def root(dst, bank):
                act.activation(dst, ps[:, bank, 0:T], ACT.Sqrt, bias=eps, scale=1.0 / D).then_inc(sd_ready, 1)

            def copy_row(hv):
                act.wait_ge(slab_used, UNIT * (hv + 1))
                if hv == 1:
                    act.wait_ge(small_t, 1)
                if hv >= 2:
                    act.wait_ge(row_t, hv - 1)
                bank = 2 * (hv % 2)
                act.activation(row[hv % 2].rearrange("p (m n) -> p m n", m=2), ps[0:4, bank:bank + 2, :],
                               ACT.Copy).then_inc(row_copied, 1)

            def beside_slab(w):
                if w in ACT_SQ_X:
                    b = ACT_SQ_X.index(w)
                    act.wait_ge(x_copied, 2 * b + 2)
                    square(b, xf[:, 1024 * b:1024 * b + 1024])
                if w == ACT_ROOT_X:
                    act.wait_ge(tab_landed, 32)
                    act.wait_ge(sq_used, 4)
                    root(stat[:, 0, :], 6)
                if 0 <= w - ACT_CTX < 8:
                    i = w - ACT_CTX
                    act.wait_ge(x_t, 8)
                    act.wait_ge(ctx_t, i + 1)
                    act.activation(fq[:, 2 * i:2 * i + 2, :], ps[:, 6 + i % 2, :].rearrange("p (c t) -> p c t", c=2),
                                   ACT.Copy).then_inc(ctx_copied, 1)
                if w in ACT_SQ_CTX:
                    b = ACT_SQ_CTX.index(w)
                    act.wait_ge(ctx_copied, 2 * b + 2)
                    square(4 + b, ff[:, 1024 * b:1024 * b + 1024])
                if w == ACT_ROOT_CTX:
                    act.wait_ge(sq_used, 8)
                    root(stat[:, 2, :], 4)
                if w % KC == ACT_ROWS and w > KC:
                    copy_row(w // KC - 1)

            def modulate(n0, xr, mt, gs, shift, hooks, batches=range(len(BATCHES)), at=HOOKS):
                for b in batches:
                    c0, n = BATCHES[b]
                    act.wait_ge(u_scaled, n0 + b + 1)
                    if n0 + b >= 2:
                        act.wait_ge(u_ready, n0 + b - 1)
                    mine = n if n < 4 else 3
                    for c in range(mine):
                        last = act.activation(mt[b % 2][:, c, :], xr[b % 2][:, c, :], ACT.Identity,
                                              scale=gs[:, c0 + c], bias=shift[:, c0 + c])
                    last.then_inc(u_shifted, 1)
                    act.wait_ge(u_shifted, n0 + b + 1)
                    if mine < n:
                        act.wait_ge(u_shifted_dve, n0 // 2 + b - 2)
                    act.activation(u[:, c0:c0 + n, 0:T], mt[b % 2][:, 0:n, :], ACT.Copy).then_inc(u_hi, 1)
                    for s in at[b]:
                        hooks(s)

            def start_modulate(*batches):
                modulate(0, start_xr, start_mt, modc_col(0, 0), modc_col(1, 0), lambda s: hi(W_F + 4 + s, s),
                         batches, START_HOOKS)

            for w in range(4 * KC + SLOTS):
                hi(w, w % SLOTS)
                beside_slab(w)
                if w in FIRST_BATCHES:
                    b = FIRST_BATCHES.index(w)
                    act.wait_ge(modc_step, 3)
                    act.wait_ge(slab_used, 3 * KC + sum(BATCHES[b]))
                    start_modulate(b)
            act.wait_ge(modc_step, 4)
            start_modulate(4, 5)

            def context_high(b):
                act.wait_ge(c_scaled, b + 1)
                for c in range(4 * b, 4 * b + 4):
                    last = act.activation(fq[:, c, :], fq[:, c, :], ACT.Identity, scale=modc_col(0, 1)[:, c],
                                          bias=modc_col(1, 1)[:, c])
                last.then_inc(c_shifted, 1)
                act.wait_ge(c_shifted, b + 1)
                act.activation(h[:, 4 * b:4 * b + 4, 0:T], fq[:, 4 * b:4 * b + 4, :], ACT.Copy).then_inc(c_hi, 1)

            def right_half(pg, bank, w_end):
                act.wait_ge(slab_used, w_end)
                if not (isinstance(pg, int) and pg == 0):
                    act.wait_ge(sum_done, pg)
                act.activation(tmp[:, :, :], ps[:, bank:bank + 2, T:2 * T], ACT.Copy).then_inc(b_copied, 1)

            def rope_swap(r):
                act.wait_ge(sum_done, PG_Q + r + 1)
                for a, b in ((0, 32), (32, 0), (64, 96), (96, 64)):
                    last = act.activation(qsw[a:a + 32], qs[b:b + 32], ACT.Copy)
                last.then_inc(rope_swapped, 1)

            def open_halves(pg0, w0, after):
                for s in range(SLOTS - 1):
                    hi(w0 + 8 + s, s)
                right_half(pg0, 0, w0 + 7)
                after(0)
                hi(w0 + 11, 3)
                right_half(pg0 + 1, 2, w0 + 8)
                after(1)

            context_high(0)
            open_halves(PG_F, W_F, lambda i: None)
            for i in range(2, 8):
                his(W_F + 4 * i + 4, (lambda: rope_swap(i - 5)) if i >= 5 else None)
                right_half(PG_F + i, 2 * (i % 2), W_F + 4 * i + 4)
                if i in CONTEXT_AT:
                    context_high(CONTEXT_AT.index(i))
            his(W_V, lambda: rope_swap(3))
            right_half(PG_K, 0, W_K + 4)
            right_half(PG_K + 1, 4, W_K + 4)
            rope_swap(4)
            act.activation(sg[:, 0:1], sg[:, 0:1], ACT.Exp)
            right_half(PG_V, 2, W_V + 4)
            right_half(PG_V + 1, 6, W_V + 4)

            def stage(pg0, n, after, q=None, opened=False, closing=False):
                w0 = slab_of(pg0)

                def pair(b, last=False):
                    for j in range(2):
                        pg, w = b * 2 + (pg0 + j), b * 8 + (w0 + 4 * j)
                        if q is not None:
                            pg, w = q * 16 + pg, q * 64 + w
                        if not (last and j == 1):
                            his(w + 4)
                        right_half(pg, 2 * j, w + 4)
                        after(pg, b * 2 + j)
                if opened:
                    open_halves(pg0, w0, lambda i: after(pg0 + i, i))
                with act.Fori(1 if opened else 0, n // 2 - closing) as b:
                    pair(b)
                if closing:
                    pair(n // 2 - 1, last=True)

            def probabilities(un):
                hd = un // 2
                act.wait_ge(negm_ready, un + 1)
                if un >= 2:
                    act.wait_ge(pt_done, un - 1)
                act.activation(sm[:, 2, un:un + 1], nsink[:, 0, hd:hd + 1], ACT.Exp, bias=sm[:, 1, un:un + 1])
                act.activation(prob[un % 2], ps[:, un % 3, :], ACT.Exp, bias=sm[:, 1, un:un + 1], scale=SCALE,
                               accum_out=sm[:, 3, un:un + 1]).then_inc(p_ready, 1)

            def normalized(un):
                act.wait_ge(p_ready, un + 1)
                act.wait_ge(rden_ready, un + 1)
                act.activation(prob[un % 2], prob[un % 2], ACT.Copy, scale=sm[:, 4, un:un + 1]).then_inc(pn_ready, 1)

            def probs_turned(un):
                hd, qt = divmod(un, 2)
                act.wait_ge(pt_done, un + 1)
                if hd >= 2:
                    act.wait_ge(pv_done, hd - 1)
                act.activation(probT[hd % 2][:, :, qt * P:(qt + 1) * P],
                               ps[:, 4 + un % 2, :].rearrange("p (k q) -> p k q", k=4), ACT.Copy).then_inc(pt_copied, 1)

            def channel_transformed(g, a):
                act.wait_ge(fa_done, 2 * g + a + 1)
                if g >= 1:
                    act.wait_ge(fb_done, 2 * g)
                for trig, sign in ((0, 1.0), (1, -1.0)):
                    act.activation(ucs[:, a, trig * T:(trig + 1) * T], ps[:, 3, trig * T:(trig + 1) * T],
                                   ACT.Copy, scale=sign / T).then_inc(fa_copied, 1)

            def fourier_high(g):
                act.wait_ge(fb_done, 2 * g + 2)
                act.activation(u[:, 2 * g:2 * g + 2, 0:T], ps[:, 7, :].rearrange("p (c t) -> p c t", c=2),
                               ACT.Copy).then_inc(fb_hi, 1)

            def o_high(hd):
                act.wait_ge(pv_done, hd + 1)
                act.activation(u[:, 8 + hd, 0:T], ps[:, 6, (hd % 2) * T:(hd % 2 + 1) * T], ACT.Copy).then_inc(o_hi, 1)

            probabilities(0)
            for kv in range(KV_HEADS):
                act.wait_ge(v_t, kv + 1)
                act.activation(v[:, :, kv * HD:(kv + 1) * HD], ps[:, 4 + kv, :].rearrange("p (k d) -> p k d", k=4),
                               ACT.Copy).then_inc(v_ready, 1)
            for un in range(2 * HEADS):
                if un + 1 < 2 * HEADS:
                    probabilities(un + 1)
                normalized(un)
                probs_turned(un)
                if un >= 2 * HEADS - 2:
                    for s in range(2):
                        hi(slab_of(PG_WO) + 2 * (un % 2) + s, 2 * (un % 2) + s)
                if un % 4 == 0 and un:
                    fourier_high(un // 4 - 1)
                if un % 4 < 2:
                    channel_transformed(un // 4, un % 4)
                if un % 2 == 0 and un >= 4:
                    o_high(un // 2 - 2)
            fourier_high(FG - 1)
            o_high(HEADS - 2)
            o_high(HEADS - 1)
            act.activation(sg[:, 0:1], eps, ACT.Sqrt)

            def y_squares(j):
                def f(pg, i):
                    act.wait_ge(sum_done, pg + 1)
                    act.activation(sq, y[:, bass.ds(i * 2, 2), :], ACT.Square).then_inc(ysq_ready, 1)
                    act.wait_ge(ysq_ready, i + (8 * j + 1))
                    for m in range(2):
                        c = bass.ds(i * 2 + m, 1)
                        last = act.activation(y[:, c, :], y[:, c, :], ACT.Copy, scale=der[:, 0, c])
                    last.then_inc(yg_ready, 1)
                return f

            def boundary(j, shift, w0=None):
                act.wait_ge(norm_sum, j + 1)
                root(stat[:, 0, :], 6)
                if shift is None:
                    return
                his(w0)
                for b in range(4):
                    act.wait_ge(x_step, 4 * j + b + 1)
                    square(8 + 4 * j + b, xf[:, b * 1024:(b + 1) * 1024])
                act.wait_ge(sq_used, 12 + 4 * j)
                root(stat[:, 2, :], 7)
                act.wait_ge(gs_ready, j + 1)
                modulate(6 + 6 * j, late_xr, late_mt, der[:, 1, :].unsqueeze(2), vt[:, shift:shift + KC].unsqueeze(2),
                         lambda s: hi(w0 + 4 + s, s))

            def mlp(l):
                pg0 = PG_MLP[l]

                def h_high(q):
                    def f(pg, i):
                        act.wait_ge(relu2_ready, q * 8 + i + (32 * l + 1))
                        act.activation(h[:, bass.ds(i * 2, 2), 0:T], relu2, ACT.Copy).then_inc(h_hi, 1)
                    return f

                def quarter(q, after2, opened=False):
                    stage(pg0, 8, h_high(q), q, opened)
                    stage(pg0 + 8, 8, after2, q)
                quarter(0, lambda pg, i: None, opened=True)
                with act.Fori(0, 2) as q:
                    quarter(q + 1, lambda pg, i: None)
                stage(pg0, 8, h_high(3), 3)
                if l == 0:
                    stage(pg0 + 8, 8, y_squares(1), 3, closing=True)
                else:
                    stage_end(pg0 + 8, y_squares(3))

            def stage_end(pg0, after):
                w0 = slab_of(pg0) + 192
                pg0 += 48
                with act.Fori(0, 3) as b:
                    for j in range(2):
                        his(b * 8 + (w0 + 4 * j + 4))
                        right_half(b * 2 + (pg0 + j), 2 * j, b * 8 + (w0 + 4 * j + 4))
                        after(b * 2 + (pg0 + j), b * 2 + j)
                his(w0 + 28)
                right_half(pg0 + 6, 0, w0 + 28)
                after(pg0 + 6, 6)
                right_half(pg0 + 7, 2, w0 + 32)
                after(pg0 + 7, 7)

            act.wait_ge(gg_ready, 1)
            stage(PG_WO, 8, y_squares(0), closing=True)
            boundary(0, 3 * KC, slab_of(PG_MLP[0]))
            mlp(0)
            boundary(1, 6 * KC, slab_of(PG_CONV))

            def triple(t, opened=False):
                if opened:
                    open_halves(PG_CONV, slab_of(PG_CONV), lambda i: None)
                for j in range(2 if opened else 0, 3):
                    pg, w = t * 3 + (PG_CONV + j), t * 12 + (slab_of(PG_CONV) + 4 * j)
                    his(w + 4)
                    right_half(pg, 2 * j, w + 4)
                act.wait_ge(conv_step, t * 5 + 5)
                act.activation(h[:, bass.ds(t * 2, 2), 0:T], cv, ACT.Copy).then_inc(v_hi, 1)
            triple(0, opened=True)
            with act.Fori(1, 8) as t:
                triple(t)
            act.wait_ge(gg_ready, 3)
            stage(PG_CO, 8, y_squares(2), closing=True)
            boundary(2, 6 * KC + 3 * KC, slab_of(PG_MLP[1]))
            mlp(1)
            boundary(3, None)
            for n in range(8):
                b, a = divmod(n, 2)
                act.wait_ge(out_t, n + 1)
                act.activation(ff[:, a * D + b * 512:a * D + (b + 1) * 512], ps[:, n % 4, :], ACT.Copy).then_inc(out_copied, 1)

        @block.vector
        def _(dve):
            def lo(w, s):
                dve.wait_ge(hi_ready, w + 1)
                dve.tensor_tensor(wlo[:, s, :], raw[:, s, :], whi[:, s, :], ALU.subtract).then_inc(lo_ready, 1)

            def los(w0):
                for s in range(SLOTS):
                    lo(w0 + s, s)

            def unit_slab(m, parity, un, k, acc_i):
                if isinstance(m, int) and M_MID <= m < M_WO:
                    slot = (m - M_MID) % SLOTS
                    src = raw[:, slot, :]
                    dve.wait_ge(mid_landed[slot], 16 * ((m - M_MID) // SLOTS + 1))
                else:
                    before = 0 if isinstance(m, int) and m < M_MID else M_WO - M_MID
                    src = mraw[:, parity, :]
                    dve.wait_ge(m_landed[parity], m * 8 + (16 - 8 * parity - 8 * before))
                dve.wait_ge(acc_zeroed, un + 1)
                if not (isinstance(m, int) and m == 0):
                    dve.wait_ge(m_used, m)
                a = acc[:, acc_i, :]
                dve.scalar_tensor_tensor(out=a, in0=src, scalar=cs[:, bass.ds(k, 1)], in1=a,
                                         op0=ALU.mult, op1=ALU.add).then_inc(m_used, 1)

            def unit_slabs(m0, un, k0, js, acc_i):
                for j in js:
                    unit_slab(m0 + j, j % 2, un, k0 + j, acc_i)

            def finish_unit(un, col):
                dve.wait_ge(unit_masked, un + 1)
                if not (isinstance(un, int) and un == 0):
                    dve.wait_ge(mod_ready, un)
                dve.tensor_reduce(t8[:, :], red[:, :].rearrange("p (c f) -> p c f", f=P), AX_X,
                                  ALU.add).then_inc(unit_read, 1)
                dve.wait_ge(unit_read, un + 1)
                dve.tensor_tensor(vt[:, bass.ds(col, KC // 2)], t8[:, :], bT[:, bass.ds(col, KC // 2)],
                                  ALU.add).then_inc(mod_ready, 1)

            dve.memset(u[:, :, 0:128].bitcast(F32), 0.0).then_inc(crs_zero, 1)
            dve.wait_ge(small_t, 1)
            dve.tensor_copy(small[:, :], ps[:, 3, 0:400]).then_inc(small_copied, 1)
            dve.wait_ge(sink_b, 1)
            dve.tensor_copy(nsink[:, 0, :], ps[:, 2, 0:HEADS])
            dve.tensor_scalar(nsink[:, 1, :], ps[:, 2, 0:HEADS], -1.0, None, ALU.mult).then_inc(sink_copied, 1)
            dve.wait_ge(silu_exp, 1)
            dve.tensor_scalar(sg[:, :], sg[:, :], 1.0, None, ALU.add).then_inc(silu_step, 1)
            dve.wait_ge(silu_step, 1)
            dve.reciprocal(sg[:, :], sg[:, :]).then_inc(silu_step, 1)
            dve.wait_ge(silu_step, 2)
            dve.wait_ge(small_copied, 1)
            dve.tensor_tensor(cs[:, :], cT, sg[:, :], ALU.mult).then_inc(silu_step, 1)
            dve.wait_ge(crs_hi, 1)
            dve.tensor_tensor(u[:, :, 2:4], cs[:, :].rearrange("p (w k) -> p k w", w=2), u[:, :, 0:2],
                              ALU.subtract).then_inc(crs_lo, 1)

            def reciprocal_root(n, i):
                dve.wait_ge(sd_ready, n)
                dve.reciprocal(stat[:, i + 1, :], stat[:, i, :]).then_inc(rstd_ready, 1)
                dve.wait_ge(rstd_ready, n)

            def both(a):
                return a.unsqueeze(2).broadcast_to([P, KC, 2])

            def pairs(a):
                return a.rearrange("p (c w) -> p c w", w=2)
            def mixer_vector(what, col, c0, n):
                turned = ps[:, 5, 64 * what + 4 * c0:64 * what + 4 * (c0 + n)].rearrange("p (c r) -> p c r", r=4)
                dst = pairs(modc[:, what, 2 * c0:2 * (c0 + n)])
                bias = bT[:, col + c0:col + c0 + n].unsqueeze(2).broadcast_to([P, n, 2])
                dve.tensor_tensor(dst, turned[:, :, 0:2], bias, ALU.add).then_inc(modc_part, 1)
                dve.wait_ge(modc_part, 1 + what + (c0 > 0))
                dve.tensor_tensor(dst, turned[:, :, 2:4], dst, ALU.add).then_inc(modc_step, 1)

            def beside_slab(w):
                if 0 <= w - DVE_X < 8:
                    i = w - DVE_X
                    dve.wait_ge(x_t, i + 1)
                    dve.tensor_copy(x[:, 2 * i:2 * i + 2, :],
                                    ps[:, 4 + i % 2, :].rearrange("p (c t) -> p c t", c=2)).then_inc(x_copied, 1)
                if w == DVE_ROOT_X:
                    reciprocal_root(1, 0)
                if w == DVE_ROOT_CTX:
                    reciprocal_root(2, 2)
                if w == DVE_SCALE:
                    dve.wait_ge(row_t, 2)
                    mixer_vector(0, KC, 0, KC)
                    dve.wait_ge(modc_step, 1)
                    dve.scalar_tensor_tensor(out=pairs(modc[:, 0, :]), in0=pairs(modc[:, 0, :]), scalar=1.0,
                                             in1=both(gT[:, 0:KC]), op0=ALU.add, op1=ALU.mult).then_inc(modc_step, 1)
                if w == DVE_SHIFT:
                    dve.wait_ge(row_t, 3)
                    mixer_vector(1, 0, 0, KC // 2)

            def modulate(n0, rstd, xr, mt, gs, shift, hooks, batches=range(len(BATCHES)), at=HOOKS):
                def scaled(b):
                    c0, n = BATCHES[b]
                    dve.tensor_tensor(xr[b % 2][:, 0:n, :], x[:, c0:c0 + n, :],
                                      rstd.unsqueeze(1).broadcast_to([P, n, T]), ALU.mult).then_inc(u_scaled, 1)
                if batches[0] == 0:
                    scaled(0)
                for b in batches:
                    c0, n = BATCHES[b]
                    if b + 1 < len(BATCHES):
                        if b >= 1:
                            dve.wait_ge(u_ready, n0 + b)
                        scaled(b + 1)
                    if n == 4:
                        dve.wait_ge(u_scaled, n0 + b + 1)
                        dve.tensor_scalar(mt[b % 2][:, 3, :], xr[b % 2][:, 3, :], gs[:, c0 + 3], shift[:, c0 + 3],
                                          ALU.mult, ALU.add).then_inc(u_shifted_dve, 1)
                    dve.wait_ge(u_hi, n0 + b + 1)
                    dve.tensor_tensor(u[:, c0:c0 + n, T:2 * T], mt[b % 2][:, 0:n, :], u[:, c0:c0 + n, 0:T],
                                      ALU.subtract).then_inc(u_ready, 1)
                    for s in at[b]:
                        hooks(s)

            def start_modulate(*batches):
                modulate(0, stat[:, 1, :], start_xr, start_mt, modc_col(0, 0), modc_col(1, 0),
                         lambda s: lo(W_F + 4 + s, s), batches, START_HOOKS)

            for w in range(4 * KC + SLOTS):
                lo(w, w % SLOTS)
                beside_slab(w)
                if w in FIRST_BATCHES:
                    b = FIRST_BATCHES.index(w)
                    if b == 0:
                        dve.wait_ge(ctx_t, 8)
                        dve.wait_ge(x_copied, 8)
                    if b == 3:
                        dve.wait_ge(modc_step, 3)
                    dve.wait_ge(slab_used, 3 * KC + sum(BATCHES[b]))
                    start_modulate(b)
            dve.wait_ge(row_t, 4)
            mixer_vector(1, 0, KC // 2, KC // 2)
            dve.wait_ge(modc_step, 4)
            start_modulate(4, 5)

            def context_scaled(b):
                c = fq[:, 4 * b:4 * b + 4, :]
                dve.tensor_tensor(c, c, stat[:, 3, :].unsqueeze(1).broadcast_to([P, 4, T]), ALU.mult).then_inc(c_scaled, 1)

            def context_low(b):
                c = fq[:, 4 * b:4 * b + 4, :]
                dve.wait_ge(c_hi, b + 1)
                dve.tensor_tensor(h[:, 4 * b:4 * b + 4, T:2 * T], c, h[:, 4 * b:4 * b + 4, 0:T],
                                  ALU.subtract).then_inc(c_ready, 1)

            def add_halves(pg, bank, dst):
                dve.wait_ge(b_copied, pg + 1)
                dve.tensor_tensor(dst, ps[:, bank:bank + 2, 0:T], tmp[:, :, :], ALU.add).then_inc(sum_done, 1)

            def rope(r, dst):
                dve.wait_ge(rope_swapped, r + 1)
                dve.tensor_tensor(qs, qs, cosT.unsqueeze(1).broadcast_to([P, 2, T]), ALU.mult).then_inc(rope_step, 1)
                dve.tensor_tensor(qsw, qsw, sinT.unsqueeze(1).broadcast_to([P, 2, T]), ALU.mult).then_inc(rope_step, 1)
                dve.wait_ge(rope_step, r * 3 + 2)
                dve.tensor_tensor(dst, qs, qsw, ALU.add).then_inc(rope_step, 1)
                dve.wait_ge(rope_step, r * 3 + 3)

            def att_group(i, at=None, between=None):
                m0 = sum(UNIT_SHARE[:i])
                if i in CONTEXT_AT:
                    context_scaled(CONTEXT_AT.index(i))
                for s in range(SLOTS):
                    if s == 1 and i - 1 in CONTEXT_AT:
                        context_low(CONTEXT_AT.index(i - 1))
                    if s == at:
                        between()
                    if 0 < i < 9:
                        lo(W_F + 4 * i + 4 + s, s)
                    for j in unit_places(i, s):
                        m = m0 + j
                        unit_slab(m, m % 2, m // UNIT, m % UNIT, m // UNIT % 2)

            def take(i):
                add_halves(PG_F + i, 2 * (i % 2), fin[:, 2 * i:2 * i + 2, :] if i < 4 else qs)

            dve.wait_ge(u_ready, 6)
            dve.wait_ge(tab_landed, 32)
            att_group(0)
            att_group(1, SLOTS - 1, lambda: take(0))
            take(1)
            for i in range(2, 8):
                att_group(i, 1 if i >= 5 else None, lambda: rope(i - 5, qh[:, 2 * i - 10:2 * i - 8, :]))
                take(i)
            att_group(8, 1, lambda: rope(3, qh[:, 6:8, :]))
            add_halves(PG_K, 0, qs)
            add_halves(PG_K + 1, 4, kT[:, :, T:2 * T])
            att_group(9, 1, lambda: rope(4, kT[:, :, 0:T]))
            add_halves(PG_V, 2, vsum[:, :, 0:T])
            add_halves(PG_V + 1, 6, vsum[:, :, T:2 * T])

            def stage(pg0, n, un, n_m, take, q=None, u_par=0, opened=False, closing=None):
                w0 = slab_of(pg0)

                def units(b, j, s):
                    js = range(s * n_m // SLOTS, (s + 1) * n_m // SLOTS)
                    if js:
                        unit_slabs(un * UNIT + (b * (2 * n_m) + j * n_m), un, b * (2 * n_m) + j * n_m, js, u_par)

                def pair(b, last=False):
                    for j in range(2):
                        pg, w = b * 2 + (pg0 + j), b * 8 + (w0 + 4 * j + 4)
                        if q is not None:
                            pg, w = q * 16 + pg, q * 64 + w
                        if last and j == 1:
                            closing()
                            take(pg, 2 * j, b * 2 + j)
                        for s in range(SLOTS):
                            if not (last and j == 1):
                                lo(w + s, s)
                            units(b, j, s)
                        if not (last and j == 1):
                            take(pg, 2 * j, b * 2 + j)
                if opened:
                    for s in range(SLOTS):
                        units(0, 0, s)
                    for s in range(SLOTS):
                        if s == SLOTS - 1:
                            take(pg0, 0, 0)
                        lo(w0 + 8 + s, s)
                    for s in range(SLOTS):
                        units(0, 1, s)
                    take(pg0 + 1, 2, 1)
                with dve.Fori(1 if opened else 0, n // 2 - (closing is not None)) as b:
                    pair(b)
                if closing:
                    pair(n // 2 - 1, last=True)

            def row_max(un):
                hd, qt = divmod(un, 2)
                dve.wait_ge(s_done, un + 1)
                far = ps[:, un % 3, (1 - qt) * P:(2 - qt) * P]
                dve.tensor_tensor(far, far, masks[qt], ALU.add).then_inc(masked, 1)
                dve.wait_ge(masked, un + 1)
                dve.tensor_reduce(sm[:, 0, un:un + 1], ps[:, un % 3, :], AX_X, ALU.max).then_inc(max_ready, 1)
                dve.wait_ge(max_ready, un + 1)
                dve.tensor_scalar(sm[:, 1, un:un + 1], sm[:, 0, un:un + 1], -SCALE, nsink[:, 1, hd:hd + 1],
                                  ALU.mult, ALU.min).then_inc(negm_ready, 1)

            def denominator(un):
                dve.wait_ge(p_ready, un + 1)
                col = slice(un, un + 1)
                dve.tensor_tensor(sm[:, 4, col], sm[:, 3, col], sm[:, 2, col], ALU.add).then_inc(den_ready, 1)
                dve.wait_ge(den_ready, un + 1)
                dve.reciprocal(sm[:, 4, col], sm[:, 4, col]).then_inc(rden_ready, 1)

            def o_low(hd):
                dve.wait_ge(o_hi, hd + 1)
                dve.tensor_tensor(u[:, 8 + hd, T:2 * T], ps[:, 6, (hd % 2) * T:(hd % 2 + 1) * T], u[:, 8 + hd, 0:T],
                                  ALU.subtract).then_inc(o_ready, 1)

            def fourier_low(g):
                dve.wait_ge(fb_hi, g + 1)
                dve.tensor_tensor(u[:, 2 * g:2 * g + 2, T:2 * T], ps[:, 7, :].rearrange("p (c t) -> p c t", c=2),
                                  u[:, 2 * g:2 * g + 2, 0:T], ALU.subtract).then_inc(f_ready, 1)

            row_max(0)
            row_max(1)
            for un in range(2 * HEADS):
                denominator(un)
                if un + 2 < 2 * HEADS:
                    row_max(un + 2)
                if un >= 2 * HEADS - 2:
                    for s in range(2):
                        lo(slab_of(PG_WO) + 2 * (un % 2) + s, 2 * (un % 2) + s)
                for m in range(M_MID + 3 * un, min(M_MID + 3 * un + 3, M_WO)):
                    unit_slab(m, m % 2, m // UNIT, m % UNIT, m // UNIT % 2)
                if un % 4 == 0 and un:
                    fourier_low(un // 4 - 1)
                if un % 2 == 0 and un >= 4:
                    o_low(un // 2 - 2)
                if un in (0, 2, 6, 11):
                    unit = (0, 2, 6, 11).index(un)
                    finish_unit(unit, unit_col(unit))
            fourier_low(FG - 1)
            o_low(HEADS - 2)
            o_low(HEADS - 1)

            def open_y(j, gate, gain):
                dve.memset(ssq, 0.0).then_inc(ssq_zeroed, 1)
                dve.tensor_tensor(der[:, 0, :], vt[:, gate:gate + KC], gT[:, gain:gain + KC], ALU.mult).then_inc(gg_ready, 1)
                dve.wait_ge(ssq_zeroed, j + 1)

            def add_squares(n, j):
                dve.wait_ge(ysq_ready, n + 1)
                dve.tensor_tensor(ssq, ssq, sq, ALU.add).then_inc(ssq_done, 1)
                dve.wait_ge(ssq_done, n + 1)

            def take_y(j):
                def f(pg, bank, i):
                    add_halves(pg, bank, y[:, bass.ds(i * 2, 2), :])
                    add_squares(i + 8 * j, j)
                return f

            open_y(0, 2 * KC, KC)
            stage(PG_WO, 8, U_WO, 2, take_y(0), u_par=1, closing=lambda: finish_unit(4, unit_col(4)))

            def boundary(j, scale, gain, last_unit, shift=None, w0=None):
                reciprocal_root(3 + 2 * j, 0)

                def chunks(t, b):
                    return t[:, 4 * b:4 * b + 4, :]

                def scale_y(b):
                    dve.wait_ge(yg_ready, 8 * j + min(2 * b + 2, 8))
                    dve.tensor_tensor(chunks(y, b), chunks(y, b), stat[:, 1, :].unsqueeze(1).broadcast_to([P, 4, T]),
                                      ALU.mult).then_inc(y_scaled, 1)
                scale_y(0)
                for b in range(4):
                    if b < 3:
                        scale_y(b + 1)
                    dve.wait_ge(y_scaled, 4 * j + b + 1)
                    dve.tensor_tensor(chunks(x, b), chunks(x, b), chunks(y, b), ALU.add).then_inc(x_step, 1)
                if scale is None:
                    return
                los(w0)
                if last_unit is not None:
                    finish_unit(last_unit, unit_col(last_unit))
                dve.wait_ge(mod_ready, MOD_NEEDED[j])
                dve.scalar_tensor_tensor(out=der[:, 1, :], in0=vt[:, scale:scale + KC], scalar=1.0,
                                         in1=gT[:, gain:gain + KC], op0=ALU.add, op1=ALU.mult).then_inc(gs_ready, 1)
                dve.wait_ge(gs_ready, j + 1)
                reciprocal_root(4 + 2 * j, 2)
                dve.wait_ge(x_step, 4 * j + 4)
                modulate(6 + 6 * j, stat[:, 3, :], late_xr, late_mt, der[:, 1, :].unsqueeze(2),
                         vt[:, shift:shift + KC].unsqueeze(2), lambda s: lo(w0 + 4 + s, s))

            def mlp(l, u0, loop_units):
                pg0 = PG_MLP[l]

                def take_h(q):
                    def f(pg, bank, i):
                        n = q * 8 + i + 32 * l
                        add_halves(pg, bank, tsum)
                        dve.wait_ge(sum_done, pg + 1)
                        dve.scalar_tensor_tensor(out=relu2, in0=tsum, scalar=0.0, in1=tsum, op0=ALU.max,
                                                 op1=ALU.mult).then_inc(relu2_ready, 1)
                        dve.wait_ge(h_hi, n + 1)
                        dve.wait_ge(relu2_ready, n + 1)
                        dve.tensor_tensor(h[:, bass.ds(i * 2, 2), T:2 * T], relu2, h[:, bass.ds(i * 2, 2), 0:T],
                                          ALU.subtract).then_inc(h_ready, 1)
                        dve.wait_ge(h_ready, n + 1)
                    return f

                def add_to_y(q):
                    def f(pg, bank, i):
                        n = q * 8 + i + (24 * l - 8)
                        yi = y[:, bass.ds(i * 2, 2), :]
                        dve.wait_ge(b_copied, pg + 1)
                        dve.tensor_tensor(yi, ps[:, bank:bank + 2, 0:T], yi, ALU.add).then_inc(y_part, 1)
                        dve.wait_ge(y_part, n + 1)
                        dve.tensor_tensor(yi, tmp[:, :, :], yi, ALU.add).then_inc(sum_done, 1)
                    return f

                def quarter(q, un, n_m, col, take2, first=False):
                    stage(pg0, 8, un, n_m, take_h(q), q, 0, first)
                    if n_m and not first:
                        finish_unit(un - 1, col - 8)
                    stage(pg0 + 8, 8, un + 1, n_m, take2, q, 1)
                    if n_m:
                        finish_unit(un, col)
                quarter(0, u0, 2, unit_col(u0), lambda pg, bank, i: add_halves(pg, bank, y[:, bass.ds(i * 2, 2), :]),
                        first=True)
                with dve.Fori(0, 2) as q:
                    quarter(q + 1, q * 2 + (u0 + 2), loop_units, q * KC + unit_col(8), add_to_y(q + 1))

                def take_last(pg, bank, i):
                    add_to_y(3)(pg, bank, i)
                    add_squares(i + (8 + 16 * l), 1 + 2 * l)
                stage(pg0, 8, u0 + 6, loop_units, take_h(3), 3, 0)
                if loop_units:
                    finish_unit(u0 + 5, unit_col(u0 + 5))
                else:
                    finish_unit(u0 + 1, unit_col(u0 + 1))
                dve.wait_ge(mod_ready, (8, 20)[l])
                open_y(1 + 2 * l, l * 6 * KC + 5 * KC, l * 4 * KC + 3 * KC)
                if l == 0:
                    stage(pg0 + 8, 8, u0 + 7, loop_units, take_last, 3, 1,
                          closing=lambda: finish_unit(u0 + 6, unit_col(u0 + 6)))
                    return
                pg1, w1 = pg0 + 56, slab_of(pg0 + 56)
                with dve.Fori(0, 3) as b:
                    for j in range(2):
                        los(b * 8 + (w1 + 4 * j + 4))
                        take_last(b * 2 + (pg1 + j), 2 * j, b * 2 + j)
                los(w1 + 28)
                take_last(pg1 + 6, 0, 6)
                take_last(pg1 + 7, 2, 7)

            boundary(0, 4 * KC, 2 * KC, 5, 3 * KC, slab_of(PG_MLP[0]))
            mlp(0, U_MLP0, 2)
            L1, G1 = 6 * KC, 4 * KC
            boundary(1, L1 + KC, G1, None, L1, slab_of(PG_CONV))

            dve.memset(zpad[:, :, 0:1], 0.0)
            dve.memset(zpad[:, :, T + 1:T + 2], 0.0).then_inc(z_edges, 1)
            dve.wait_ge(z_edges, 1)

            def triple(t, t0, un, n_m, opened=False):
                for j, dst in enumerate((cgc, cxv, cgb)):
                    pg = t * 3 + (PG_CONV + 3 * t0 + j)
                    w = t * 12 + (slab_of(PG_CONV) + 12 * t0 + 4 * j + 4)
                    if opened and j == 0:
                        for s in range(SLOTS):
                            unit_slabs(un * UNIT, un, 0, conv_unit_slabs(s, n_m), un % 2)
                        continue
                    for s in range(SLOTS):
                        if opened and j == 1 and s == SLOTS - 1:
                            add_halves(pg - 1, 0, cgc)
                        lo(w + s, s)
                        if not (opened and j == 1):
                            unit_slabs(un * UNIT + t * n_m, un, t * n_m, conv_unit_slabs(4 * j + s, n_m), un % 2)
                    if opened and j == 1:
                        unit_slabs(un * UNIT, un, 0, range(4 * n_m // 12, 8 * n_m // 12), un % 2)
                    add_halves(pg, 2 * j, dst)
                    step = t * 5 + 5 * t0
                    if j == 1:
                        dve.wait_ge(sum_done, pg + 1)
                        dve.tensor_tensor(zpad[:, :, 1:T + 1], cgc, cxv, ALU.mult).then_inc(conv_step, 1)
                        dve.wait_ge(conv_step, step + 1)
                        for tap, wait in ((1, 2), (0, 3), (2, 4)):
                            for m in range(2):
                                z = zpad[:, m, tap:tap + T]
                                w_tap = cwT[:, bass.ds(t * 2 + (tap * KC + 2 * t0 + m), 1)]
                                if tap == 1:
                                    last = dve.tensor_scalar(cy[:, m, :], z, w_tap, None, ALU.mult)
                                else:
                                    last = dve.scalar_tensor_tensor(out=cy[:, m, :], in0=z, scalar=w_tap,
                                                                    in1=cy[:, m, :], op0=ALU.mult, op1=ALU.add)
                            last.then_inc(conv_step, 1)
                            dve.wait_ge(conv_step, step + wait)
                hc = bass.ds(t * 2 + 2 * t0, 2)
                dve.wait_ge(sum_done, pg + 1)
                dve.tensor_tensor(cv, cgb, cy, ALU.mult).then_inc(conv_step, 1)
                dve.wait_ge(conv_step, step + 5)
                dve.wait_ge(v_hi, t + (t0 + 1))
                dve.tensor_tensor(h[:, hc, T:2 * T], cv, h[:, hc, 0:T], ALU.subtract).then_inc(conv_ready, 1)
                dve.wait_ge(conv_ready, t + (t0 + 1))

            for t0, n_t, un, n_m in CONV_PARTS:
                if t0 == 0:
                    triple(0, 0, un, n_m, opened=True)
                with dve.Fori(1 if t0 == 0 else 0, n_t) as t:
                    triple(t, t0, un, n_m)
                finish_unit(un - 1, unit_col(un - 1))
            open_y(2, L1 + 2 * KC, G1 + KC)
            stage(PG_CO, 8, U_CO, 2, take_y(2), u_par=1, closing=lambda: finish_unit(16, unit_col(16)))
            boundary(2, L1 + 4 * KC, G1 + 2 * KC, 17, L1 + 3 * KC, slab_of(PG_MLP[1]))
            mlp(1, U_MLP1, 0)
            boundary(3, None, None, None)

        @block.gpsimd
        def _(pool):
            pool.wait_ge(small_t, 1)
            pool.memset(acc[:, 0, :], 0.0).then_inc(acc_zeroed, 1)
            pool.wait_ge(row_t, 4)
            pool.memset(acc[:, 1, :], 0.0).then_inc(acc_zeroed, 1)
            for un in range(len(UNITS)):
                pool.wait_ge(m_used, UNIT * (un + 1))
                if un:
                    pool.wait_ge(unit_read, un)
                pool.partition_all_reduce(red[:, :], acc[:, un % 2, :], P, RADD).then_inc(unit_summed, 1)
                pool.wait_ge(unit_summed, un + 1)
                r = red[:, :].rearrange("p (c f) -> p c f", f=P)
                pool.tensor_tensor(r, r, ident.unsqueeze(1).broadcast_to([P, KC // 2, P]), ALU.mult).then_inc(unit_masked, 1)
                if un + 2 < len(UNITS):
                    pool.memset(acc[:, un % 2, :], 0.0).then_inc(acc_zeroed, 1)


UNIT_SHARE = (2, 3, 3, 3, 4, 4, 4, 3, 8, 4)
M_MID, M_WO = sum(UNIT_SHARE), UNIT * U_WO
CONTEXT_AT = (0, 2, 4, 6)
LOAD_X, LOAD_CTX = 3, 11
PE_TURN_X, DVE_X = 3, 4
ACT_SQ_X, PE_SUM_X, ACT_ROOT_X, DVE_ROOT_X = (7, 9, 11, 13), (9, 11, 13, 15), 17, 18
PE_TURN_CTX, ACT_CTX = 20, 22
ACT_SQ_CTX, PE_SUM_CTX, ACT_ROOT_CTX, DVE_ROOT_CTX = (31, 33, 35, 37), (33, 35, 37, 39), 41, 42
ACT_ROWS, PE_TURN_ROWS, DVE_SCALE, DVE_SHIFT = 2, 4, 38, 54
FIRST_BATCHES = (54, 56, 58, 61)
CONV_PARTS = ((0, 2, 14, 8), (2, 2, 15, 8), (4, 4, 16, 4))


def unit_places(i, s):
    n = UNIT_SHARE[i]
    if i == 1:
        return range(n if s == SLOTS - 1 else 0)
    return range(s * n // SLOTS, (s + 1) * n // SLOTS)


def conv_unit_slabs(i, n_m):
    return range(i * n_m // 12, (i + 1) * n_m // 12)


MOD_NEEDED = (6, 13, 18, 20)


def shape_tables():
    import numpy as np

    f = np.float32
    t = np.zeros((P, TAB_W), f)
    t[:, 0:128] = np.eye(P)
    t[:, 128:256] = 1
    tok = np.arange(T)
    inv_freq = f(10000.0) ** (-np.arange(0, 64, 2, dtype=f) / f(64))
    for p in range(P):
        axis, second, i = p // 64, (p % 64) // 32, p % 32
        pos = (tok // 64, tok % 64)[axis].astype(f)
        ang = pos * inv_freq[i]
        t[p, 256:512] = np.cos(ang)
        t[p, 512:768] = np.sin(ang) if second else -np.sin(ang)
    q, k = np.arange(P)[:, None], np.arange(P)[None, :]
    t[:, 768:896] = np.where(k <= q, 0, -1e30)
    t[:, 896:1024] = np.where(q <= k, 0, -1e30)
    i = np.arange(T)
    ang = 2 * np.pi * ((i[:, None] * i[None, :]) % T) / T
    dft = np.concatenate([np.cos(ang), np.sin(ang)], axis=1).astype(f)
    t[:, 1024:2048] = dft.reshape(2, P, 2 * T).transpose(1, 0, 2).reshape(P, 4 * T)
    t[:, EPS_COL] = 1e-6
    return t


_INS = ["x", "c", "ctx", "c_ctx", "w_mod", "b_mod", "norm_gains", "att_w_in", "att_sink", "att_w_out", "conv_w_in",
        "conv_w", "conv_w_out", "mlp_w1", "mlp_w2"]


def kernel(**inputs):
    import numpy as _np
    import concourse.bacc as _bacc
    from concourse import mybir as _mybir
    from concourse.bass_utils import run_bass_kernel_spmd as _run

    nc = _bacc.Bacc("TRN2", target_bir_lowering=False, num_devices=1)
    arrays = {f"in_{n}_dram": _np.ascontiguousarray(inputs[n]) for n in _INS}
    arrays["tables_dram"] = shape_tables()
    args = [nc.dram_tensor(n, a.shape, _mybir.dt.from_np(a.dtype), kind="ExternalInput").ap()
            for n, a in arrays.items()]
    args.append(nc.dram_tensor("out_0_dram", (1, T, D), F32, kind="ExternalOutput").ap())
    backbone_program(nc, *args)
    r = _run(nc, [arrays], core_ids=[0])
    return r.results[0]["out_0_dram"]
```
